# Optimizing a Trainium2 kernel written in Bass

```python
import math
import jax, jax.numpy as jnp
from jax import lax
import numpy as np

D_MODEL = 1024
BATCH = 1
SEQ = 1024
DEPTH = 2

CHUNK = 64
Q_BLOCK = 128
LRU_WIDTH = 256
LRU_BLOCKS = 4
LRU_BLOCK_W = LRU_WIDTH // LRU_BLOCKS
CONV_WIDTH = 4
RG_C = 8.0
DIFF_HEADS = 6
DIFF_HEAD_DIM = 32
DIFF_V_DIM = 2 * DIFF_HEAD_DIM
DIFF_QK_WIDTH = DIFF_HEADS * 2 * DIFF_HEAD_DIM
DIFF_WIDTH = DIFF_HEADS * DIFF_V_DIM
ALIBI_MAX_BIAS = 8.0
MLA_HEADS = 6
MLA_Q_RANK = 192
MLA_KV_RANK = 128
MLA_NOPE_DIM = 64
MLA_ROPE_DIM = 32
MLA_V_DIM = 64
MLA_QK_DIM = MLA_NOPE_DIM + MLA_ROPE_DIM
MLA_WIDTH = MLA_HEADS * MLA_V_DIM
ROPE_THETA = 10000.0
D_MIX = LRU_WIDTH + DIFF_WIDTH + MLA_WIDTH
IN_SIZES = (LRU_WIDTH, LRU_WIDTH, DIFF_QK_WIDTH, DIFF_QK_WIDTH, DIFF_WIDTH, MLA_Q_RANK, MLA_KV_RANK, MLA_ROPE_DIM)
D_IN = 2 * LRU_WIDTH + 2 * DIFF_QK_WIDTH + DIFF_WIDTH + MLA_Q_RANK + MLA_KV_RANK + MLA_ROPE_DIM
N_GROUPS = 4
EXPERTS_PER_GROUP = 8
N_EXPERTS = N_GROUPS * EXPERTS_PER_GROUP
TOP_K = 2
D_EXPERT = 256
ROW_BLOCK = 128
EPS = 1e-6

kernel_name = "hymba_lru_diffattn_mla_hmoe"

def rms_norm(x, g):
    xf = x.astype(jnp.float32)
    y = xf * lax.rsqrt(jnp.mean(xf * xf, axis=-1, keepdims=True) + EPS)
    return (y * g.astype(jnp.float32)).astype(x.dtype)

def rotary_tables(seq):
    half = MLA_ROPE_DIM // 2
    inv_freq = ROPE_THETA ** (-jnp.arange(half, dtype=jnp.float32) / half)
    ang = jnp.arange(seq, dtype=jnp.float32)[:, None] * inv_freq[None, :]
    return jnp.cos(ang), jnp.sin(ang)

def apply_rotary(x, cos, sin):
    half = x.shape[-1] // 2
    x1 = x[..., :half].astype(jnp.float32)
    x2 = x[..., half:].astype(jnp.float32)
    c = cos[None, :, None, :]
    s = sin[None, :, None, :]
    return jnp.concatenate([x1 * c - x2 * s, x1 * s + x2 * c], axis=-1).astype(x.dtype)

def chunk_allowed(q0, q1, kv_end):
    qpos = jnp.arange(q0, q1)
    kpos = jnp.arange(kv_end)
    return (kpos[None, :] // CHUNK) <= (qpos[:, None] // CHUNK)

def sweep_query_blocks(block_fn, seq):
    outs = []
    for q0 in range(0, seq, Q_BLOCK):
        q1 = q0 + Q_BLOCK
        kv_end = min(seq, -(-q1 // CHUNK) * CHUNK)
        outs.append(block_fn(q0, q1, kv_end))
    return jnp.concatenate(outs, axis=1)

def alibi_slopes(n_heads):
    return jnp.asarray([2.0 ** (-ALIBI_MAX_BIAS * (h + 1) / n_heads) for h in range(n_heads)], dtype=jnp.float32)

def rg_lru_mixer(u, gate, conv_w, conv_b, wa, ba, wx, bx, lam, out_g):
    B, S, W = u.shape
    xc = lax.conv_general_dilated(u, conv_w[:, None, :], window_strides=(1,), padding=[(CONV_WIDTH - 1, 0)],
                                  dimension_numbers=('NWC', 'WIO', 'NWC'), feature_group_count=W) + conv_b
    xb = xc.reshape(B, S, LRU_BLOCKS, LRU_BLOCK_W)
    r = jax.nn.sigmoid((jnp.einsum('bsni,nij->bsnj', xb, wa).reshape(B, S, W) + ba).astype(jnp.float32))
    i = jax.nn.sigmoid((jnp.einsum('bsni,nij->bsnj', xb, wx).reshape(B, S, W) + bx).astype(jnp.float32))
    log_a = -RG_C * r * jax.nn.softplus(-lam.astype(jnp.float32))
    a = jnp.exp(log_a)
    b = jnp.sqrt(-jnp.expm1(2.0 * log_a)) * i * xc.astype(jnp.float32)

    def combine(left, right):
        a1, b1 = left
        a2, b2 = right
        return a1 * a2, a2 * b1 + b2

    _, h = lax.associative_scan(combine, (a, b), axis=1)
    y = h * jax.nn.gelu(gate.astype(jnp.float32))
    return rms_norm(y.astype(u.dtype), out_g)

def diff_attention_mixer(q, k, v, q_g, k_g, lq1, lk1, lq2, lk2, sub_g, lambda_init):
    B, S, _ = q.shape
    q = rms_norm(q.reshape(B, S, DIFF_HEADS, 2, DIFF_HEAD_DIM), q_g)
    k = rms_norm(k.reshape(B, S, DIFF_HEADS, 2, DIFF_HEAD_DIM), k_g)
    v = v.reshape(B, S, DIFF_HEADS, DIFF_V_DIM)
    f32 = jnp.float32
    lam = (jnp.exp(jnp.sum(lq1.astype(f32) * lk1.astype(f32)))
           - jnp.exp(jnp.sum(lq2.astype(f32) * lk2.astype(f32))) + lambda_init)
    slopes = alibi_slopes(DIFF_HEADS)
    scale = DIFF_HEAD_DIM ** -0.5

    def block(q0, q1, kv_end):
        allowed = chunk_allowed(q0, q1, kv_end)
        dist = jnp.abs(jnp.arange(q0, q1)[:, None] - jnp.arange(kv_end)[None, :]).astype(f32)
        bias = jnp.where(allowed[None], -slopes[:, None, None] * dist[None], -jnp.inf)
        s = jnp.einsum('bqhmd,bkhmd->bmhqk', q[:, q0:q1], k[:, :kv_end]).astype(f32) * scale + bias
        p = jax.nn.softmax(s, axis=-1)
        p_diff = p[:, 0] - lam * p[:, 1]
        return jnp.einsum('bhqk,bkhd->bqhd', p_diff.astype(v.dtype), v[:, :kv_end])

    o = sweep_query_blocks(block, S)
    o = rms_norm(o, sub_g) * (1.0 - lambda_init)
    return o.reshape(B, S, DIFF_WIDTH)

def mla_mixer(c_q, c_kv, k_rope, cq_g, ckv_g, w_uq, w_ukv, q_g, k_g, out_g, cos, sin):
    B, S, _ = c_q.shape
    q = (rms_norm(c_q, cq_g) @ w_uq).reshape(B, S, MLA_HEADS, MLA_QK_DIM)
    kv = (rms_norm(c_kv, ckv_g) @ w_ukv).reshape(B, S, MLA_HEADS, MLA_NOPE_DIM + MLA_V_DIM)
    k_nope, v = kv[..., :MLA_NOPE_DIM], kv[..., MLA_NOPE_DIM:]
    k_r = jnp.broadcast_to(k_rope[:, :, None, :], (B, S, MLA_HEADS, MLA_ROPE_DIM))
    k = jnp.concatenate([k_nope, k_r], axis=-1)
    q = rms_norm(q, q_g)
    k = rms_norm(k, k_g)
    q = jnp.concatenate([q[..., :MLA_NOPE_DIM], apply_rotary(q[..., MLA_NOPE_DIM:], cos, sin)], axis=-1)
    k = jnp.concatenate([k[..., :MLA_NOPE_DIM], apply_rotary(k[..., MLA_NOPE_DIM:], cos, sin)], axis=-1)
    scale = MLA_QK_DIM ** -0.5

    def block(q0, q1, kv_end):
        allowed = chunk_allowed(q0, q1, kv_end)
        s = jnp.einsum('bqhd,bkhd->bhqk', q[:, q0:q1], k[:, :kv_end]).astype(jnp.float32) * scale
        p = jax.nn.softmax(jnp.where(allowed, s, -jnp.inf), axis=-1)
        return jnp.einsum('bhqk,bkhd->bqhd', p.astype(v.dtype), v[:, :kv_end])

    o = sweep_query_blocks(block, S)
    return rms_norm(o.reshape(B, S, MLA_WIDTH), out_g)

def hierarchical_moe(h, wg, bg, we, be, w1, w3, w2):
    B, S, D = h.shape
    N = B * S
    f32 = jnp.float32
    hf = h.reshape(N, D)
    g_logits = (hf @ wg).astype(f32) + bg.astype(f32)
    pg = jax.nn.softmax(g_logits, axis=-1)
    g_idx = jnp.argmax(g_logits, axis=-1)
    pg_top = jnp.take_along_axis(pg, g_idx[:, None], axis=-1)
    e_logits = ((hf @ we).astype(f32) + be.astype(f32)).reshape(N, N_GROUPS, EXPERTS_PER_GROUP)
    e_in = jnp.take_along_axis(e_logits, g_idx[:, None, None], axis=1)[:, 0]
    top_p, top_i = lax.top_k(jax.nn.softmax(e_in, axis=-1), TOP_K)
    gate = pg_top * top_p / jnp.sum(top_p, axis=-1, keepdims=True)
    expert_id = g_idx[:, None] * EXPERTS_PER_GROUP + top_i

    NK = N * TOP_K
    flat_e = expert_id.reshape(NK).astype(jnp.int32)
    flat_t = jnp.repeat(jnp.arange(N, dtype=jnp.int32), TOP_K)
    flat_w = gate.reshape(NK)
    order = jnp.argsort(flat_e)
    se, st, sw = flat_e[order], flat_t[order], flat_w[order]
    counts = jnp.bincount(flat_e, length=N_EXPERTS)
    starts = jnp.cumsum(counts) - counts
    padded = (counts + ROW_BLOCK - 1) // ROW_BLOCK * ROW_BLOCK
    pad_ends = jnp.cumsum(padded)
    pad_starts = pad_ends - padded
    dest = pad_starts[se] + (jnp.arange(NK, dtype=jnp.int32) - starts[se])
    n_rows = (-(-NK // ROW_BLOCK) + N_EXPERTS) * ROW_BLOCK
    n_blk = n_rows // ROW_BLOCK
    row_tok = jnp.full((n_rows,), N, jnp.int32).at[dest].set(st)
    row_w = jnp.zeros((n_rows,), hf.dtype).at[dest].set(sw.astype(hf.dtype))
    blk_expert = jnp.minimum(jnp.searchsorted(pad_ends, jnp.arange(n_blk, dtype=jnp.int32) * ROW_BLOCK, side='right'),
                             N_EXPERTS - 1)
    x_pad = jnp.concatenate([hf, jnp.zeros((1, D), hf.dtype)], axis=0)
    x_rows = x_pad[row_tok].reshape(n_blk, ROW_BLOCK, D)

    def expert_block(args):
        xb, e = args
        return (jax.nn.silu(xb @ w1[e]) * (xb @ w3[e])) @ w2[e]

    y_rows = lax.map(expert_block, (x_rows, blk_expert)).reshape(n_rows, D)
    y = jax.ops.segment_sum(y_rows * row_w[:, None], row_tok, num_segments=N + 1)[:N]
    return y.reshape(B, S, D)

def setup_inputs(seed: int = 0) -> dict:
    key = jax.random.key(seed)
    ks = jax.random.split(key, 40)
    counter = [0]
    f32 = jnp.float32
    L = DEPTH

    def nxt():
        k = ks[counter[0]]
        counter[0] += 1
        return k

    def normal(shape, scale):
        return jax.random.normal(nxt(), shape, f32) * scale

    def gain(width):
        return 1.0 + normal((L, width), 0.02)

    x = normal((BATCH, SEQ, D_MODEL), 1.0)
    norm1_g = gain(D_MODEL)
    w_in = normal((L, D_MODEL, D_IN), D_MODEL ** -0.5)
    lru_conv_w = normal((L, CONV_WIDTH, LRU_WIDTH), CONV_WIDTH ** -0.5)
    lru_conv_b = normal((L, LRU_WIDTH), 0.01)
    lru_wa = normal((L, LRU_BLOCKS, LRU_BLOCK_W, LRU_BLOCK_W), LRU_BLOCK_W ** -0.5)
    lru_ba = normal((L, LRU_WIDTH), 0.01)
    lru_wx = normal((L, LRU_BLOCKS, LRU_BLOCK_W, LRU_BLOCK_W), LRU_BLOCK_W ** -0.5)
    lru_bx = normal((L, LRU_WIDTH), 0.01)
    u = jax.random.uniform(nxt(), (L, LRU_WIDTH), f32, minval=0.9, maxval=0.999)
    s = u ** (1.0 / RG_C)
    lru_lambda = jnp.log(s) - jnp.log1p(-s)
    lru_out_g = gain(LRU_WIDTH)
    diff_q_g = gain(DIFF_HEAD_DIM)
    diff_k_g = gain(DIFF_HEAD_DIM)
    diff_lq1 = normal((L, DIFF_HEAD_DIM), 0.1)
    diff_lk1 = normal((L, DIFF_HEAD_DIM), 0.1)
    diff_lq2 = normal((L, DIFF_HEAD_DIM), 0.1)
    diff_lk2 = normal((L, DIFF_HEAD_DIM), 0.1)
    diff_sub_g = gain(DIFF_V_DIM)
    mla_cq_g = gain(MLA_Q_RANK)
    mla_ckv_g = gain(MLA_KV_RANK)
    mla_w_uq = normal((L, MLA_Q_RANK, MLA_HEADS * MLA_QK_DIM), MLA_Q_RANK ** -0.5)
    mla_w_ukv = normal((L, MLA_KV_RANK, MLA_HEADS * (MLA_NOPE_DIM + MLA_V_DIM)), MLA_KV_RANK ** -0.5)
    mla_q_g = gain(MLA_QK_DIM)
    mla_k_g = gain(MLA_QK_DIM)
    mla_out_g = gain(MLA_WIDTH)
    w_out = normal((L, D_MIX, D_MODEL), D_MIX ** -0.5)
    norm2_g = gain(D_MODEL)
    router_g_w = normal((L, D_MODEL, N_GROUPS), D_MODEL ** -0.5)
    router_g_b = normal((L, N_GROUPS), 0.01)
    router_e_w = normal((L, D_MODEL, N_EXPERTS), D_MODEL ** -0.5)
    router_e_b = normal((L, N_EXPERTS), 0.01)
    exp_w1 = normal((L, N_EXPERTS, D_MODEL, D_EXPERT), D_MODEL ** -0.5)
    exp_w3 = normal((L, N_EXPERTS, D_MODEL, D_EXPERT), D_MODEL ** -0.5)
    exp_w2 = normal((L, N_EXPERTS, D_EXPERT, D_MODEL), D_EXPERT ** -0.5)
    return {"x": x, "norm1_g": norm1_g, "w_in": w_in, "lru_conv_w": lru_conv_w, "lru_conv_b": lru_conv_b,
            "lru_wa": lru_wa, "lru_ba": lru_ba, "lru_wx": lru_wx, "lru_bx": lru_bx, "lru_lambda": lru_lambda,
            "lru_out_g": lru_out_g, "diff_q_g": diff_q_g, "diff_k_g": diff_k_g, "diff_lq1": diff_lq1,
            "diff_lk1": diff_lk1, "diff_lq2": diff_lq2, "diff_lk2": diff_lk2, "diff_sub_g": diff_sub_g,
            "mla_cq_g": mla_cq_g, "mla_ckv_g": mla_ckv_g, "mla_w_uq": mla_w_uq, "mla_w_ukv": mla_w_ukv,
            "mla_q_g": mla_q_g, "mla_k_g": mla_k_g, "mla_out_g": mla_out_g, "w_out": w_out, "norm2_g": norm2_g,
            "router_g_w": router_g_w, "router_g_b": router_g_b, "router_e_w": router_e_w, "router_e_b": router_e_b,
            "exp_w1": exp_w1, "exp_w3": exp_w3, "exp_w2": exp_w2}

def reference(x, norm1_g, w_in, lru_conv_w, lru_conv_b, lru_wa, lru_ba, lru_wx, lru_bx, lru_lambda, lru_out_g,
              diff_q_g, diff_k_g, diff_lq1, diff_lk1, diff_lq2, diff_lk2, diff_sub_g,
              mla_cq_g, mla_ckv_g, mla_w_uq, mla_w_ukv, mla_q_g, mla_k_g, mla_out_g, w_out, norm2_g,
              router_g_w, router_g_b, router_e_w, router_e_b, exp_w1, exp_w3, exp_w2):
    B, S, _ = x.shape
    cos, sin = rotary_tables(S)
    split_at = [int(v) for v in np.cumsum(IN_SIZES)[:-1]]
    for l in range(DEPTH):
        hn = rms_norm(x, norm1_g[l])
        proj = hn @ w_in[l]
        lru_x, lru_gate, dq, dk, dv, c_q, c_kv, k_rope = jnp.split(proj, split_at, axis=-1)
        y_lru = rg_lru_mixer(lru_x, lru_gate, lru_conv_w[l], lru_conv_b[l], lru_wa[l], lru_ba[l],
                             lru_wx[l], lru_bx[l], lru_lambda[l], lru_out_g[l])
        lambda_init = 0.8 - 0.6 * math.exp(-0.3 * l)
        y_diff = diff_attention_mixer(dq, dk, dv, diff_q_g[l], diff_k_g[l], diff_lq1[l], diff_lk1[l],
                                      diff_lq2[l], diff_lk2[l], diff_sub_g[l], lambda_init)
        y_mla = mla_mixer(c_q, c_kv, k_rope, mla_cq_g[l], mla_ckv_g[l], mla_w_uq[l], mla_w_ukv[l],
                          mla_q_g[l], mla_k_g[l], mla_out_g[l], cos, sin)
        x = x + jnp.concatenate([y_lru, y_diff, y_mla], axis=-1) @ w_out[l]
        x = x + hierarchical_moe(rms_norm(x, norm2_g[l]), router_g_w[l], router_g_b[l], router_e_w[l],
                                 router_e_b[l], exp_w1[l], exp_w3[l], exp_w2[l])
    return x


_drawn_inputs = setup_inputs


def setup_inputs(seed=0):
    import zlib

    import numpy as np

    out = dict(_drawn_inputs(seed))
    spreads = {}
    factors = {'lru_ba': 5.977,
     'lru_bx': 4.869,
     'diff_q_g': 2.817,
     'diff_k_g': 2.87,
     'mla_q_g': 2.687,
     'mla_k_g': 2.751,
     'router_g_b': 3.463,
     'router_e_b': 2.918}
    for name, (base, spread) in spreads.items():
        noise = np.random.default_rng([zlib.crc32(name.encode()), seed]).standard_normal(out[name].shape)
        drawn = base * np.exp(spread * noise) if base else spread * noise
        out[name] = __import__('jax').numpy.asarray(drawn.astype(out[name].dtype))
    for name, factor in factors.items():
        out[name] = (out[name] * factor).astype(out[name].dtype)
    return out
```

```python
from contextlib import ExitStack

import numpy as np

import concourse.bass as bass
from concourse import mybir

F32 = mybir.dt.float32
I32 = mybir.dt.int32
ALU = mybir.AluOpType
ACT = mybir.ActivationFunctionType
AX = mybir.AxisListType

P = 128
SEQ, D = 1024, 1024
DEPTH = 2
T = SEQ // P
KC = D // P
CHUNK = 64
LRU = 256
DH, DHD, DVD = 6, 32, 64
MH, MN, MR, MV = 6, 64, 32, 64
MQK = MN + MR
QR, KVR = 192, 128
G, EPG = 4, 8
E = G * EPG
FE = 256
EPS = 1e-6
RG_C = 8.0
DSCALE = DHD ** -0.5
MSCALE = MQK ** -0.5
SLOPE = [2.0 ** (-8.0 * (h + 1) / DH) for h in range(DH)]
GELU_C = 0.7978845608028654
LAMBDA_INIT = [0.8 - 0.6 * float(np.exp(-0.3 * l)) for l in range(DEPTH)]
MASKED = -1.0e30

GROUPS = [(0, 512), (512, 384), (896, 384), (1280, 384), (1664, 352)]

R_G1, R_G2, R_LOUT, R_SUB, R_MOUT, R_CQ, R_CKV = 0, 8, 16, 18, 19, 22, 24
R_CW, R_CB, R_BA, R_BX, R_LAM, R_DQ, R_DK, R_MQ, R_MK, NROW = 25, 33, 35, 37, 39, 41, 42, 43, 44, 48

NOV = (2 * SEQ - 1) // P
NBLK = E + NOV

HEADS = DH + MH
NH = T * HEADS


def is_diff(h):
    return h % HEADS < DH


def chunks_of(h):
    n = h // HEADS + 1
    return [(c, min(c + 4, n)) for c in range(0, n, 4)]


def number_items():
    s, t, v = {}, {}, []

    def scores(h):
        for m in range(2 if is_diff(h) else 1):
            s["map", h, m] = len(s)

    scores(0)
    scores(1)
    for i in range(T + 1):
        for n in range(HEADS):
            h = i * HEADS + n
            if h + 2 < NH:
                scores(h + 2)
            if i < T:
                for c in range(len(chunks_of(h))):
                    t["p", h, c] = len(t)
                v.append((v[-1] if v else 0) + len(chunks_of(h)))
            if n == 0 and i < T:
                s["q", i] = len(s)
            if n == 3 and i < T:
                for c in range(2):
                    t["q", i, c] = len(t)
            if n == 4 and i >= 1:
                for c in range(2):
                    t["y", i - 1, c] = len(t)
            if n == 6 and i >= 1:
                s["out", i - 1] = len(s)
            if n == 9 and i >= 1:
                for c in range(2):
                    t["h2", i - 1, c] = len(t)
            if n == 10 and i >= 1:
                t["route", i - 1] = len(t)
    return s, t, v


def number_projections():
    order = [("lru", k) for k in range(8)]
    order += [(1, i) for i in range(T)]
    order += [(2, 0)] + [("gate", k) for k in range(8)] + [(2, i) for i in range(1, T)]
    order += [(3, i) for i in range(T)] + [(4, i) for i in range(T)]
    order += [("lss", k) for k in range(2)]
    order += [("kv", k) for k in range(2 * T)]
    return {k: n for n, k in enumerate(order)}


S_ITEM, T_ITEM, V_DONE = number_items()
PJ = number_projections()


def constants():
    p = np.arange(P)[:, None]
    c = np.arange(SEQ)[None, :]
    q = p + SEQ - P
    barred = (c // CHUNK) > (q // CHUNK)
    dist = np.where(barred, MASKED, -np.abs(q - c).astype(np.float32)).astype(np.float32)
    mask = np.where(barred, MASKED, 0.0).astype(np.float32)
    half = MR // 2
    inv = (np.float32(10000.0) ** (-np.arange(half, dtype=np.float32) / half)).astype(np.float32)
    ang = np.arange(SEQ, dtype=np.float32)[:, None] * inv[None, :]
    co, si = np.cos(ang).astype(np.float32), np.sin(ang).astype(np.float32)
    rope = np.concatenate([co, si, si, co], 1).reshape(T, P, 2 * MR).transpose(1, 0, 2).reshape(P, -1)
    slope = np.zeros((P, 3), np.float32)
    for k in range(3):
        for m in range(4):
            slope[32 * m:32 * m + 32, k] = DSCALE / SLOPE[(4 * k + m) // 2]
    misc = np.zeros((P, 320), np.float32)
    misc[:, 0:3] = slope
    for l in range(DEPTH):
        misc[:, 4 + 2 * l] = 1.0 - LAMBDA_INIT[l]
        misc[:, 5 + 2 * l] = LAMBDA_INIT[l]
    misc[:, 8:16] = np.arange(T)[None, :] * P + p
    misc[:, 16:24] = 8 - np.arange(8)
    misc[:, 24:56] = P * np.arange(E)
    misc[:, 56:88] = E * P - P - P * np.arange(E)
    misc[:, 88:103] = np.arange(NOV)
    misc[:, 103] = EPS
    misc[:, 104:116] = -0.5
    misc[:, 116:244] = SEQ
    tri = (np.arange(P)[:, None] < np.arange(P)[None, :]).astype(np.float32)
    mats = np.concatenate([np.eye(P, dtype=np.float32), np.ones((P, P), np.float32), tri], 1)
    return {"c_dist": dist, "c_mask": mask, "c_rope": np.ascontiguousarray(rope), "c_misc": misc, "c_mats": mats}


MAPS_BEFORE = [sum(2 if is_diff(g) else 1 for g in range(h)) for h in range(NH + 1)]
DIFFS_UPTO = [sum(is_diff(g) for g in range(h + 1)) for h in range(NH)]


def build(nc, a, out):
    x1d = nc.dram_tensor("x1_rows", [SEQ, D], F32)
    xrd = nc.dram_tensor("x_rows", [SEQ, D], F32)
    h2d = nc.dram_tensor("h2_rows", [SEQ, D], F32)
    yd = nc.dram_tensor("y_rows", [NBLK * P, D], F32)
    rtok = nc.dram_tensor("slot_token", [NBLK * P, 1], F32)

    with ExitStack() as ctx:
        KB = 256
        mem = ctx.enter_context(nc.sbuf_tensor("mem", [P, 206 * KB], F32))
        PS = ctx.enter_context(nc.psum_tensor("PS", [P, 8 * 512], F32))
        slot_i = ctx.enter_context(nc.sbuf_tensor("slot_i", [P, 2 * T], I32))
        ov_i = ctx.enter_context(nc.sbuf_tensor("ov_i", [P, NOV + 2], I32))
        gidx = ctx.enter_context(nc.sbuf_tensor("gidx", [P, NBLK], I32))
        ov_tot = ctx.enter_context(nc.sbuf_tensor("ov_tot", [P, 1], F32))

        def at(word, *shape, parts=P):
            n = int(np.prod(shape))
            v = mem[0:parts, word:word + n]
            if len(shape) == 2:
                return v.rearrange("p (a b) -> p a b", a=shape[0])
            if len(shape) == 3:
                return v.rearrange("p (a b c) -> p a b c", a=shape[0], b=shape[1])
            return v

        def bank(b, lo=0, hi=512, parts=P):
            return PS[0:parts, b * 512 + lo:b * 512 + hi]

        def spread(ap, axis, shape):
            return ap.unsqueeze(axis).to_broadcast(shape)

        def tile(i):
            return slice(i * P, (i + 1) * P)

        RA, RB, RC, RD, RE, RL = 0, 32 * KB, 64 * KB, 100 * KB, 136 * KB, 158 * KB
        X = at(RC, T, D)
        xnT = at(RA, KC, SEQ)
        w_in_sb = [at(RB, KC, 512), at(RB + 16 * KB, KC, 512)]
        xsq = [at(RD + 4 * KB * k, D) for k in range(2)]
        xs = [at(RD + 16 * KB + 4 * KB * k, D) for k in range(2)]
        l_xc, l_t2, l_t3, l_t4 = (at(RD + 8 * KB * k, 2, SEQ) for k in range(4))
        l_t5 = at(RE, 2, SEQ)
        u = at(RE + 13 * KB, 2, SEQ + 3)
        l_g = at(RE + 13 * KB, 2, SEQ)
        yl = at(RL, 2, SEQ)
        rows = at(RD + 32 * KB, P, parts=NROW)
        lqk = at(RD + 32 * KB + P, 4, DHD)
        gr = at(RD + 32 * KB + 2 * P, 2, 64)
        ropes = at(RD + 32 * KB + 3 * P, T, 64)
        w_out_sb = at(RA, KC, D)
        Pm = [at(RB + 4 * KB * k, SEQ) for k in range(4)]
        PT = [at(RB + 16 * KB + 2 * KB * k, 512) for k in range(4)]
        wukv = at(RB + 24 * KB, MH * (MN + MV))
        h2 = at(RB + 24 * KB, D)
        h2T = at(RB + 28 * KB, KC, P)
        qT = at(RC, 3, SEQ)
        kT = at(RC + 12 * KB, 3, SEQ)
        Vd = at(RC + 24 * KB, T, DH * DVD)
        kTm = at(RD, MH, SEQ, parts=MQK)
        Vm = at(RD + 24 * KB, T, MH, MV)
        cqT = at(RE, 2, SEQ)
        ckvT = at(RE + 8 * KB, SEQ)
        qsq = at(RE + 8 * KB, MH, MQK)
        osq = at(RE + 8 * KB + MH * MQK, DH * DVD)
        kr = at(RE + 12 * KB, T, MR)
        xr = [at(RE + 13 * KB + 4 * KB * k, D) for k in range(2)]
        w_ex = [(at(o, 2, KC, FE), at(o + 16 * KB, 2, D)) for o in (0, 24 * KB, RD, RE)]
        xg = [at(48 * KB + 4 * KB * k, D) for k in range(2)]
        yo = [at(56 * KB + 4 * KB * k, D) for k in range(2)]
        xgT = [at(RD + 24 * KB + 4 * KB * k, KC, P) for k in range(2)]
        yg = [[at(8 * KB * k + 4 * KB * m, D) for m in range(2)] for k in range(2)]

        top = [166 * KB]

        def new(*shape, parts=P):
            v = at(top[0], *shape, parts=parts)
            top[0] += int(np.prod(shape))
            assert top[0] <= 206 * KB, top[0] / KB
            return v

        dist, mask = new(SEQ), new(SEQ)
        tabq, tabk = new(T, 2, MR), new(T, 2, MR)
        mats = new(3, P)
        ident, ones, tri = mats[:, 0, :], mats[:, 1, :], mats[:, 2, :]
        misc = new(320)
        c_slope, c_lam = misc[:, 0:3], misc[:, 4:8]
        c_tok, c_first, c_e128, c_toov = misc[:, 8:16], misc[:, 16:24], misc[:, 24:56], misc[:, 56:88]
        c_j, c_eps, c_nh, c_none = misc[:, 88:103], misc[:, 103:104], misc[:, 104:116], misc[:, 116:244]
        wuq = new(2, MH * MQK)
        wr = new(KC, G + E)
        wab = new(2, 2, P)
        prm = new(NROW)
        rbias = new(G + E)
        lg = new(T, G + E)
        gate1, gate2 = new(T), new(T)
        toks = new(P)
        ms1, rs1 = new(T), new(T)
        gd3, gm, hb, dsub, tmp1 = new(3), new(1), new(4), new(1), new(1)
        c4, lsum, lex, neglam, lcur = new(2), new(2), new(2), new(1), new(2)
        sp_ = new(6, 2)
        ss, rs = [new(12), new(12)], [new(12), new(12)]
        krs = new(T)
        mxs, nbs, sums, rat, rinv = new(4), new(4), new(4), new(2), new(HEADS)
        qss, qrs, oss, ors, mss, mrs, xss, xrs = new(6), new(6), new(6), new(6), new(1), new(1), new(1), new(1)
        scratch = top[0]
        ob, yT, qraw, uw = new(HEADS * 64), new(6, P), new(MH, MQK), new(MH, 2, MR)
        qTm = new(MH, P, parts=MQK)
        sq = [at(scratch + 384 * k, 384) for k in range(2)]
        qn = [at(scratch + 768 + 576 * k, 576) for k in range(2)]
        th = [at(scratch + 256 * k, FE) for k in range(2)]
        hh = [at(scratch + 512 + 256 * k, FE) for k in range(2)]
        hT = [at(scratch + 1024 + 256 * k, 2, P) for k in range(2)]

        rt = [RD + 24 * KB]

        def rnew(*shape):
            v = at(rt[0], *shape)
            rt[0] += int(np.prod(shape))
            assert rt[0] <= 136 * KB
            return v

        r_gm, r_m, r_pg, r_m1, r_m2 = (rnew(T) for _ in range(5))
        r_t4, r_gs, r_ge, r_oh = (rnew(T, G) for _ in range(4))
        r_t8, r_ein, r_es, r_p, r_o1, r_o2 = (rnew(T, EPG) for _ in range(6))
        r_prod = rnew(T, G, EPG)
        r_M1, r_M2, r_M, r_pre = rnew(T, E), rnew(T, E), rnew(T, E), rnew(T + 1, E)
        r_cnt, r_ov, r_inc, r_ej = rnew(E), rnew(E), rnew(E), rnew(NOV)
        r_sl, r_le = rnew(T, E), rnew(NOV, E)

        lay = []

        def sem(name, per_layer=True):
            s = ctx.enter_context(nc.semaphore(name))
            if per_layer:
                lay.append(s)
            return s

        s_con, s_x, s_zero, s_layer, s_tick, s_out, s_yz = (
            sem(n, False) for n in ("constants_in", "x_in", "zeroed", "layer_may_start", "tick", "out_stored",
                                     "overflow_rows_filled"))
        g_sc, g_ov = sem("tokens_scattered", False), sem("ov_rows_gathered", False)
        g_x = [sem(f"rows_gathered{k}", False) for k in range(2)]
        g_y = [sem(f"outputs_gathered{k}", False) for k in range(2)]
        s_row, s_bc, s_wq, s_wkv, s_wr, s_wab, s_wout, s_xrs = (
            sem(n) for n in ("param_rows_in", "param_bcast_in", "w_uq_in", "w_ukv_in", "router_w_in",
                             "lru_gate_w_in", "w_out_in", "x_rows_saved"))
        s_win = [sem(f"w_in{k}_in") for k in range(2)]
        s_xr = [sem(f"x_tile{k}_in") for k in range(2)]
        s_x1s, s_h2s = [sem(f"x1_stored{k}") for k in range(2)], sem("h2_stored")
        s_pad = sem("conv_pad_zeroed")
        pe_par, dv_par, dv_lam, a_lam, dv_pr = (
            sem(n) for n in ("params_turned", "params_ready", "lambda_dots", "lambda_exp", "params_derived"))
        a_ss, pl_rs, dv_xs, pe_xn, dv_xe = (
            sem(n) for n in ("x_squared", "x_rstd", "x_scaled", "x_turned", "x_evacuated"))
        pe_pj, pe_tr = sem("projected"), sem("qk_turned")
        a_sq, dv_ss, pl_qk, dv_qn = (sem(n) for n in ("qk_squared", "qk_sums", "qk_rstd", "qk_normed"))
        dv_qT, a_kT, dv_cT, a_kTm, dv_kn = (
            sem(n) for n in ("qT_out", "kT_out", "latents_out", "kTm_out", "k_latent_normed"))
        a_v, a_vm, dv_kr = sem("values_out"), sem("latent_values_out"), sem("k_rope_turned")
        l_u, l_conv, l_sig, l_gp, l_dec, l_exp, l_b2, l_sr, l_y, l_y2, l_ms, l_fin = (
            sem(n) for n in ("lru_in", "lru_conv", "lru_gates", "gelu_poly", "lru_decay", "lru_exp", "lru_b2",
                             "lru_root", "lru_y", "lru_y_squared", "lru_rms", "lru_done"))
        dv_ch, pl_ch = sem("vector_chain"), sem("pool_chain")
        pe_s, pe_t, pe_v = sem("scores"), sem("turned"), sem("pv")
        dv_pass, dv_nb, a_exp, dv_comb, a_pt = (
            sem(n) for n in ("biased", "neg_max", "exped", "combined", "p_out"))
        dv_q, a_q, dv_qs, pl_q, dv_qr, a_qT = (
            sem(n) for n in ("q_raw", "q_squared", "q_sums", "q_rstd", "q_rotated", "q_out"))
        dv_o, a_o, dv_os, pl_o, dv_on, a_yT = (
            sem(n) for n in ("o_scaled", "o_squared", "o_sums", "o_rstd", "o_normed", "y_out"))
        dv_x1, a_x1, pl_x1, dv_h2, a_h2T, a_lg = (
            sem(n) for n in ("x1", "x1_squared", "x1_rstd", "h2", "h2_out", "logits"))
        dv_r, a_r, pe_r, dv_slot, dv_idx, dv_xg0 = (
            sem(n) for n in ("route_vector", "route_exp", "route_tensor", "slots", "gather_index", "xg_zeroed"))
        s_fill, s_rtl, pl_sc, s_x1l = (
            sem(n) for n in ("slots_cleared", "slot_tokens_in", "slot_tokens_complete", "x1_reloaded"))
        s_w13 = [sem(f"w13_{k}_in") for k in range(4)]
        s_w2 = [sem(f"w2_{k}_in") for k in range(4)]
        m_tx, m_xt, m_up, m_th, m_u, m_h, m_ht, m_hte, m_dn, m_y = (
            sem(n) for n in ("rows_turned", "rows_out", "up", "tanh", "silu", "hidden", "hidden_turned",
                             "hidden_out", "down", "y_evacuated"))
        m_st = [sem(f"y_stored{k}") for k in range(2)]
        o_free, o_w, o_tx, o_xt, o_up, o_th, o_u, o_h, o_ht, o_hte, o_dn, o_y, o_st = (
            sem("ov_" + n) for n in ("free", "w_in", "rows_turned", "rows_out", "up", "tanh", "silu", "hidden",
                                     "hidden_turned", "hidden_out", "down", "y", "stored"))
        y_done, c_x, c_t = sem("all_y_stored"), sem("combined_x"), sem("combined_first")
        end_sp, end_act, end_dve, end_pe = (sem(f"{k}_layer_end") for k in ("sp", "act", "dve", "pe"))

        w_in, w_out = a["w_in"], a["w_out"]
        ew = {n: a[n].rearrange("l e d f -> (l e d) f") for n in ("exp_w1", "exp_w3", "exp_w2")}

        def new_layer(eng, l):
            eng.wait_ge(s_layer, l + 1)
            eng.sem_inc(s_tick, 1)

        block = ctx.enter_context(nc.Block())

        @block.sync
        def _(sp):
            def load_expert(e, k, s13, s2):
                for m, n in enumerate(("exp_w1", "exp_w3")):
                    src = ew[n][bass.ds(e * D, D), :].rearrange("(k p) f -> p k f", p=P)
                    sp.dma_start(w_ex[k][0][:, m, :, :], src).then_inc(s13, 16)
                src = ew["exp_w2"][bass.ds(e * FE, FE), :].rearrange("(k p) d -> p k d", p=P)
                sp.dma_start(w_ex[k][1][:, :, :], src).then_inc(s2, 16)

            def store_tile(i):
                sp.wait_ge(dv_x1, i + 1)
                sp.dma_start(x1d[tile(i), :], xr[i % 2]).then_inc(s_x1s[i % 2], 16)
                sp.wait_ge(dv_h2, i + 1)
                sp.dma_start(h2d[tile(i), :], h2).then_inc(s_h2s, 16)

            sp.dma_start(mats.rearrange("p a b -> p (a b)"), a["c_mats"]).then_inc(s_con, 16)
            for dst, name in ((misc, "c_misc"), (dist, "c_dist"), (mask, "c_mask")):
                sp.dma_start(dst, a[name]).then_inc(s_con, 16)
            sp.wait_ge(s_zero, 3)
            with sp.Fori(0, DEPTH) as l:
                new_layer(sp, l)

                def param(name):
                    return a[name][bass.ds(l, 1), :]

                def rowdma(r, n, src, width=P):
                    sp.dma_start(rows[r:r + n, 0:width], src).then_inc(s_row, 16)

                for r, name in ((R_G1, "norm1_g"), (R_G2, "norm2_g"), (R_LOUT, "lru_out_g"), (R_MOUT, "mla_out_g"),
                                (R_CKV, "mla_ckv_g"), (R_CB, "lru_conv_b"), (R_BA, "lru_ba"), (R_BX, "lru_bx"),
                                (R_LAM, "lru_lambda")):
                    rowdma(r, a[name].shape[1] // P, param(name).rearrange("o (k p) -> (o k) p", p=P))
                for k in range(2):
                    sp.dma_start(rows[R_SUB:R_SUB + 1, 64 * k:64 * k + 64], param("diff_sub_g")).then_inc(s_row, 16)
                rowdma(R_CQ, 1, a["mla_cq_g"][bass.ds(l, 1), 0:P])
                rowdma(R_CQ + 1, 1, a["mla_cq_g"][bass.ds(l, 1), P:QR], QR - P)
                rowdma(R_CW, 8, a["lru_conv_w"][bass.ds(l, 1), :, :].rearrange("o j (k p) -> (o j k) p", p=P))
                for k in range(4):
                    sp.dma_start(rows[R_DQ:R_DQ + 1, 32 * k:32 * k + 32], param("diff_q_g")).then_inc(s_row, 16)
                    sp.dma_start(rows[R_DK:R_DK + 1, 32 * k:32 * k + 32], param("diff_k_g")).then_inc(s_row, 16)
                rowdma(R_MQ, 1, param("mla_q_g"), MQK)
                rowdma(R_MK, 1, param("mla_k_g"), MQK)

                def load_in(g):
                    c, n = GROUPS[g]
                    src = w_in[bass.ds(l, 1), :, c:c + n].rearrange("o (k p) c -> p (o k) c", p=P)
                    sp.dma_start(w_in_sb[g % 2][:, :, 0:n], src).then_inc(s_win[g % 2], 16)

                load_in(0)
                load_in(1)
                sp.wait_ge(s_x, 16 * T)
                sp.dma_start(xrd.rearrange("(t p) d -> p t d", p=P), X[:, :, :]).then_inc(s_xrs, 16)
                sp.dma_start(ropes.rearrange("p a b -> p (a b)"), a["c_rope"]).then_inc(s_bc, 16)
                for k, name in enumerate(("diff_lq1", "diff_lk1", "diff_lq2", "diff_lk2")):
                    sp.dma_start(lqk[:, k, :], param(name).to_broadcast([P, DHD])).then_inc(s_bc, 16)
                for k, name in enumerate(("mla_q_g", "mla_k_g")):
                    for c in range(2):
                        sp.dma_start(gr[:, k, MR * c:MR * c + MR],
                                     a[name][bass.ds(l, 1), MN:MQK].to_broadcast([P, MR])).then_inc(s_bc, 16)
                sp.dma_start(rbias[:, 0:G], param("router_g_b").to_broadcast([P, G])).then_inc(s_bc, 16)
                sp.dma_start(rbias[:, G:G + E], param("router_e_b").to_broadcast([P, E])).then_inc(s_bc, 16)
                for m, name in enumerate(("lru_wa", "lru_wx")):
                    for b in range(4):
                        o = 64 * (b % 2)
                        sp.dma_start(wab[o:o + 64, m, b // 2, o:o + 64],
                                     a[name][bass.ds(l, 1), b, :, :].rearrange("o i j -> (o i) j")).then_inc(s_wab, 16)
                w = a["mla_w_uq"]
                sp.dma_start(wuq[:, 0, :], w[bass.ds(l, 1), 0:P, :].rearrange("o k c -> (o k) c")).then_inc(s_wq, 16)
                sp.dma_start(wuq[0:QR - P, 1, :],
                             w[bass.ds(l, 1), P:QR, :].rearrange("o k c -> (o k) c")).then_inc(s_wq, 16)
                for o, n, name in ((0, G, "router_g_w"), (G, E, "router_e_w")):
                    src = a[name][bass.ds(l, 1), :, :].rearrange("o (k p) c -> p (o k) c", p=P)
                    sp.dma_start(wr[:, :, o:o + n], src).then_inc(s_wr, 16)
                for g in range(2, 5):
                    sp.wait_ge(pe_pj, PJ[("lru", 7) if g == 2 else (g - 2, T - 1)] + 1)
                    load_in(g)
                sp.wait_ge(pe_pj, PJ[3, T - 1] + 1)
                sp.dma_start(wukv, a["mla_w_ukv"][bass.ds(l, 1), :, :].rearrange("o k c -> (o k) c")).then_inc(s_wkv, 16)
                sp.wait_ge(pe_pj, PJ[4, T - 1] + 1)
                for c in range(2):
                    src = w_out[bass.ds(l, 1), :, 512 * c:512 * c + 512].rearrange("o (k p) c -> p (o k) c", p=P)
                    sp.dma_start(w_out_sb[:, :, 512 * c:512 * c + 512], src).then_inc(s_wout, 16)
                with sp.If(l < 1):
                    sp.dma_start(yd[E * P:NBLK * P, :].rearrange("(b p) d -> p b d", p=P),
                                 spread(mask, 1, [P, NOV, D])).then_inc(s_yz, 16)
                sp.wait_ge(s_xrs, 16)
                sp.wait_ge(l_fin, 2)
                for i in range(T):
                    if i >= 2:
                        sp.wait_ge(dv_h2, i - 1)
                        sp.wait_ge(s_x1s[i % 2], 16 * (i // 2))
                    sp.dma_start(xr[i % 2], xrd[tile(i), :]).then_inc(s_xr[i % 2], 16)
                    if i >= 1:
                        store_tile(i - 1)
                store_tile(T - 1)
                sp.wait_ge(a_lg, T)
                for s in s_x1s:
                    sp.wait_ge(s, 16 * (T // 2))
                sp.wait_ge(s_h2s, 16 * T)
                sp.wait_ge(s_yz, 16)
                sp.dma_start(rtok.rearrange("(b p) o -> b (p o)", p=P), c_none[0:NBLK, :]).then_inc(s_fill, 16)
                for b in range(4):
                    load_expert(l * E + b, b, s_w13[b], s_w2[b])
                sp.dma_start(X[:, :, :], x1d.rearrange("(t p) d -> p t d", p=P)).then_inc(s_x1l, 16)
                sp.wait_ge(pl_sc, 1)
                sp.dma_start(toks[0:NBLK, :], rtok.rearrange("(b p) o -> b (p o)", p=P)).then_inc(s_rtl, 16)
                with sp.Fori(1, E // 4) as it:
                    for j in range(4):
                        sp.wait_ge(m_dn, 8 * it + (2 * j - 6))
                        load_expert(l * E + 4 * it + j, j, s_w13[j], s_w2[j])
                sp.wait_ge(dv_slot, 2)
                n = sp.value_load(ov_i[0:1, NOV:NOV + 1], min_val=0, max_val=NOV)
                with sp.Fori(0, NOV) as j:
                    with sp.If(j < n):
                        sp.wait_ge(o_free, j + 1)
                        sp.sem_inc(s_tick, 1)
                        e = sp.value_load(ov_i[0:1, bass.ds(j, 1)], min_val=0, max_val=E - 1)
                        load_expert(l * E + e, 0, o_w, o_w)
                sp.drain().then_inc(end_sp, 1)
            sp.wait_ge(s_layer, DEPTH + 1)
            sp.dma_start(out.rearrange("o (t p) d -> p (o t) d", p=P), X[:, :, :]).then_inc(s_out, 16)
            sp.wait_ge(s_out, 16)

        @block.gpsimd
        def _(pool):
            chain = [0]

            def rstd(dst, src, n, signal):
                chain[0] += 1
                nc.gpsimd.tensor_scalar(dst, src, 1.0, EPS, ALU.mult, ALU.add).then_inc(pl_ch, 1)
                pool.wait_ge(pl_ch, chain[0])
                nc.gpsimd.tensor_tensor(dst, dst, c_nh[:, 0:n], ALU.pow).then_inc(signal, 1)

            pool.wait_ge(s_con, 64)
            pool.wait_ge(s_zero, 3)
            pool.sem_inc(s_layer, 1)
            with pool.Fori(0, DEPTH) as l:
                nc.gpsimd.memset(u[:, :, 0:3], 0.0).then_inc(s_pad, 1)
                for i in range(T):
                    pool.wait_ge(a_ss, i + 1)
                    rstd(rs1[:, i:i + 1], ms1[:, i:i + 1], 1, pl_rs)
                for q in range(4 * T):
                    if q < 2 * T:
                        n = 12
                        pool.wait_ge(dv_ss, q + 1)
                    elif q < 3 * T:
                        n = 2
                        pool.wait_ge(a_sq, q + 1)
                    else:
                        n = MH
                        pool.wait_ge(dv_ss, q - T + 1)
                    if 2 <= q < 3 * T + 2:
                        pool.wait_ge(dv_qn, q - 1)
                    elif q >= 3 * T + 2:
                        pool.wait_ge(dv_kn, 3 * (q - 2 - 3 * T) + 3)
                    rstd(rs[q % 2][:, 0:n], ss[q % 2][:, 0:n], n, pl_qk)
                for i in range(T + 1):
                    if i < T:
                        pool.wait_ge(dv_qs, i + 1)
                        rstd(qrs, qss, MH, pl_q)
                    if i >= 1:
                        pool.wait_ge(a_o, 2 * i)
                        rstd(mrs, mss, 1, pl_o)
                        pool.wait_ge(a_x1, i)
                        rstd(xrs, xss, 1, pl_x1)
                    if i < T:
                        pool.wait_ge(dv_os, i + 1)
                        rstd(ors, oss, DH, pl_o)
                pool.wait_ge(dv_slot, 1)
                pool.wait_ge(s_fill, 16)
                for k in range(2 * T):
                    nc.gpsimd.indirect_dma_start(
                        rtok[:, :], bass.IndirectOffsetOnAxis(ap=slot_i[:, k:k + 1], axis=0), c_tok[:, k % T:k % T + 1],
                        None, bounds_check=NBLK * P - 1, oob_is_err=False).then_inc(g_sc, 16)
                pool.wait_ge(g_sc, l * (32 * T) + 32 * T)
                pool.sem_inc(s_tick, 1)
                pool.sem_inc(pl_sc, 1)
                pool.wait_ge(dv_idx, 1)
                pool.wait_ge(dv_xg0, 2)

                def gather(dst, table, index, signal, bound):
                    nc.gpsimd.indirect_dma_start(dst, None, table[:, :], bass.IndirectOffsetOnAxis(ap=index, axis=0),
                                                 bounds_check=bound, oob_is_err=False).then_inc(signal, 16)

                for b in range(E):
                    if b >= 2:
                        pool.wait_ge(m_tx, 2 * (b - 1))
                    gather(xg[b % 2], h2d, gidx[:, b:b + 1], g_x[b % 2], SEQ - 1)
                n = pool.value_load(ov_i[0:1, NOV:NOV + 1], min_val=0, max_val=NOV)
                for j in range(NOV):
                    with pool.If(n > j):
                        pool.wait_ge(o_free, j + 1)
                        gather(xg[0], h2d, gidx[:, E + j:E + j + 1], g_ov, SEQ - 1)
                pool.wait_ge(y_done, 1)
                for i in range(T):
                    if i >= 2:
                        pool.wait_ge(c_x, i - 1)
                    for k in range(2):
                        gather(yg[i % 2][k], yd, slot_i[:, k * T + i:k * T + i + 1], g_y[i % 2], NBLK * P - 1)
                for s in (end_sp, end_act, end_dve, end_pe):
                    pool.wait_ge(s, 1)
                pool.sem_clear(range(lay[0].num, lay[-1].num + 1))
                pool.sem_inc(s_layer, 1)

        @block.scalar
        def _(act):
            A = nc.scalar.activation
            for i in range(T):
                act.dma_start(X[:, i, :], a["x"][0, tile(i), :]).then_inc(s_x, 16)
            with act.Fori(0, DEPTH) as l:
                new_layer(act, l)
                act.wait_ge(s_x, 16 * T)
                for i in range(T):
                    if i >= 2:
                        act.wait_ge(a_ss, i - 1)
                    A(xsq[i % 2], X[:, i, :], ACT.Square, scale=D ** -0.5,
                      accum_out=ms1[:, i:i + 1]).then_inc(a_ss, 1)
                act.wait_ge(dv_par, 1)
                for k in range(8):
                    f, c = k // 2, k % 2
                    act.wait_ge(pe_pj, PJ["lru", k] + 1)
                    dst = u[:, f, 3 + 512 * c:515 + 512 * c] if f < 2 else yl[:, f - 2, 512 * c:512 * c + 512]
                    A(dst, bank(PJ["lru", k] % 4), ACT.Copy).then_inc(l_u, 1)
                act.wait_ge(s_xrs, 16)
                act.wait_ge(dv_lam, 1)
                A(lex, lsum, ACT.Exp)
                A(sp_[:, 1, :], sp_[:, 0, :], ACT.Exp, scale=-1.0).then_inc(a_lam, 1)

                def square_qk(q):
                    if q >= 2:
                        act.wait_ge(dv_ss, q - 1)
                    b = PJ[1 + q // T, q % T]
                    act.wait_ge(pe_pj, b + 1)
                    A(sq[q % 2], bank(b % 4, 0, 384), ACT.Square, scale=DHD ** -0.5).then_inc(a_sq, 1)

                def k_out(i):
                    act.wait_ge(pe_tr, T + i + 1)
                    A(kT[:, :, tile(i)], bank(4 + i % 2, 0, 384).rearrange("p (a b) -> p a b", a=3),
                      ACT.Copy).then_inc(a_kT, 1)

                for q in range(T):
                    square_qk(q)
                square_qk(T)
                act.wait_ge(dv_pr, 1)
                for k in range(8):
                    m, f, c = k // 4, (k // 2) % 2, k % 2
                    b = PJ["gate", k]
                    act.wait_ge(pe_pj, b + 1)
                    dst = (l_t2, l_t3)[m][:, f, 512 * c:512 * c + 512]
                    A(dst, bank(b % 4), ACT.Tanh, bias=hb[:, 2 * m + f:2 * m + f + 1], scale=0.5).then_inc(l_sig, 1)
                for i in range(1, T):
                    square_qk(T + i)
                    k_out(i - 1)

                def v_out(i):
                    act.wait_ge(pe_pj, PJ[3, i] + 1)
                    A(Vd[:, i, :], bank(PJ[3, i] % 4, 0, 384), ACT.Copy).then_inc(a_v, 1)

                v_out(0)
                k_out(T - 1)
                act.wait_ge(l_dec, 2)
                A(l_t4[:, :, :], l_t2[:, :, :], ACT.Exp).then_inc(l_exp, 1)
                act.wait_ge(l_exp, 1)
                A(l_t2[:, :, :], l_t2[:, :, :], ACT.Tanh, scale=-1.0).then_inc(l_exp, 1)
                act.wait_ge(l_gp, 1)
                A(l_g[:, :, :], l_g[:, :, :], ACT.Tanh, scale=GELU_C).then_inc(l_exp, 1)
                v_out(1)
                v_out(2)
                act.wait_ge(l_b2, 1)
                A(l_t2[:, :, :], l_t2[:, :, :], ACT.Sqrt).then_inc(l_sr, 1)
                for i in range(3, T):
                    v_out(i)
                for i in range(T):
                    q = 2 * T + i
                    b = PJ[4, i]
                    act.wait_ge(pe_pj, b + 1)
                    act.wait_ge(pl_qk, q - 1)
                    act.wait_ge(a_sq, q - 1)
                    bb = b % 4
                    A(sq[q % 2][:, 0:QR], bank(bb, 0, QR), ACT.Square, scale=QR ** -0.5, accum_out=ss[q % 2][:, 0:1])
                    A(sq[q % 2][:, QR:QR + KVR], bank(bb, QR, QR + KVR), ACT.Square, scale=KVR ** -0.5,
                      accum_out=ss[q % 2][:, 1:2])
                    A(sq[q % 2][:, QR + KVR:QR + KVR + MR], bank(bb, QR + KVR, QR + KVR + MR), ACT.Square,
                      scale=MQK ** -0.5, accum_out=krs[:, i:i + 1])
                    A(kr[:, i, :], bank(bb, QR + KVR, QR + KVR + MR), ACT.Copy).then_inc(a_sq, 1)
                    if i == 3:
                        act.wait_ge(l_y, 1)
                        A(l_t2[:, :, :], yl[:, :, :], ACT.Square, scale=LRU ** -0.5).then_inc(l_y2, 1)
                for c in range(2):
                    b = PJ["lss", c]
                    act.wait_ge(pe_pj, b + 1)
                    A(l_t3[:, 0, 512 * c:512 * c + 512], bank(b % 4), ACT.Sqrt, bias=c_eps).then_inc(l_ms, 1)

                def km_out(i):
                    for c in range(2):
                        r = 3 * T + 2 * i + c
                        act.wait_ge(pe_tr, r + 1)
                        nh = 4 - 2 * c
                        A(kTm[:, 4 * c:4 * c + nh, tile(i)],
                          bank(4 + r % 2, 0, nh * P, parts=MQK).rearrange("p (a b) -> p a b", a=nh),
                          ACT.Copy).then_inc(a_kTm, 1)

                for i in range(T):
                    q = 3 * T + i
                    if i < 2:
                        act.wait_ge(a_sq, q - 1)
                        act.wait_ge(l_fin, 2)
                    else:
                        act.wait_ge(dv_ss, 2 * T + i - 1)
                    for c in range(2):
                        b = PJ["kv", 2 * i + c]
                        act.wait_ge(pe_pj, b + 1)
                        kv = bank(b % 4, 0, 384).rearrange("p (h w) -> p h w", h=3)
                        A(Vm[:, i, 3 * c:3 * c + 3, :], kv[:, :, MN:MN + MV], ACT.Copy).then_inc(a_vm, 1)
                        ins = A(sq[q % 2][:, 192 * c:192 * c + 192].rearrange("p (h w) -> p h w", h=3), kv[:, :, 0:MN],
                                ACT.Square, scale=MQK ** -0.5)
                    ins.then_inc(a_sq, 1)
                    if i >= 1:
                        km_out(i - 1)
                km_out(T - 1)

                pc = [0]

                def exp_maps(h):
                    for m in range(2 if is_diff(h) else 1):
                        k = (h % 2) * 2 + m
                        i, n = h // HEADS, h % HEADS
                        act.wait_ge(dv_nb, MAPS_BEFORE[h] + m + 1)
                        v = Pm[k][:, 0:(i + 1) * P]
                        A(v, v, ACT.Exp, bias=nbs[:, k:k + 1], scale=SLOPE[n] if n < DH else 1.0,
                          accum_out=sums[:, k:k + 1]).then_inc(a_exp, 1)

                def p_out(h):
                    for c, (lo, hi) in enumerate(chunks_of(h)):
                        r = T_ITEM["p", h, c]
                        act.wait_ge(pe_t, r + 1)
                        if pc[0] >= 4:
                            act.wait_ge(pe_v, pc[0] - 3)
                        n = (hi - lo) * P
                        A(PT[pc[0] % 4][:, 0:n], bank(4 + r % 2, 0, n), ACT.Copy).then_inc(a_pt, 1)
                        pc[0] += 1

                exp_maps(0)
                exp_maps(1)
                for i in range(T + 1):
                    for n in range(HEADS):
                        h = i * HEADS + n
                        if i < T:
                            p_out(h)
                        if n == 3 and i < T:
                            for c in range(2):
                                r = T_ITEM["q", i, c]
                                act.wait_ge(pe_t, r + 1)
                                nh = 4 - 2 * c
                                A(qTm[:, 4 * c:4 * c + nh, :],
                                  bank(4 + r % 2, 0, nh * P, parts=MQK).rearrange("p (a b) -> p a b", a=nh),
                                  ACT.Copy, scale=gm[0:MQK, :]).then_inc(a_qT, 1)
                        if n == 4 and i >= 1:
                            for b in range(6):
                                r = T_ITEM["y", i - 1, b // 4]
                                act.wait_ge(pe_t, r + 1)
                                g = dsub if b < 3 else prm[:, R_MOUT + b - 3:R_MOUT + b - 2]
                                A(yT[:, b, :], bank(4 + r % 2, (b % 4) * P, (b % 4) * P + P), ACT.Copy,
                                  scale=g).then_inc(a_yT, 1)
                        if n == 9 and i >= 1:
                            for k in range(KC):
                                r = T_ITEM["h2", i - 1, k // 4]
                                act.wait_ge(pe_t, r + 1)
                                A(h2T[:, k, :], bank(4 + r % 2, (k % 4) * P, (k % 4) * P + P), ACT.Copy,
                                  scale=prm[:, R_G2 + k:R_G2 + k + 1]).then_inc(a_h2T, 1)
                        if n == 10 and i >= 1:
                            r = T_ITEM["route", i - 1]
                            act.wait_ge(pe_t, r + 1)
                            A(lg[:, i - 1, :], bank(4 + r % 2, 0, G + E), ACT.Copy).then_inc(a_lg, 1)
                        if h + 2 < NH:
                            exp_maps(h + 2)
                        if n == 0 and i < T:
                            act.wait_ge(dv_q, i + 1)
                            A(qsq[:, :, :], qraw[:, :, :], ACT.Square, scale=MQK ** -0.5).then_inc(a_q, 1)
                        if n == 1 and i >= 1:
                            act.wait_ge(dv_o, 2 * i)
                            A(osq, ob[:, 384:768], ACT.Square, scale=(MH * MV) ** -0.5, accum_out=mss).then_inc(a_o, 1)
                        if n == 7 and i >= 1:
                            act.wait_ge(dv_x1, i)
                            if i >= 2:
                                act.wait_ge(s_h2s, 16 * (i - 1))
                            A(h2, xr[(i - 1) % 2], ACT.Square, scale=D ** -0.5, accum_out=xss).then_inc(a_x1, 1)
                        if n == 7 and i < T:
                            act.wait_ge(dv_o, 2 * i + 1)
                            act.wait_ge(a_o, 2 * i)
                            A(osq, ob[:, 0:384], ACT.Square, scale=DVD ** -0.5).then_inc(a_o, 1)

                act.wait_ge(dv_r, 1)
                A(r_ge, r_gs, ACT.Exp)
                A(r_p, r_es, ACT.Exp).then_inc(a_r, 1)

                def tanh_a1(b4, b):
                    k = b % 2
                    act.wait_ge(m_up, 4 * b4 + b + 1)
                    if not (isinstance(b4, int) and 4 * b4 + b < 2):
                        act.wait_ge(m_u, 4 * b4 + b - 1)
                    A(th[k], bank(2 + k, 0, FE), ACT.Tanh, scale=0.5).then_inc(m_th, 1)

                def finish(b4, b):
                    k = b % 2
                    early = isinstance(b4, int) and 4 * b4 + b < 2
                    act.wait_ge(m_ht, 4 * b4 + b + 1)
                    if not early:
                        act.wait_ge(m_dn, 8 * b4 + 2 * b - 2)
                    A(hT[k], bank(4, 0, 256).rearrange("p (a b) -> p a b", a=2), ACT.Copy).then_inc(m_hte, 1)
                    if not early:
                        act.wait_ge(m_st[k], 32 * b4 + 16 * (b // 2))
                    for c in range(2):
                        act.wait_ge(m_dn, 8 * b4 + 2 * b + c + 1)
                        A(yo[k][:, 512 * c:512 * c + 512], bank(5 + c), ACT.Copy).then_inc(m_y, 1)
                    act.wait_ge(m_y, 8 * b4 + 2 * b + 2)
                    act.dma_start(yd[bass.ds((4 * b4 + b) * P, P), :], yo[k]).then_inc(m_st[k], 16)

                tanh_a1(0, 0)
                for b in range(4):
                    tanh_a1(0, b + 1)
                    finish(0, b)
                with act.Fori(1, E // 4 - 1) as it:
                    for b in range(4):
                        tanh_a1(it, b + 1)
                        finish(it, b)
                for b in range(4):
                    if b < 3:
                        tanh_a1(E // 4 - 1, b + 1)
                    finish(E // 4 - 1, b)
                for s in m_st:
                    act.wait_ge(s, 8 * E)
                act.wait_ge(dv_slot, 2)
                n = act.value_load(ov_i[0:1, NOV:NOV + 1], min_val=0, max_val=NOV)
                with act.Fori(0, NOV) as j:
                    with act.If(j < n):
                        act.wait_ge(o_up, j + 1)
                        A(th[0], bank(2, 0, FE), ACT.Tanh, scale=0.5).then_inc(o_th, 1)
                        act.wait_ge(o_ht, j + 1)
                        A(hT[0], bank(4, 0, 256).rearrange("p (a b) -> p a b", a=2), ACT.Copy).then_inc(o_hte, 1)
                        act.wait_ge(o_dn, j + 1)
                        A(yo[0], PS[:, 5 * 512:7 * 512], ACT.Copy).then_inc(o_y, 1)
                        act.wait_ge(o_y, j + 1)
                        act.dma_start(yd[bass.ds((j + E) * P, P), :], yo[0]).then_inc(o_st, 16)
                        act.wait_ge(o_st, 16 * j + 16)
                        act.sem_inc(s_tick, 1)
                act.sem_inc(y_done, 1)
                act.drain().then_inc(end_act, 1)

        @block.vector
        def _(dve):
            V = nc.vector
            chain = [0]

            def link(ins):
                chain[0] += 1
                ins.then_inc(dv_ch, 1)
                dve.wait_ge(dv_ch, chain[0])

            V.memset(rows, 0.0).then_inc(s_zero, 1)
            V.memset(wab[:, :, :, :], 0.0).then_inc(s_zero, 1)
            V.memset(ov_tot[:, :], 0.0).then_inc(s_zero, 1)
            with dve.Fori(0, DEPTH) as l:
                new_layer(dve, l)
                dve.wait_ge(pe_par, 1)
                V.tensor_copy(prm, bank(7, 0, NROW)).then_inc(dv_par, 1)
                dve.wait_ge(dv_par, 1)

                def xn_out(i):
                    for c in range(2):
                        r = 2 * i + c
                        dve.wait_ge(pe_xn, r + 1)
                        V.tensor_tensor(xnT[:, 4 * c:4 * c + 4, tile(i)],
                                        bank(4 + c).rearrange("p (a b) -> p a b", a=4),
                                        spread(prm[:, R_G1 + 4 * c:R_G1 + 4 * c + 4], 2, [P, 4, P]),
                                        ALU.mult).then_inc(dv_xe, 1)

                for i in range(T):
                    dve.wait_ge(pl_rs, i + 1)
                    if i >= 2:
                        dve.wait_ge(pe_xn, 2 * (i - 1))
                    V.tensor_scalar(xs[i % 2], X[:, i, :], rs1[:, i:i + 1], None, ALU.mult).then_inc(dv_xs, 1)
                    if i >= 1:
                        xn_out(i - 1)
                xn_out(T - 1)

                dve.wait_ge(s_bc, 16 * 11)
                link(V.tensor_tensor(tmp1, prm[:, R_DQ:R_DQ + 1], prm[:, R_DK:R_DK + 1], ALU.mult))
                V.tensor_scalar(gd3, c_slope, tmp1, None, ALU.mult)
                V.tensor_scalar(hb, prm[:, R_BA:R_BA + 4], 0.5, None, ALU.mult)
                V.tensor_copy(lcur, c_lam[:, bass.ds(2 * l, 2)])
                V.scalar_tensor_tensor(sp_[:, 0, :], prm[:, R_LAM:R_LAM + 2], -1.0, prm[:, R_LAM:R_LAM + 2], ALU.mult, ALU.max)
                link(V.tensor_tensor(gm[0:MQK, :], prm[0:MQK, R_MQ:R_MQ + 1], prm[0:MQK, R_MK:R_MK + 1], ALU.mult))
                V.tensor_scalar(gm[0:MN, :], gm[0:MN, :], MSCALE, None, ALU.mult)
                V.memset(gm[MN:MQK, :], MSCALE)
                V.tensor_scalar(dsub, prm[:, R_SUB:R_SUB + 1], lcur[:, 0:1], None, ALU.mult).then_inc(dv_pr, 1)
                V.tensor_tensor_reduce(uw[:, 0, 0, :], lqk[:, 0, :], lqk[:, 1, :], 1.0, 0.0, ALU.mult, ALU.add,
                                       lsum[:, 0:1])
                V.tensor_tensor_reduce(uw[:, 1, 0, :], lqk[:, 2, :], lqk[:, 3, :], 1.0, 0.0, ALU.mult, ALU.add,
                                       lsum[:, 1:2]).then_inc(dv_lam, 1)
                V.tensor_tensor(tabq[:, :, :, :].rearrange("p t a b -> p t (a b)"), ropes[:, :, :],
                                spread(gr[:, 0, :], 1, [P, T, 64]), ALU.mult)
                link(V.tensor_tensor(tabk[:, :, :, :].rearrange("p t a b -> p t (a b)"), ropes[:, :, :],
                                     spread(gr[:, 1, :], 1, [P, T, 64]), ALU.mult))
                dve.wait_ge(a_lam, 1)
                link(V.tensor_tensor(neglam, lex[:, 1:2], lex[:, 0:1], ALU.subtract))
                link(V.tensor_tensor(neglam, neglam, lcur[:, 1:2], ALU.subtract))
                z, s1, s2, po, mx0 = (sp_[:, k, :] for k in range(1, 6))
                link(V.tensor_scalar(s1, z, 2.0, None, ALU.add))
                link(V.reciprocal(s1, s1))
                link(V.tensor_tensor(s1, s1, z, ALU.mult))
                link(V.tensor_tensor(s2, s1, s1, ALU.mult))
                link(V.tensor_scalar(po, s2, 1.0 / 17, None, ALU.mult))
                for k in (15, 13, 11, 9, 7, 5, 3):
                    link(V.scalar_tensor_tensor(po, po, 1.0 / k, s2, ALU.add, ALU.mult))
                link(V.scalar_tensor_tensor(po, po, 1.0, s1, ALU.add, ALU.mult))
                link(V.tensor_scalar(mx0, prm[:, R_LAM:R_LAM + 2], -1.0, 0.0, ALU.mult, ALU.max))
                link(V.scalar_tensor_tensor(po, po, 2.0, mx0, ALU.mult, ALU.add))
                link(V.tensor_scalar(c4, po, -RG_C / 2, None, ALU.mult))

                def conv(k):
                    f, j = k // 4, k % 4
                    w = prm[:, R_CW + 2 * j + f:R_CW + 2 * j + f + 1]
                    if k == 0:
                        dve.wait_ge(l_u, 8)
                        dve.wait_ge(s_pad, 1)
                    else:
                        dve.wait_ge(l_conv, k)
                    win = u[:, f, j:j + SEQ]
                    if j == 0:
                        V.tensor_scalar(l_xc[:, f, :], win, w, prm[:, R_CB + f:R_CB + f + 1], ALU.mult,
                                        ALU.add).then_inc(l_conv, 1)
                    else:
                        V.scalar_tensor_tensor(l_xc[:, f, :], win, w, l_xc[:, f, :], ALU.mult,
                                               ALU.add).then_inc(l_conv, 1)

                def gelu_poly(k):
                    if k == 0:
                        dve.wait_ge(l_conv, 8)
                        link(V.tensor_tensor(l_g[:, :, :], yl[:, :, :], yl[:, :, :], ALU.mult))
                    elif k == 1:
                        link(V.tensor_scalar(l_g[:, :, :], l_g[:, :, :], 0.044715, 1.0, ALU.mult, ALU.add))
                    else:
                        V.tensor_tensor(l_g[:, :, :], l_g[:, :, :], yl[:, :, :], ALU.mult).then_inc(l_gp, 1)

                def decay():
                    dve.wait_ge(l_sig, 8)
                    for f in range(2):
                        V.tensor_scalar(l_t2[:, f, :], l_t2[:, f, :], 1.0, c4[:, f:f + 1], ALU.add,
                                        ALU.mult).then_inc(l_dec, 1)

                def q_out(i):
                    dve.wait_ge(pe_tr, i + 1)
                    V.tensor_tensor(qT[:, :, tile(i)], bank(4 + i % 2, 0, 384).rearrange("p (a b) -> p a b", a=3),
                                    spread(gd3, 2, [P, 3, P]), ALU.mult).then_inc(dv_qT, 1)

                dve.wait_ge(s_xrs, 16)
                for q in range(2 * T):
                    b = PJ[1 + q // T, q % T]
                    dve.wait_ge(a_sq, q + 1)
                    if q >= 2:
                        dve.wait_ge(pl_qk, q - 1)
                    V.tensor_reduce(ss[q % 2], sq[q % 2].rearrange("p (m d) -> p m d", d=DHD), AX.X,
                                    ALU.add).then_inc(dv_ss, 1)
                    if q < T:
                        conv(q)
                    elif q in (T + 1, T + 2, T + 3):
                        gelu_poly(q - T - 1)
                    elif q == T + 5:
                        decay()
                    dve.wait_ge(pl_qk, q + 1)
                    if q >= 2:
                        dve.wait_ge(pe_tr, q - 1)
                    V.tensor_tensor(qn[q % 2][:, 0:384].rearrange("p (m d) -> p m d", d=DHD),
                                    bank(b % 4, 0, 384).rearrange("p (m d) -> p m d", d=DHD),
                                    spread(rs[q % 2], 2, [P, 12, DHD]), ALU.mult).then_inc(dv_qn, 1)
                    if 1 <= q <= T:
                        q_out(q - 1)

                dve.wait_ge(l_exp, 2)
                link(V.tensor_tensor(l_t5[:, :, :], l_t4[:, :, :], l_t4[:, :, :], ALU.mult))
                V.scalar_tensor_tensor(l_t2[:, :, :], l_t5[:, :, :], 1.0, l_t2[:, :, :], ALU.add,
                                       ALU.mult).then_inc(l_b2, 1)
                link(V.scalar_tensor_tensor(l_t3[:, :, :], l_t3[:, :, :], 1.0, l_xc[:, :, :], ALU.add, ALU.mult))
                dve.wait_ge(l_sr, 1)
                link(V.scalar_tensor_tensor(l_t3[:, :, :], l_t3[:, :, :], 0.5, l_t2[:, :, :], ALU.mult, ALU.mult))
                for f in range(2):
                    link(V.tensor_tensor_scan(l_xc[:, f, :], l_t4[:, f, :], l_t3[:, f, :], 0.0, ALU.mult, ALU.add))
                dve.wait_ge(l_exp, 3)
                link(V.scalar_tensor_tensor(l_g[:, :, :], l_g[:, :, :], 1.0, yl[:, :, :], ALU.add, ALU.mult))
                V.scalar_tensor_tensor(yl[:, :, :], l_g[:, :, :], 0.5, l_xc[:, :, :], ALU.mult,
                                       ALU.mult).then_inc(l_y, 1)

                def latents_out(i):
                    r = 2 * T + i
                    dve.wait_ge(pe_tr, r + 1)
                    b = 4 + r % 2
                    V.tensor_scalar(cqT[:, 0, tile(i)], bank(b, 0, P), prm[:, R_CQ:R_CQ + 1], None, ALU.mult)
                    V.tensor_scalar(cqT[0:64, 1, tile(i)], bank(b, P, 2 * P, parts=64), prm[0:64, R_CQ + 1:R_CQ + 2],
                                    None, ALU.mult)
                    V.tensor_scalar(ckvT[:, tile(i)], bank(b, 2 * P, 3 * P), prm[:, R_CKV:R_CKV + 1], None,
                                    ALU.mult).then_inc(dv_cT, 1)

                for i in range(T):
                    q = 2 * T + i
                    b = PJ[4, i] % 4
                    dve.wait_ge(a_sq, q + 1)
                    dve.wait_ge(pl_qk, q + 1)
                    dve.wait_ge(pe_tr, q - 1)
                    V.tensor_scalar(qn[q % 2][:, 0:QR], bank(b, 0, QR), rs[q % 2][:, 0:1], None, ALU.mult)
                    V.tensor_scalar(qn[q % 2][:, QR:QR + KVR], bank(b, QR, QR + KVR), rs[q % 2][:, 1:2], None,
                                    ALU.mult).then_inc(dv_qn, 1)
                    if i >= 1:
                        latents_out(i - 1)
                latents_out(T - 1)
                kx = qn[0][:, 0:512].rearrange("p (t a b) -> p t a b", t=T, a=2)
                link(V.tensor_tensor(kx, spread(kr, 2, [P, T, 2, MR]), tabk, ALU.mult))
                V.tensor_tensor(kr[:, :, 0:16], kx[:, :, 0, 0:16], kx[:, :, 0, 16:32], ALU.subtract)
                link(V.tensor_tensor(kr[:, :, 16:32], kx[:, :, 1, 0:16], kx[:, :, 1, 16:32], ALU.add))
                dve.wait_ge(l_ms, 2)
                link(V.reciprocal(l_t3[:, 0, :], l_t3[:, 0, :]))
                for f in range(2):
                    V.scalar_tensor_tensor(yl[:, f, :], yl[:, f, :], prm[:, R_LOUT + f:R_LOUT + f + 1],
                                           l_t3[:, 0, :], ALU.mult, ALU.mult).then_inc(l_fin, 1)

                for i in range(T):
                    q = 3 * T + i
                    dve.wait_ge(a_sq, q + 1)
                    dve.wait_ge(pl_qk, q - 1)
                    link(V.tensor_reduce(ss[q % 2][:, 0:MH], sq[q % 2].rearrange("p (h d) -> p h d", d=MN), AX.X,
                                         ALU.add))
                    V.tensor_scalar(ss[q % 2][:, 0:MH], ss[q % 2][:, 0:MH], krs[:, i:i + 1], None,
                                    ALU.add).then_inc(dv_ss, 1)
                    dve.wait_ge(pl_qk, q + 1)
                    dve.wait_ge(pe_tr, 3 * T + max(0, 2 * i - 2))
                    kn = qn[q % 2].rearrange("p (h d) -> p h d", h=MH)
                    for c in range(2):
                        b = PJ["kv", 2 * i + c] % 4
                        V.tensor_tensor(kn[:, 3 * c:3 * c + 3, 0:MN],
                                        bank(b, 0, 384).rearrange("p (h w) -> p h w", h=3)[:, :, 0:MN],
                                        spread(rs[q % 2][:, 3 * c:3 * c + 3], 2, [P, 3, MN]),
                                        ALU.mult).then_inc(dv_kn, 1)
                    V.tensor_tensor(kn[:, :, MN:MQK], spread(kr[:, i, :], 1, [P, MH, MR]),
                                    spread(rs[q % 2][:, 0:MH], 2, [P, MH, MR]), ALU.mult).then_inc(dv_kn, 1)

                def bias_maps(h):
                    i, n = h // HEADS, h % HEADS
                    nk = (i + 1) * P
                    for m in range(2 if n < DH else 1):
                        k = (h % 2) * 2 + m
                        s = S_ITEM["map", h, m]
                        c = MAPS_BEFORE[h] + m
                        dve.wait_ge(pe_s, s + 1)
                        if h >= 2:
                            dve.wait_ge(pe_t, T_ITEM["p", h - 2, len(chunks_of(h - 2)) - 1] + 1)
                        V.tensor_tensor_reduce(Pm[k][:, 0:nk], PS[:, (s % 2) * 1024:(s % 2) * 1024 + nk],
                                               (dist if n < DH else mask)[:, SEQ - nk:SEQ], 1.0, -3.0e38, ALU.add,
                                               ALU.max, mxs[:, k:k + 1]).then_inc(dv_pass, 1)
                        dve.wait_ge(dv_pass, c + 1)
                        V.tensor_scalar(nbs[:, k:k + 1], mxs[:, k:k + 1], -SLOPE[n] if n < DH else -1.0, None,
                                        ALU.mult).then_inc(dv_nb, 1)

                def combine(h):
                    i, n = h // HEADS, h % HEADS
                    k = (h % 2) * 2
                    dve.wait_ge(a_exp, MAPS_BEFORE[h + 1])
                    if n >= DH:
                        link(V.reciprocal(rinv[:, n:n + 1], sums[:, k:k + 1]))
                        return
                    link(V.reciprocal(rat[:, 0:1], sums[:, k + 1:k + 2]))
                    link(V.scalar_tensor_tensor(rat[:, 1:2], sums[:, k:k + 1], neglam, rat[:, 0:1], ALU.mult,
                                                ALU.mult))
                    nk = (i + 1) * P
                    link(V.reciprocal(rinv[:, n:n + 1], sums[:, k:k + 1]))
                    V.scalar_tensor_tensor(Pm[k][:, 0:nk], Pm[k + 1][:, 0:nk], rat[:, 1:2], Pm[k][:, 0:nk], ALU.mult,
                                           ALU.add).then_inc(dv_comb, 1)

                dve.wait_ge(s_wout, 32)
                bias_maps(0)
                bias_maps(1)
                combine(0)
                for i in range(T + 1):
                    for n in range(HEADS):
                        h = i * HEADS + n
                        if h + 2 < NH:
                            bias_maps(h + 2)
                        if h + 1 < NH:
                            combine(h + 1)
                        if n == 0 and i < T:
                            s = S_ITEM["q", i]
                            dve.wait_ge(pe_s, s + 1)
                            if i >= 1:
                                dve.wait_ge(pe_t, T_ITEM["q", i - 1, 1] + 1)
                            o = (s % 2) * 1024
                            V.tensor_copy(qraw[:, 0:4, :], PS[:, o:o + 384].rearrange("p (h d) -> p h d", h=4))
                            V.tensor_copy(qraw[:, 4:6, :],
                                          PS[:, o + 512:o + 704].rearrange("p (h d) -> p h d", h=2)).then_inc(dv_q, 1)
                        if n == 1 and i < T:
                            dve.wait_ge(a_q, i + 1)
                            V.tensor_reduce(qss, qsq[:, :, :], AX.X, ALU.add).then_inc(dv_qs, 1)
                        if n == 1 and i >= 1:
                            dve.wait_ge(pe_v, V_DONE[h - 2])
                            V.tensor_tensor(ob[:, 384:768].rearrange("p (h d) -> p h d", h=MH),
                                            bank(7, 0, 384).rearrange("p (h d) -> p h d", h=MH),
                                            spread(rinv[:, 6:12], 2, [P, MH, MV]), ALU.mult).then_inc(dv_o, 1)
                        if n == 2 and i < T:
                            dve.wait_ge(pl_q, i + 1)
                            link(V.tensor_tensor(qraw[:, :, :], qraw[:, :, :], spread(qrs, 2, [P, MH, MQK]), ALU.mult))
                            link(V.tensor_tensor(uw[:, :, :, :], spread(qraw[:, :, MN:MQK], 2, [P, MH, 2, MR]),
                                                 spread(tabq[:, i, :, :], 1, [P, MH, 2, MR]), ALU.mult))
                            V.tensor_tensor(qraw[:, :, MN:MN + 16], uw[:, :, 0, 0:16], uw[:, :, 0, 16:32], ALU.subtract)
                            V.tensor_tensor(qraw[:, :, MN + 16:MQK], uw[:, :, 1, 0:16], uw[:, :, 1, 16:32],
                                            ALU.add).then_inc(dv_qr, 1)
                        if n == 2 and i >= 1:
                            dve.wait_ge(pl_o, 2 * i)
                            V.tensor_scalar(ob[:, 384:768], ob[:, 384:768], mrs, None, ALU.mult).then_inc(dv_on, 1)
                        if n == 6 and i >= 1:
                            s = S_ITEM["out", i - 1]
                            x = xr[(i - 1) % 2]
                            dve.wait_ge(pe_s, s + 1)
                            dve.wait_ge(s_xr[(i - 1) % 2], 16 * ((i - 1) // 2 + 1))
                            V.tensor_tensor(x, PS[:, (s % 2) * 1024:(s % 2) * 1024 + 1024], x, ALU.add).then_inc(dv_x1, 1)
                        if n == 7 and i < T:
                            dve.wait_ge(pe_v, V_DONE[h - 2])
                            if i >= 1:
                                dve.wait_ge(pe_t, T_ITEM["y", i - 1, 1] + 1)
                            V.tensor_tensor(ob[:, 0:384].rearrange("p (h d) -> p h d", h=DH),
                                            bank(6, 0, 384).rearrange("p (h d) -> p h d", h=DH),
                                            spread(rinv[:, 0:6], 2, [P, DH, DVD]), ALU.mult).then_inc(dv_o, 1)
                        if n == 8 and i >= 1:
                            dve.wait_ge(pl_x1, i)
                            if i >= 2:
                                dve.wait_ge(pe_t, T_ITEM["h2", i - 2, 1] + 1)
                            V.tensor_scalar(h2, xr[(i - 1) % 2], xrs, None, ALU.mult).then_inc(dv_h2, 1)
                        if n == 8 and i < T:
                            dve.wait_ge(a_o, 2 * i + 1)
                            V.tensor_reduce(oss, osq.rearrange("p (h d) -> p h d", h=DH), AX.X,
                                            ALU.add).then_inc(dv_os, 1)
                        if n == 9 and i < T:
                            dve.wait_ge(pl_o, 2 * i + 1)
                            V.tensor_tensor(ob[:, 0:384].rearrange("p (h d) -> p h d", h=DH),
                                            ob[:, 0:384].rearrange("p (h d) -> p h d", h=DH),
                                            spread(ors, 2, [P, DH, DVD]), ALU.mult).then_inc(dv_on, 1)

                dve.wait_ge(a_lg, T)
                for k in range(2):
                    V.memset(xg[k], 0.0).then_inc(dv_xg0, 1)

                def first_max(dst, x, mx, tmp, n):
                    link(V.tensor_reduce(mx, x, AX.X, ALU.max))
                    link(V.tensor_tensor(tmp, x, spread(mx, 2, [P, T, n]), ALU.is_equal))
                    link(V.tensor_tensor(tmp, tmp, spread(c_first[:, 0:n], 1, [P, T, n]), ALU.mult))
                    link(V.tensor_reduce(r_m, tmp, AX.X, ALU.max))
                    link(V.tensor_tensor(dst, tmp, spread(r_m, 2, [P, T, n]), ALU.is_equal))

                link(V.tensor_tensor(lg[:, :, :], lg[:, :, :], spread(rbias, 1, [P, T, G + E]), ALU.add))
                gl = lg[:, :, 0:G]
                first_max(r_oh, gl, r_gm, r_t4, G)
                V.tensor_tensor(r_gs, gl, spread(r_gm, 2, [P, T, G]), ALU.subtract)
                link(V.tensor_tensor(r_prod, lg[:, :, G:G + E].rearrange("p t (g e) -> p t g e", g=G),
                                     spread(r_oh, 3, [P, T, G, EPG]), ALU.mult))
                link(V.tensor_reduce(r_ein, r_prod.rearrange("p t g e -> p t e g"), AX.X, ALU.add))
                link(V.tensor_reduce(r_m, r_ein, AX.X, ALU.max))
                V.tensor_tensor(r_es, r_ein, spread(r_m, 2, [P, T, EPG]), ALU.subtract).then_inc(dv_r, 1)
                dve.wait_ge(a_r, 1)
                V.tensor_reduce(r_pg, r_ge, AX.X, ALU.add)
                link(V.tensor_reduce(r_m, r_p, AX.X, ALU.add))
                V.reciprocal(r_pg, r_pg)
                link(V.reciprocal(r_m, r_m))
                link(V.tensor_tensor(r_p, r_p, spread(r_m, 2, [P, T, EPG]), ALU.mult))
                first_max(r_o1, r_p, r_m1, r_t8, EPG)
                link(V.scalar_tensor_tensor(r_p, r_o1, -2.0, r_p, ALU.mult, ALU.add))
                first_max(r_o2, r_p, r_m2, r_t8, EPG)
                link(V.tensor_tensor(r_m, r_m1, r_m2, ALU.add))
                link(V.reciprocal(r_m, r_m))
                link(V.tensor_tensor(r_m, r_m, r_pg, ALU.mult))
                V.tensor_tensor(gate1, r_m1, r_m, ALU.mult)
                V.tensor_tensor(gate2, r_m2, r_m, ALU.mult)
                for mk, o in ((r_M1, r_o1), (r_M2, r_o2)):
                    V.tensor_tensor(mk.rearrange("p t (g e) -> p t g e", g=G), spread(r_oh, 3, [P, T, G, EPG]),
                                    spread(o, 2, [P, T, G, EPG]), ALU.mult)
                link(V.memset(r_pre[:, 0, :], 0.0))
                link(V.tensor_tensor(r_M, r_M1, r_M2, ALU.add))
                for k in range(T):
                    link(V.tensor_tensor(r_pre[:, k + 1, :], r_pre[:, k, :], r_M[:, k, :], ALU.add))
                V.tensor_copy(r_cnt, r_pre[:, T, :]).then_inc(dv_r, 1)
                dve.wait_ge(pe_r, 1)
                rank = bank(7, 0, T * E).rearrange("p (t e) -> p t e", t=T)
                link(V.tensor_copy(r_cnt, bank(7, T * E, T * E + E)))
                link(V.tensor_scalar(r_ov, r_cnt, float(P), None, ALU.is_gt))
                for k in range(2, SEQ // P):
                    link(V.scalar_tensor_tensor(r_ov, r_cnt, float(k * P), r_ov, ALU.is_gt, ALU.add))
                link(V.tensor_tensor_scan(r_inc, ones[:, 0:E], r_ov, 0.0, ALU.mult, ALU.add))
                link(V.tensor_tensor(r_ov, r_inc, r_ov, ALU.subtract))
                link(V.scalar_tensor_tensor(r_ov, r_ov, float(P), c_toov, ALU.mult, ALU.add))
                link(V.scalar_tensor_tensor(r_sl, rank, float(P), spread(r_ov, 1, [P, T, E]), ALU.is_ge, ALU.mult))
                link(V.tensor_tensor(r_sl, rank, r_sl, ALU.add))
                link(V.tensor_tensor(r_sl, r_sl, spread(c_e128, 1, [P, T, E]), ALU.add))
                for k, mk in enumerate((r_M1, r_M2)):
                    link(V.tensor_tensor(mk, mk, r_sl, ALU.mult))
                    link(V.tensor_reduce(r_m, mk, AX.X, ALU.add))
                    ins = V.tensor_copy(slot_i[:, k * T:(k + 1) * T], r_m)
                    if k == 0:
                        link(ins)
                ins.then_inc(dv_slot, 1)
                link(V.tensor_tensor(r_le, spread(r_inc, 1, [P, NOV, E]), spread(c_j, 2, [P, NOV, E]), ALU.is_le))
                link(V.tensor_reduce(r_ej, r_le, AX.X, ALU.add))
                link(V.tensor_scalar(r_ej, r_ej, float(E - 1), None, ALU.min))
                V.tensor_copy(ov_i[:, 0:NOV], r_ej)
                V.tensor_copy(ov_i[:, NOV:NOV + 1], r_inc[:, E - 1:E])
                link(V.tensor_copy(ov_i[:, NOV + 1:NOV + 2], ov_tot[:, :]))
                V.tensor_tensor(ov_tot[:, :], ov_tot[:, :], r_inc[:, E - 1:E], ALU.add).then_inc(dv_slot, 1)
                dve.wait_ge(pe_r, 2)
                V.tensor_copy(gidx[:, :], bank(7, 320, 320 + NBLK)).then_inc(dv_idx, 1)
                dve.wait_ge(dv_idx, 1)

                def rows_out(b4, b):
                    k = b % 2
                    if not (isinstance(b4, int) and 4 * b4 + b < 2):
                        dve.wait_ge(m_up, 4 * b4 + b - 1)
                    for c in range(2):
                        dve.wait_ge(m_tx, 8 * b4 + 2 * b + c + 1)
                        V.tensor_tensor(xgT[k][:, 4 * c:4 * c + 4, :], bank(c).rearrange("p (a b) -> p a b", a=4),
                                        spread(prm[:, R_G2 + 4 * c:R_G2 + 4 * c + 4], 2, [P, 4, P]),
                                        ALU.mult).then_inc(m_xt, 1)

                def hidden(b4, b):
                    k = b % 2
                    dve.wait_ge(m_th, 4 * b4 + b + 1)
                    V.scalar_tensor_tensor(th[k], th[k], 1.0, bank(2 + k, 0, FE), ALU.add, ALU.mult).then_inc(m_u, 1)
                    dve.wait_ge(m_u, 4 * b4 + b + 1)
                    if not (isinstance(b4, int) and 4 * b4 + b < 2):
                        dve.wait_ge(m_ht, 4 * b4 + b - 1)
                    V.scalar_tensor_tensor(hh[k], th[k], 0.5, bank(2 + k, FE, 2 * FE), ALU.mult,
                                           ALU.mult).then_inc(m_h, 1)

                rows_out(0, 0)
                rows_out(0, 1)
                hidden(0, 0)
                for b in range(4):
                    hidden(0, b + 1)
                    rows_out(0, b + 2)
                with dve.Fori(1, E // 4 - 1) as it:
                    for b in range(4):
                        hidden(it, b + 1)
                        rows_out(it, b + 2)
                for b in range(4):
                    if b < 3:
                        hidden(E // 4 - 1, b + 1)
                    if b < 2:
                        rows_out(E // 4 - 1, b + 2)
                n = dve.value_load(ov_i[0:1, NOV:NOV + 1], min_val=0, max_val=NOV)
                with dve.Fori(0, NOV) as j:
                    with dve.If(j < n):
                        for c in range(2):
                            dve.wait_ge(o_tx, 2 * j + c + 1)
                            V.tensor_tensor(xgT[0][:, 4 * c:4 * c + 4, :], bank(c).rearrange("p (a b) -> p a b", a=4),
                                            spread(prm[:, R_G2 + 4 * c:R_G2 + 4 * c + 4], 2, [P, 4, P]),
                                            ALU.mult).then_inc(o_xt, 1)
                        dve.wait_ge(o_th, j + 1)
                        V.scalar_tensor_tensor(th[0], th[0], 1.0, bank(2, 0, FE), ALU.add, ALU.mult).then_inc(o_u, 1)
                        dve.wait_ge(o_u, j + 1)
                        V.scalar_tensor_tensor(hh[0], th[0], 0.5, bank(2, FE, 2 * FE), ALU.mult,
                                               ALU.mult).then_inc(o_h, 1)

                dve.wait_ge(s_x1l, 16)
                for i in range(T):
                    dve.wait_ge(g_y[i % 2], l * (16 * T) + 32 * (i // 2 + 1))
                    V.scalar_tensor_tensor(X[:, i, :], yg[i % 2][0], gate1[:, i:i + 1], X[:, i, :], ALU.mult,
                                           ALU.add).then_inc(c_t, 1)
                    dve.wait_ge(c_t, i + 1)
                    V.scalar_tensor_tensor(X[:, i, :], yg[i % 2][1], gate2[:, i:i + 1], X[:, i, :], ALU.mult,
                                           ALU.add).then_inc(c_x, 1)
                dve.wait_ge(c_x, T)
                dve.drain().then_inc(end_dve, 1)

        @block.tensor
        def _(pe):
            MM, TR = nc.tensor.matmul, nc.tensor.transpose

            def released(key):
                kind, i = key
                if kind == "lru":
                    return l_u, i + 1
                if kind in (1, 2):
                    return dv_qn, (kind - 1) * T + i + 1
                if kind == "gate":
                    return l_sig, i + 1
                if kind == 3:
                    return a_v, i + 1
                if kind == 4:
                    return dv_qn, 2 * T + i + 1
                if kind == "lss":
                    return l_ms, i + 1
                return dv_kn, 3 * (i // 2) + i % 2 + 1

            key_of = {n: k for k, n in PJ.items()}

            def take(key):
                n = PJ[key]
                if n >= 4:
                    pe.wait_ge(*released(key_of[n - 4]))
                return n % 4

            def slot(key):
                s = S_ITEM[key]
                if s >= 2:
                    k = s_key[s - 2]
                    if k[0] == "map":
                        pe.wait_ge(dv_pass, MAPS_BEFORE[k[1]] + k[2] + 1)
                    else:
                        pe.wait_ge(dv_q if k[0] == "q" else dv_x1, k[1] + 1)
                return (s % 2) * 1024

            def turn_bank(key):
                t = T_ITEM[key]
                if t >= 2:
                    k = t_key[t - 2]
                    if k[0] == "p":
                        pe.wait_ge(a_pt, (V_DONE[k[1] - 1] if k[1] else 0) + k[2] + 1)
                    elif k[0] == "q":
                        pe.wait_ge(a_qT, 2 * k[1] + k[2] + 1)
                    elif k[0] == "y":
                        pe.wait_ge(a_yT, 6 * k[1] + (4, 6)[k[2]])
                    elif k[0] == "h2":
                        pe.wait_ge(a_h2T, 8 * k[1] + 4 * k[2] + 4)
                    else:
                        pe.wait_ge(a_lg, k[1] + 1)
                return 4 + t % 2

            s_key = {n: k for k, n in S_ITEM.items()}
            t_key = {n: k for k, n in T_ITEM.items()}

            pe.wait_ge(s_con, 64)
            with pe.Fori(0, DEPTH) as l:
                new_layer(pe, l)
                pe.wait_ge(s_row, 16 * 24)
                TR(bank(7, 0, NROW), rows, ident[0:NROW, 0:NROW]).then_inc(pe_par, 1)
                for i in range(T):
                    pe.wait_ge(dv_xs, i + 1)
                    for c in range(2):
                        if i >= 1:
                            pe.wait_ge(dv_xe, 2 * (i - 1) + c + 1)
                        for k in range(4):
                            o = (4 * c + k) * P
                            ins = TR(bank(4 + c, k * P, k * P + P), xs[i % 2][:, o:o + P], ident)
                        ins.then_inc(pe_xn, 1)
                pe.wait_ge(dv_xe, 2 * T)

                def token_major(g, i):
                    c, n = GROUPS[g]
                    if i == 0:
                        pe.wait_ge(s_win[g % 2], 16 * (g // 2 + 1))
                    b = take((g, i))
                    for k in range(KC):
                        ins = MM(bank(b, 0, n), xnT[:, k, tile(i)], w_in_sb[g % 2][:, k, 0:n], start=(k == 0),
                                 stop=(k == KC - 1))
                    ins.then_inc(pe_pj, 1)

                def turn_qk(q):
                    pe.wait_ge(dv_qn, q + 1)
                    if q >= 2:
                        pe.wait_ge(*((dv_qT, q - 1) if q - 2 < T else (a_kT, q - 1 - T)))
                    for k in range(3):
                        ins = TR(bank(4 + q % 2, k * P, k * P + P), qn[q % 2][:, k * P:k * P + P], ident)
                    ins.then_inc(pe_tr, 1)

                def turn_latents(i):
                    q = 2 * T + i
                    pe.wait_ge(dv_qn, q + 1)
                    pe.wait_ge(*((a_kT, T - 1 + i) if i < 2 else (dv_cT, i - 1)))
                    b = 4 + q % 2
                    TR(bank(b, 0, P), qn[q % 2][:, 0:P], ident)
                    TR(bank(b, P, 2 * P, parts=64), qn[q % 2][:, P:QR], ident)
                    TR(bank(b, 2 * P, 3 * P), qn[q % 2][:, QR:QR + KVR], ident).then_inc(pe_tr, 1)

                pe.wait_ge(s_win[0], 16)
                for m in range(8):
                    f, c = m // 2, m % 2
                    b = take(("lru", m))
                    for k in range(KC):
                        ins = MM(bank(b), w_in_sb[0][:, k, f * P:f * P + P], xnT[:, k, 512 * c:512 * c + 512],
                                 start=(k == 0), stop=(k == KC - 1))
                    ins.then_inc(pe_pj, 1)
                for q in range(2 * T):
                    token_major(1 + q // T, q % T)
                    if q >= 1:
                        turn_qk(q - 1)
                    if q == T:
                        pe.wait_ge(l_conv, 8)
                        pe.wait_ge(s_wab, 128)
                        for n in range(8):
                            m, f, c = n // 4, (n // 2) % 2, n % 2
                            b = take(("gate", n))
                            MM(bank(b), wab[:, m, f, :], l_xc[:, f, 512 * c:512 * c + 512], start=True,
                               stop=True).then_inc(pe_pj, 1)
                for i in range(T):
                    token_major(3, i)
                    if i == 0:
                        turn_qk(2 * T - 1)
                for i in range(T):
                    token_major(4, i)
                    if i >= 1:
                        turn_latents(i - 1)
                turn_latents(T - 1)
                pe.wait_ge(l_y2, 1)
                for c in range(2):
                    b = take(("lss", c))
                    for f in range(2):
                        ins = MM(bank(b), ones, l_t2[:, f, 512 * c:512 * c + 512], start=(f == 0), stop=(f == 1))
                    ins.then_inc(pe_pj, 1)

                def turn_keys(i):
                    pe.wait_ge(dv_kn, 3 * i + 3)
                    for c in range(2):
                        r = 3 * T + 2 * i + c
                        if i == 0:
                            pe.wait_ge(dv_cT, T - 1 + c)
                        else:
                            pe.wait_ge(a_kTm, 2 * i + c - 1)
                        for k in range(4 - 2 * c):
                            o = (4 * c + k) * MQK
                            ins = TR(bank(4 + r % 2, k * P, k * P + P, parts=MQK),
                                     qn[(3 * T + i) % 2][:, o:o + MQK], ident)
                        ins.then_inc(pe_tr, 1)

                pe.wait_ge(s_wkv, 16)
                pe.wait_ge(dv_cT, T)
                for i in range(T):
                    for c in range(2):
                        b = take(("kv", 2 * i + c))
                        MM(bank(b, 0, 384), ckvT[:, tile(i)], wukv[:, 384 * c:384 * c + 384], start=True,
                           stop=True).then_inc(pe_pj, 1)
                    if i >= 1:
                        turn_keys(i - 1)
                turn_keys(T - 1)

                pe.wait_ge(dv_kn, 3 * T)
                pe.wait_ge(a_kTm, 2 * T)
                pe.wait_ge(a_vm, 2 * T)
                pe.wait_ge(dv_qT, T)
                pe.wait_ge(a_kT, T)
                pe.wait_ge(a_v, T)
                pe.wait_ge(l_ms, 2)
                pe.wait_ge(s_wq, 32)
                vc = [0]

                def scores(h):
                    i, n = h // HEADS, h % HEADS
                    nk = (i + 1) * P
                    if n == DH:
                        pe.wait_ge(a_qT, 2 * i + 2)
                    for m in range(2 if n < DH else 1):
                        o = slot(("map", h, m))
                        if n < DH:
                            mp = 2 * n + m
                            r = 32 * (mp % 4)
                            lhs, rhs = qT[r:r + 32, mp // 4, tile(i)], kT[r:r + 32, mp // 4, 0:nk]
                        else:
                            lhs, rhs = qTm[:, n - DH, :], kTm[:, n - DH, 0:nk]
                        for c in range(0, nk, 512):
                            w = min(512, nk - c)
                            ins = MM(PS[:, o + c:o + c + w], lhs, rhs[:, c:c + w], start=True, stop=True)
                        ins.then_inc(pe_s, 1)

                def turn_p(h):
                    if is_diff(h):
                        pe.wait_ge(dv_comb, DIFFS_UPTO[h])
                    else:
                        pe.wait_ge(a_exp, MAPS_BEFORE[h + 1])
                    for c, (lo, hi) in enumerate(chunks_of(h)):
                        b = turn_bank(("p", h, c))
                        for k in range(lo, hi):
                            ins = TR(bank(b, (k - lo) * P, (k - lo) * P + P), Pm[(h % 2) * 2][:, k * P:k * P + P],
                                     ident)
                        ins.then_inc(pe_t, 1)

                def pv(h):
                    i, n = h // HEADS, h % HEADS
                    if n % DH == 0 and i >= 1:
                        pe.wait_ge(dv_o, 2 * i - 1 if n == 0 else 2 * i)
                    o = 64 * (n % DH)
                    for lo, hi in chunks_of(h):
                        pe.wait_ge(a_pt, vc[0] + 1)
                        for k in range(lo, hi):
                            v = Vd[:, k, n * DVD:(n + 1) * DVD] if n < DH else Vm[:, k, n - DH, :]
                            ins = MM(bank(6 + n // DH, o, o + 64), PT[vc[0] % 4][:, (k - lo) * P:(k - lo) * P + P], v,
                                     start=(k == 0), stop=(k == i))
                        ins.then_inc(pe_v, 1)
                        vc[0] += 1

                def turn(key, srcs, parts=P):
                    b = turn_bank(key)
                    for k, src in enumerate(srcs):
                        ins = TR(bank(b, k * P, k * P + P, parts=parts), src, ident)
                    ins.then_inc(pe_t, 1)

                scores(0)
                scores(1)
                for i in range(T + 1):
                    for n in range(HEADS):
                        h = i * HEADS + n
                        if h + 2 < NH:
                            scores(h + 2)
                        if i < T:
                            turn_p(h)
                        if 0 <= h - 1 < NH:
                            pv(h - 1)
                        if n == 0 and i < T:
                            o = slot(("q", i))
                            for c, (lo, hi) in enumerate(((0, 384), (384, 576))):
                                dst = PS[:, o + 512 * c:o + 512 * c + hi - lo]
                                MM(dst, cqT[:, 0, tile(i)], wuq[:, 0, lo:hi], start=True, stop=False)
                                ins = MM(dst, cqT[0:QR - P, 1, tile(i)], wuq[0:QR - P, 1, lo:hi], start=False,
                                         stop=True)
                            ins.then_inc(pe_s, 1)
                        if n == 3 and i < T:
                            pe.wait_ge(dv_qr, i + 1)
                            turn(("q", i, 0), [qraw[:, k, :] for k in range(4)], MQK)
                            turn(("q", i, 1), [qraw[:, k, :] for k in range(4, 6)], MQK)
                        if n == 4 and i >= 1:
                            pe.wait_ge(dv_on, 2 * i)
                            turn(("y", i - 1, 0), [ob[:, k * P:k * P + P] for k in range(4)])
                            turn(("y", i - 1, 1), [ob[:, k * P:k * P + P] for k in range(4, 6)])
                        if n == 6 and i >= 1:
                            pe.wait_ge(a_yT, 6 * i)
                            pe.wait_ge(l_fin, 2)
                            pe.wait_ge(s_wout, 32)
                            o = slot(("out", i - 1))
                            for c in range(2):
                                for k in range(KC):
                                    lhs = yl[:, k, tile(i - 1)] if k < 2 else yT[:, k - 2, :]
                                    ins = MM(PS[:, o + 512 * c:o + 512 * c + 512], lhs,
                                             w_out_sb[:, k, 512 * c:512 * c + 512], start=(k == 0),
                                             stop=(k == KC - 1))
                            ins.then_inc(pe_s, 1)
                        if n == 9 and i >= 1:
                            pe.wait_ge(dv_h2, i)
                            for c in range(2):
                                turn(("h2", i - 1, c), [h2[:, k * P:k * P + P] for k in range(4 * c, 4 * c + 4)])
                        if n == 10 and i >= 1:
                            pe.wait_ge(a_h2T, 8 * i)
                            pe.wait_ge(s_wr, 32)
                            b = turn_bank(("route", i - 1))
                            for k in range(KC):
                                ins = MM(bank(b, 0, G + E), h2T[:, k, :], wr[:, k, :], start=(k == 0),
                                         stop=(k == KC - 1))
                            ins.then_inc(pe_t, 1)

                pe.wait_ge(dv_r, 2)
                MM(bank(7, 0, T * E), tri, r_M.rearrange("p t e -> p (t e)"), start=True, stop=False)
                MM(bank(7, 0, T * E), ones, r_pre[:, 0:T, :].rearrange("p t e -> p (t e)"), start=False, stop=True)
                MM(bank(7, T * E, T * E + E), ones, r_pre[:, T, :], start=True, stop=True).then_inc(pe_r, 1)
                pe.wait_ge(dv_slot, 2)
                pe.wait_ge(s_rtl, 16)
                TR(bank(7, 320, 320 + NBLK), toks[0:NBLK, :], ident[0:NBLK, 0:NBLK]).then_inc(pe_r, 1)

                def turn_rows(b4, b):
                    k = b % 2
                    first = isinstance(b4, int) and 4 * b4 + b == 0
                    pe.wait_ge(g_x[k], l * (8 * E) + (32 * b4 + 16 * (b // 2) + 16))
                    for c in range(2):
                        if not first:
                            pe.wait_ge(m_xt, 8 * b4 + 2 * b + c - 1)
                        for m in range(4):
                            o = (4 * c + m) * P
                            ins = TR(bank(c, m * P, m * P + P), xg[k][:, o:o + P], ident)
                        ins.then_inc(m_tx, 1)

                def up(b4, b):
                    k, w = b % 2, b % 4
                    pe.wait_ge(m_xt, 8 * b4 + 2 * b + 2)
                    if not (isinstance(b4, int) and 4 * b4 + b < 2):
                        pe.wait_ge(m_h, 4 * b4 + b - 1)
                    pe.wait_ge(s_w13[w], 32 * b4 + 32 * (b // 4 + 1))
                    for m in range(KC):
                        ins = MM(bank(2 + k), xgT[k][:, m, :], w_ex[w][0][:, :, m, :], start=(m == 0),
                                 stop=(m == KC - 1))
                    ins.then_inc(m_up, 1)

                def turn_hidden(b4, b):
                    k = b % 2
                    pe.wait_ge(m_h, 4 * b4 + b + 1)
                    if not (isinstance(b4, int) and 4 * b4 + b == 0):
                        pe.wait_ge(m_hte, 4 * b4 + b)
                    for m in range(2):
                        ins = TR(bank(4, m * P, m * P + P), hh[k][:, m * P:m * P + P], ident)
                    ins.then_inc(m_ht, 1)

                def down(b4, b):
                    k, w = b % 2, b % 4
                    pe.wait_ge(m_hte, 4 * b4 + b + 1)
                    pe.wait_ge(s_w2[w], 16 * b4 + 16 * (b // 4 + 1))
                    for c in range(2):
                        if not (isinstance(b4, int) and 4 * b4 + b == 0):
                            pe.wait_ge(m_y, 8 * b4 + 2 * b + c - 1)
                        for m in range(2):
                            ins = MM(bank(5 + c), hT[k][:, m, :], w_ex[w][1][:, m, 512 * c:512 * c + 512],
                                     start=(m == 0), stop=(m == 1))
                        ins.then_inc(m_dn, 1)

                turn_rows(0, 0)
                turn_rows(0, 1)
                up(0, 0)
                for b in range(4):
                    up(0, b + 1)
                    turn_hidden(0, b)
                    turn_rows(0, b + 2)
                    down(0, b)
                with pe.Fori(1, E // 4 - 1) as it:
                    for b in range(4):
                        up(it, b + 1)
                        turn_hidden(it, b)
                        turn_rows(it, b + 2)
                        down(it, b)
                for b in range(4):
                    if b < 3:
                        up(E // 4 - 1, b + 1)
                    turn_hidden(E // 4 - 1, b)
                    if b < 2:
                        turn_rows(E // 4 - 1, b + 2)
                    down(E // 4 - 1, b)
                pe.wait_ge(m_y, 2 * E)
                pe.sem_inc(o_free, 1)
                n = pe.value_load(ov_i[0:1, NOV:NOV + 1], min_val=0, max_val=NOV)
                before = pe.value_load(ov_i[0:1, NOV + 1:NOV + 2], min_val=0, max_val=NOV * DEPTH)
                with pe.Fori(0, NOV) as j:
                    with pe.If(j < n):
                        pe.wait_ge(g_ov, 16 * before + 16 * j + 16)
                        for c in range(2):
                            for m in range(4):
                                o = (4 * c + m) * P
                                ins = TR(bank(c, m * P, m * P + P), xg[0][:, o:o + P], ident)
                            ins.then_inc(o_tx, 1)
                        pe.wait_ge(o_xt, 2 * j + 2)
                        pe.wait_ge(o_w, 48 * j + 48)
                        for m in range(KC):
                            ins = MM(bank(2), xgT[0][:, m, :], w_ex[0][0][:, :, m, :], start=(m == 0),
                                     stop=(m == KC - 1))
                        ins.then_inc(o_up, 1)
                        pe.wait_ge(o_h, j + 1)
                        for m in range(2):
                            ins = TR(bank(4, m * P, m * P + P), hh[0][:, m * P:m * P + P], ident)
                        ins.then_inc(o_ht, 1)
                        pe.wait_ge(o_hte, j + 1)
                        for c in range(2):
                            for m in range(2):
                                ins = MM(bank(5 + c), hT[0][:, m, :], w_ex[0][1][:, m, 512 * c:512 * c + 512],
                                         start=(m == 0), stop=(m == 1))
                        ins.then_inc(o_dn, 1)
                        pe.wait_ge(o_y, j + 1)
                        pe.sem_inc(o_free, 1)
                pe.drain().then_inc(end_pe, 1)


_INS = ["x", "norm1_g", "w_in", "lru_conv_w", "lru_conv_b", "lru_wa", "lru_ba", "lru_wx", "lru_bx", "lru_lambda",
        "lru_out_g", "diff_q_g", "diff_k_g", "diff_lq1", "diff_lk1", "diff_lq2", "diff_lk2", "diff_sub_g",
        "mla_cq_g", "mla_ckv_g", "mla_w_uq", "mla_w_ukv", "mla_q_g", "mla_k_g", "mla_out_g", "w_out", "norm2_g",
        "router_g_w", "router_g_b", "router_e_w", "router_e_b", "exp_w1", "exp_w3", "exp_w2"]


def kernel(**inputs):
    import concourse.bacc as bacc
    from concourse.bass_utils import run_bass_kernel_spmd

    nc = bacc.Bacc("TRN2", target_bir_lowering=False, num_devices=1)
    arrays, aps = {}, {}
    for name, value in [(n, inputs[n]) for n in _INS] + list(constants().items()):
        value = np.ascontiguousarray(value)
        arrays[f"in_{name}"] = value
        aps[name] = nc.dram_tensor(f"in_{name}", value.shape, mybir.dt.from_np(value.dtype), kind="ExternalInput").ap()
    out = nc.dram_tensor("out_0", (1, SEQ, D), F32, kind="ExternalOutput").ap()
    build(nc, aps, out)
    r = run_bass_kernel_spmd(nc, [arrays], core_ids=[0])
    return r.results[0]["out_0"]
```

```python
from contextlib import ExitStack

import numpy as np

import concourse.bass as bass
from concourse import mybir

F32 = mybir.dt.float32
F32R = mybir.dt.float32r
I32 = mybir.dt.int32
ALU = mybir.AluOpType
ACT = mybir.ActivationFunctionType
AX = mybir.AxisListType

P = 128
SEQ, D = 1024, 1024
DEPTH = 2
T = SEQ // P
KC = D // P
CHUNK = 64
LRU = 256
DH, DHD, DVD = 6, 32, 64
MH, MN, MR, MV = 6, 64, 32, 64
MQK = MN + MR
QR, KVR = 192, 128
G, EPG = 4, 8
E = G * EPG
FE = 256
EPS = 1e-6
HEADS = DH + MH
RG_C = 8.0
DSCALE = DHD ** -0.5
MSCALE = MQK ** -0.5
SLOPE = [2.0 ** (-8.0 * (h + 1) / DH) for h in range(DH)]
GELU_C = 0.7978845608028654
LAMBDA_INIT = [0.8 - 0.6 * float(np.exp(-0.3 * l)) for l in range(DEPTH)]
MASKED = -1.0e30
NO_ROW = 4 * SEQ

GROUPS = [(0, 512), (512, 384), (896, 384), (1280, 384), (1664, 352)]

R_G1, R_G2, R_LOUT, R_SUB, R_MOUT, R_CQ, R_CKV = 0, 8, 16, 18, 19, 22, 24
R_CW, R_CB, R_BA, R_BX, R_LAM, R_DQ, R_DK, R_MQ, R_MK, R_G2P, NROW = 25, 33, 35, 37, 39, 41, 42, 43, 44, 45, 53

NWIDE = 4 * DHD + 4 * MR + G + E

NOV = (2 * SEQ - 1) // P
NBLK = E + NOV

DIFF_TILES = [7, 0, 6, 1, 5, 2, 4, 3]
MLA_TILES = [0, 7, 1, 6, 2, 5, 3, 4]
UNITS = [unit for p in range(DH) for d, m in zip(DIFF_TILES, MLA_TILES) for unit in ((0, p, d), (1, p, m))]
NU = len(UNITS)
PAIR = NU // DH


def chunks_of(u):
    n = UNITS[u][2] + 1
    return [(c, min(c + 4, n)) for c in range(0, n, 4)]


def maps_of(u):
    return 1 if UNITS[u][0] else 2


AHEAD = 3
NYG = 4
NPM = AHEAD + 1

MAPS_BEFORE = [sum(maps_of(v) for v in range(u)) for u in range(NU + 1)]
DIFFS_BEFORE = [sum(1 - UNITS[v][0] for v in range(u)) for u in range(NU + 1)]
CHUNKS_BEFORE = [sum(len(chunks_of(v)) for v in range(u)) for u in range(NU + 1)]


def number_projections():
    order = [("lru", k) for k in range(8)]
    order += [(1, i) for i in range(T)]
    order += [(2, 0)] + [("gate", k) for k in range(8)] + [(2, i) for i in range(1, T)]
    order += [(3, i) for i in range(T)] + [(4, i) for i in range(T - 2)]
    order += [("lss", k) for k in range(2)] + [(4, i) for i in range(T - 2, T)]
    order += [(kind, 2 * i + c) for i in range(T) for kind in ("kv", "qu") for c in range(2)]
    return {k: n for n, k in enumerate(order)}


PJ = number_projections()


def head_bank(kind, n):
    return n % 2 if kind == "kv" else (2, 3, 6, 7)[n % 4]


def constants():
    p = np.arange(P)[:, None]
    c = np.arange(SEQ)[None, :]
    q = p + SEQ - P
    barred = (c // CHUNK) > (q // CHUNK)
    dist = np.where(barred, MASKED, -np.abs(q - c).astype(np.float32)).astype(np.float32)
    mask = np.where(barred, MASKED, 0.0).astype(np.float32)
    half = MR // 2
    inv = (np.float32(10000.0) ** (-np.arange(half, dtype=np.float32) / half)).astype(np.float32)
    ang = np.arange(SEQ, dtype=np.float32)[:, None] * inv[None, :]
    co, si = np.cos(ang).astype(np.float32), np.sin(ang).astype(np.float32)
    rope = np.concatenate([co, si, si, co], 1).reshape(T, P, 2 * MR).transpose(1, 0, 2).reshape(P, -1)
    slope = np.zeros((P, 3), np.float32)
    for k in range(3):
        for m in range(4):
            slope[32 * m:32 * m + 32, k] = DSCALE / SLOPE[(4 * k + m) // 2]
    misc = np.zeros((P, 320), np.float32)
    misc[:, 0:3] = slope
    for l in range(DEPTH):
        misc[:, 4 + 2 * l] = 1.0 - LAMBDA_INIT[l]
        misc[:, 5 + 2 * l] = LAMBDA_INIT[l]
    misc[:, 16:24] = 8 - np.arange(8)
    misc[:, 24:56] = P * np.arange(E)
    misc[:, 56:88] = E * P - P - P * np.arange(E)
    misc[:, 88:103] = np.arange(NOV)
    misc[:, 103] = EPS
    misc[:, 104:116] = -0.5
    misc[:, 116:244] = np.arange(P)[None, :]
    misc[:, 244:252] = np.arange(T)[None, :] * P + p - NO_ROW
    misc[:, 252:260] = np.arange(T)[None, :] * P + p + SEQ - NO_ROW
    tri = (np.arange(P)[:, None] < np.arange(P)[None, :]).astype(np.float32)
    mats = np.concatenate([np.eye(P, dtype=np.float32), np.ones((P, P), np.float32), tri], 1)
    return {"c_dist": dist, "c_mask": mask, "c_rope": np.ascontiguousarray(rope), "c_misc": misc, "c_mats": mats}


def build(nc, a, out):
    x1d = nc.dram_tensor("x1_rows", [SEQ, D], F32)
    xrd = out.rearrange("o s d -> (o s) d")
    h2d = nc.dram_tensor("h2_rows", [SEQ, D], F32)
    yd = nc.dram_tensor("y_rows", [2 * SEQ, D], F32)
    qkd = nc.dram_tensor("qk_parts", [4, DH * 2 * DHD, SEQ], F32)

    with ExitStack() as ctx:
        KB = 256
        MEM = 206 * KB + 128
        def rounded(name, word, *shape, parts=P):
            n = int(np.prod(shape))
            with ExitStack() as gone:
                if word:
                    gone.enter_context(nc.sbuf_tensor(name + "_below", [P, word], F32))
                v = gone.enter_context(nc.sbuf_tensor(name, [P, n], F32))
            return v[0:parts, :].rearrange("p (a b) -> p a b", a=shape[0])

        RC = 64 * KB
        WO_LO = [0, 4, 8, 12, 32, 36, 40, 44]
        WO_HI = [64, 68, 72, 76, 80, 48, 52, 84]
        wo_hi = [rounded(f"w_out_high{k}", WO_HI[k] * KB, 1, D) for k in range(KC)]
        wo_lo = [rounded(f"w_out_low{k}", WO_LO[k] * KB, 1, D) for k in range(KC)]
        yl_hi, yl_lo = rounded("y_lru_high", 88 * KB, 2, SEQ), rounded("y_lru_low", 158 * KB, 2, SEQ)
        yT_lo = [rounded(f"y_low{k}", (144 + 3 * k) * KB, 6, P) for k in range(2)]
        yT_hi = [rounded(f"y_high{k}", (150 + 3 * k) * KB, 6, P) for k in range(2)]
        qk_hi = [rounded(f"qk_high{k}", RC + 12 * KB * k, 3, 512) for k in range(2)]
        qk_lo = [rounded(f"qk_low{k}", RC + 12 * KB * k + 6 * KB, 3, 512) for k in range(2)]
        kst = [rounded(f"k_stack{k}", 16 * KB * k, 2, SEQ, parts=3 * DHD) for k in range(2)]
        qst = [rounded(f"q_stack{k}", 16 * KB * k + 8 * KB, 2, SEQ, parts=3 * DHD) for k in range(2)]
        mem = ctx.enter_context(nc.sbuf_tensor("mem", [P, MEM], F32))
        PS = ctx.enter_context(nc.psum_tensor("PS", [P, 8 * 512], F32))
        slot_i = ctx.enter_context(nc.sbuf_tensor("slot_i", [P, 2 * T], I32))
        row_i = ctx.enter_context(nc.sbuf_tensor("row_i", [P, 2 * T], I32))
        ov_i = ctx.enter_context(nc.sbuf_tensor("ov_i", [P, NOV + 2], I32))
        gidx = ctx.enter_context(nc.sbuf_tensor("gidx", [P, NBLK], I32))
        yidx = ctx.enter_context(nc.sbuf_tensor("yidx", [P, NBLK], I32))
        ov_tot = ctx.enter_context(nc.sbuf_tensor("ov_tot", [P, 1], F32))

        def at(word, *shape, parts=P):
            n = int(np.prod(shape))
            v = mem[0:parts, word:word + n]
            if len(shape) == 2:
                return v.rearrange("p (a b) -> p a b", a=shape[0])
            if len(shape) == 3:
                return v.rearrange("p (a b c) -> p a b c", a=shape[0], b=shape[1])
            return v

        def bank(b, lo=0, hi=512, parts=P):
            return PS[0:parts, b * 512 + lo:b * 512 + hi]

        def spread(ap, axis, shape):
            return ap.unsqueeze(axis).to_broadcast(shape)

        def tile(i):
            return slice(i * P, (i + 1) * P)

        RA, RB, RD, RE, RL = 0, 32 * KB, 100 * KB, 136 * KB, 158 * KB
        top = [166 * KB]
        X = at(RC, T, D)
        xnT = at(RA, KC, SEQ)
        w_in_sb = [at(RB, KC, 512), at(RB + 16 * KB, KC, 512)]
        xsq = [at(RD + 4 * KB * k, D) for k in range(2)]
        xs = [at(RD + 16 * KB + 4 * KB * k, D) for k in range(2)]
        l_xc, l_t2, l_t3, l_t4 = (at(RD + 8 * KB * k, 2, SEQ) for k in range(4))
        l_t5 = at(RE, 2, SEQ)
        l_in = at(RE + 13 * KB, 2, SEQ + 3)
        l_g = at(RE + 13 * KB, 2, SEQ)
        yl = at(RL, 2, SEQ)
        rows = at(RD + 32 * KB, P, parts=NROW)
        wide = at(top[0], NWIDE)
        lqk, gr = at(top[0], 4, DHD), at(top[0] + 4 * DHD, 2, 2 * MR)
        rbias = at(top[0] + 4 * DHD + 4 * MR, G + E)
        top[0] += NWIDE
        ropes = at(RD + 32 * KB + 3 * P, T, 64)
        qk = [at(RC + 12 * KB * k + 6 * KB, 3, 512) for k in range(2)]
        wukv = at(RB + 24 * KB, MH * (MN + MV))
        cqT = at(RE, 2, SEQ)
        ckvT = at(RE + 8 * KB, SEQ)
        kr = at(RE + 12 * KB, T, MR)
        kTm = at(RB, MH, SEQ, parts=MQK)
        qTm = at(RC, MH, SEQ, parts=MQK)
        Vd = at(RC + 24 * KB, T, DH * DVD)
        Vm = at(RD, T, MH, MV)
        O = at(RD + 12 * KB, T, HEADS * 64)
        w_out_sb = [at(WO_LO[k] * KB, 1, D) for k in range(KC)]
        xr = [at(16 * KB + 4 * KB * k, D) for k in range(2)]
        h2 = [at(24 * KB + 4 * KB * k, D) for k in range(2)]
        h2T = [at(RE + 4 * KB * k, KC, P) for k in range(2)]
        yT = [at(RE + 8 * KB + 3 * KB * k, 6, P) for k in range(2)]
        xsq2 = at(RD + 6 * KB, D)
        w_ex = [(at(o, 2, KC, FE), at(o + 16 * KB, 2, D)) for o in (0, 24 * KB, RD, RE)]
        xg = [at(48 * KB + 4 * KB * k, D) for k in range(2)]
        xgp = [x.rearrange("t (p k) -> t k p", k=KC) for x in xg]
        yo = [at(56 * KB + 4 * KB * k, D) for k in range(2)]
        xgT = [at(RD + 24 * KB + 4 * KB * k, KC, P) for k in range(2)]
        yg = [[at(8 * KB * k + 4 * KB * m, D) for m in range(2)] for k in range(NYG)]

        def new(*shape, parts=P):
            v = at(top[0], *shape, parts=parts)
            top[0] += int(np.prod(shape))
            assert top[0] <= MEM, top[0] / KB
            return v

        dist, mask = new(SEQ), new(SEQ)
        tabq, tabk = new(T, 2, MR), new(T, 2, MR)
        mats = new(3, P)
        ident, ones, tri = mats[:, 0, :], mats[:, 1, :], mats[:, 2, :]
        misc = new(320)
        c_slope, c_lam = misc[:, 0:3], misc[:, 4:8]
        c_first, c_e128, c_toov = misc[:, 16:24], misc[:, 24:56], misc[:, 56:88]
        c_j, c_eps, c_nh = misc[:, 88:103], misc[:, 103:104], misc[:, 104:116]
        c_iota, c_yrow = misc[:, 116:244], misc[:, 244:260]
        wuq = new(2, MH * MQK)
        pm_at = [RE + 4 * KB * k for k in range(5)] + [60 * KB, 56 * KB, top[0] - 2 * MH * MQK]
        Pm = [[at(pm_at[2 * k + m], SEQ) for m in range(2)] for k in range(NPM)]
        wr = new(KC, G + E)
        wab = new(2, 2, P)
        prm = new(NROW)
        lg = new(T, G + E)
        gate1, gate2 = new(T), new(T)
        ms1, rs1 = new(T), new(T)
        gd3, gm, hb, dsub, tmp1 = new(3), new(1), new(4), new(1), new(1)
        c4, lsum, lex, neglam, lcur = new(2), new(2), new(2), new(1), new(2)
        sp_ = new(6, 2)
        ss, rs = [new(12), new(12)], [new(12), new(12)]
        krs = new(T)
        mxs, sums, rat, rinv = new(2 * NPM), new(2 * NPM), new(NPM), new(4, T, 2)
        qss, qrs, xss, xrs, gy = new(6), new(6), new(2), new(2), new(6)
        oss, ors, mss, mrs = new(HEADS, T), new(DH, T), new(T), new(T)
        scratch = top[0]
        top[0] += 1920
        qraw, uw, qsq = new(MH, MQK), new(MH, 2, MR), new(MH, MQK)
        osq = at(scratch, T * 64)
        PT = [at(scratch + 512 + 512 * k, 512) for k in range(4)]
        sq = [at(scratch + 384 * k, 384) for k in range(2)]
        qn = [at(scratch + 768 + 576 * k, 576) for k in range(2)]
        th = [at(scratch + 256 * k, FE) for k in range(2)]
        hh = [at(scratch + 512 + 256 * k, FE) for k in range(2)]
        hT = [at(scratch + 1024 + 256 * k, 2, P) for k in range(2)]

        rt = [RD + 24 * KB]

        def rnew(*shape):
            v = at(rt[0], *shape)
            rt[0] += int(np.prod(shape))
            assert rt[0] <= 136 * KB
            return v

        r_gm, r_m, r_pg, r_m1, r_m2 = (rnew(T) for _ in range(5))
        r_t4, r_gs, r_ge, r_oh = (rnew(T, G) for _ in range(4))
        r_t8, r_ein, r_es, r_p, r_o1, r_o2 = (rnew(T, EPG) for _ in range(6))
        r_prod = rnew(T, G, EPG)
        r_M1, r_M2, r_M, r_pre = rnew(T, E), rnew(T, E), rnew(T, E), rnew(T + 1, E)
        r_cnt, r_ov, r_inc, r_ej = rnew(E), rnew(E), rnew(E), rnew(NOV)
        r_sl, r_le = rnew(T, E), rnew(NOV, E)
        r_row, r_blk = rnew(2, T), rnew(2, T)
        r_yrow, r_second = rnew(NBLK), rnew(NBLK)
        hot_row = at(56 * KB, 2 * T, P)
        hot_blk = at(scratch + 2048, 2 * T, NBLK)

        lay = []

        def sem(name, per_layer=True):
            s = ctx.enter_context(nc.semaphore(name))
            if per_layer:
                lay.append(s)
            return s

        s_con, s_zero, s_layer, s_tick, s_out, s_bias = (
            sem(n, False) for n in ("constants_in", "zeroed", "layer_may_start", "tick", "x_stored",
                                     "biases_in"))
        s_x = [sem(f"x_half{k}_in", False) for k in range(2)]
        g_ov, g_os = sem("ov_rows_gathered", False), sem("ov_y_scattered", False)
        g_x = [sem(f"rows_gathered{k}", False) for k in range(2)]
        g_y = [sem(f"y_scattered{k}", False) for k in range(2)]
        s_row, s_bc, s_wq, s_wr, s_wab, s_wout, s_xrs = (
            sem(n) for n in ("param_rows_in", "param_bcast_in", "latent_w_in", "router_w_in",
                             "lru_gate_w_in", "w_out_in", "x_rows_saved"))
        s_win = [sem(f"w_in{k}_in") for k in range(2)]
        s_xr = [sem(f"x_tile{k}_in") for k in range(2)]
        s_x1s = [sem(f"x1_stored{k}") for k in range(2)]
        s_h2s = [sem(f"h2_stored{k}") for k in range(2)]
        s_pad = sem("conv_pad_zeroed")
        pe_par, dv_par, dv_lam, a_lam, dv_pr = (
            sem(n) for n in ("params_turned", "params_ready", "lambda_dots", "lambda_exp", "params_derived"))
        a_ss, pl_rs, dv_xs, pe_xn, dv_xe = (
            sem(n) for n in ("x_squared", "x_rstd", "x_scaled", "x_turned", "x_evacuated"))
        pe_pj, pe_tr = sem("projected"), sem("qk_turned")
        a_sq, dv_ss, pl_qk, dv_qn = (sem(n) for n in ("qk_squared", "qk_sums", "qk_rstd", "qk_normed"))
        dv_qT, a_kT, dv_cT, a_kTm, dv_kn = (
            sem(n) for n in ("qT_out", "kT_out", "latents_out", "kTm_out", "k_latent_normed"))
        a_v, a_vm = sem("values_out"), sem("latent_values_out")
        l_u, l_conv, l_sig, l_gp, l_dec, l_exp, l_b2, l_sr, l_y, l_y2, l_ms, l_fin = (
            sem(n) for n in ("lru_in", "lru_conv", "lru_gates", "gelu_poly", "lru_decay", "lru_exp", "lru_b2",
                             "lru_root", "lru_y", "lru_y_squared", "lru_rms", "lru_done"))
        dv_ch, pl_ch = sem("vector_chain"), sem("pool_chain")
        a_wh, dv_wl, dv_yr, a_yh = (sem(n) for n in ("w_out_high", "w_out_low", "y_raw", "y_high"))
        a_qh, dv_ql = sem("qk_high"), sem("qk_low")
        s_qks = [sem(f"qk_parts{k}_stored") for k in range(2)]
        s_st = [sem(f"qk_stack{k}_in") for k in range(2)]
        pe_s, pe_t, pe_v = sem("scores"), sem("turned"), sem("pv")
        dv_pass, a_exp, dv_comb, a_pt = (sem(n) for n in ("biased", "exped", "combined", "p_out"))
        a_q, dv_qs, pl_q, dv_qu, dv_qr = (
            sem(n) for n in ("q_squared", "q_sums", "q_rstd", "q_normed", "q_rotated"))
        dv_o, a_o, dv_os, pl_o, dv_on, pe_y, dv_yT = (
            sem(n) for n in ("o_scaled", "o_squared", "o_sums", "o_rstd", "o_normed", "y_turned", "y_out"))
        pe_x1, dv_x1, a_x1, pl_x1, dv_h2, pe_h2, dv_h2T, pe_lg, a_lg = (
            sem(n) for n in ("out_projected", "x1", "x1_squared", "x1_rstd", "h2", "h2_turned", "h2_out",
                             "routed", "logits"))
        dv_r, a_r, pe_r, dv_slot, dv_idx, dv_xg0 = (
            sem(n) for n in ("route_vector", "route_exp", "route_tensor", "slots", "gather_index", "xg_zeroed"))
        s_x1l = sem("x1_reloaded")
        s_w13 = [sem(f"w13_{k}_in") for k in range(4)]
        s_w2 = [sem(f"w2_{k}_in") for k in range(4)]
        m_tx, m_xt, m_up, m_th, m_u, m_h, m_ht, m_hte, m_dn, m_y = (
            sem(n) for n in ("rows_turned", "rows_out", "up", "tanh", "silu", "hidden", "hidden_turned",
                             "hidden_out", "down", "y_evacuated"))
        s_yg = [sem(f"y_rows{k}_in") for k in range(NYG)]
        o_free, o_w, o_tx, o_xt, o_up, o_th, o_u, o_h, o_ht, o_hte, o_dn, o_y, o_st = (
            sem("ov_" + n) for n in ("free", "w_in", "rows_turned", "rows_out", "up", "tanh", "silu", "hidden",
                                     "hidden_turned", "hidden_out", "down", "y", "stored"))
        y_done, c_x, c_t = sem("all_y_stored"), sem("combined_x"), sem("combined_first")
        end_sp, end_act, end_dve, end_pe = (sem(f"{k}_layer_end") for k in ("sp", "act", "dve", "pe"))

        w_in, w_out = a["w_in"], a["w_out"]
        ew = {n: a[n].rearrange("l e d f -> (l e d) f") for n in ("exp_w1", "exp_w3", "exp_w2")}

        def new_layer(eng, l):
            eng.wait_ge(s_layer, l + 1)
            eng.sem_inc(s_tick, 1)

        block = ctx.enter_context(nc.Block())

        @block.sync
        def _(sp):
            def load_expert(e, k, s13, s2):
                for m, n in enumerate(("exp_w1", "exp_w3")):
                    src = ew[n][bass.ds(e * D, D), :].rearrange("(p k) f -> p k f", p=P)
                    sp.dma_start(w_ex[k][0][:, m, :, :], src).then_inc(s13, 16)
                src = ew["exp_w2"][bass.ds(e * FE, FE), :].rearrange("(k p) d -> p k d", p=P)
                sp.dma_start(w_ex[k][1][:, :, :], src).then_inc(s2, 16)

            def store_tile(i):
                sp.wait_ge(dv_x1, i + 1)
                sp.dma_start(x1d[tile(i), :], xr[i % 2]).then_inc(s_x1s[i % 2], 16)
                sp.wait_ge(dv_h2, i + 1)
                sp.dma_start(h2d[tile(i), :], h2[i % 2]).then_inc(s_h2s[i % 2], 16)

            for dst, name in ((mats.rearrange("p a b -> p (a b)"), "c_mats"), (misc, "c_misc")):
                sp.dma_start(dst, a[name]).then_inc(s_con, 16)
            with sp.Fori(0, DEPTH) as l:
                new_layer(sp, l)

                sp.dma_start(rows, a["rows"][bass.ds(l, 1), :, :].rearrange("o r p -> (o r) p")).then_inc(s_row, 16)
                def load_in(g):
                    c, n = GROUPS[g]
                    src = w_in[bass.ds(l, 1), :, c:c + n].rearrange("o (k p) c -> p (o k) c", p=P)
                    sp.dma_start(w_in_sb[g % 2][:, :, 0:n], src).then_inc(s_win[g % 2], 16)

                load_in(0)
                load_in(1)
                for s in s_x:
                    sp.wait_ge(s, 16 * 4)
                sp.dma_start(xrd.rearrange("(t p) d -> p t d", p=P), X[:, :, :]).then_inc(s_xrs, 16)
                with sp.If(l < 1):
                    for dst, name in ((dist, "c_dist"), (mask, "c_mask")):
                        sp.dma_start(dst, a[name]).then_inc(s_bias, 16)
                sp.dma_start(ropes.rearrange("p a b -> p (a b)"), a["c_rope"]).then_inc(s_bc, 16)
                sp.dma_start(wide, a["wide"][bass.ds(l, 1), :].to_broadcast([P, NWIDE])).then_inc(s_bc, 16)
                sp.dma_start(wab[:, :, :, :].rearrange("p m f c -> p (m f c)"),
                             a["gates"][bass.ds(l, 1), :, :].rearrange("o p c -> (o p) c")).then_inc(s_wab, 16)
                w = a["mla_w_uq"]
                sp.dma_start(wuq[:, 0, :], w[bass.ds(l, 1), 0:P, :].rearrange("o k c -> (o k) c")).then_inc(s_wq, 16)
                sp.dma_start(wuq[0:QR - P, 1, :],
                             w[bass.ds(l, 1), P:QR, :].rearrange("o k c -> (o k) c")).then_inc(s_wq, 16)
                src = a["router"][bass.ds(l, 1), :, :].rearrange("o (k p) c -> p (o k) c", p=P)
                sp.dma_start(wr[:, :, :], src).then_inc(s_wr, 16)
                def store_parts(g):
                    sp.wait_ge(dv_ql, g + 1)
                    for m, part in enumerate((qk_hi, qk_lo)):
                        dst = qkd[2 * (g // 2) + m, :, 512 * (g % 2):512 * (g % 2) + 512]
                        sp.dma_start(dst.rearrange("(c p) s -> p c s", p=P), part[g % 2]).then_inc(s_qks[g % 2], 16)

                for g in range(2, 5):
                    sp.wait_ge(pe_pj, PJ[("lru", 7) if g == 2 else (g - 2, T - 1)] + 1)
                    load_in(g)
                    if g == 3:
                        for k in range(2):
                            store_parts(k)
                sp.wait_ge(pe_pj, PJ[3, T - 1] + 1)
                sp.dma_start(wukv, a["mla_w_ukv"][bass.ds(l, 1), :, :].rearrange("o k c -> (o k) c")).then_inc(s_wq, 16)
                store_parts(2)
                store_parts(3)

                def load_stacks(p):
                    for dst, parts in ((kst[p % 2], (2, 3, 2)), (qst[p % 2], (0, 0, 1))):
                        for k, part in enumerate(parts):
                            src = qkd[part, 64 * p:64 * p + 64, :].rearrange("(m d) s -> d m s", m=2)
                            sp.dma_start(dst[DHD * k:DHD * k + DHD, :, :], src).then_inc(s_st[p % 2], 16)

                for s in s_qks:
                    sp.wait_ge(s, 64)
                sp.wait_ge(pe_pj, PJ[4, T - 1] + 1)
                load_stacks(0)
                load_stacks(1)
                for p in range(2, DH):
                    sp.wait_ge(pe_s, MAPS_BEFORE[PAIR * (p - 1)])
                    load_stacks(p)
                sp.wait_ge(pe_s, MAPS_BEFORE[PAIR * (DH - 1)])
                for k in range(KC):
                    src = w_out[bass.ds(l, 1), k * P:k * P + P, :].rearrange("o p c -> (o p) c")
                    sp.dma_start(w_out_sb[k][:, 0, :], src).then_inc(s_wout, 16)
                sp.wait_ge(pe_s, MAPS_BEFORE[NU - 1])
                sp.wait_ge(s_xrs, 16)
                for i in range(T):
                    if i >= 2:
                        sp.wait_ge(dv_h2, i - 1)
                        sp.wait_ge(s_x1s[i % 2], 16 * (i // 2))
                    sp.dma_start(xr[i % 2], xrd[tile(i), :]).then_inc(s_xr[i % 2], 16)
                    if i >= 1:
                        store_tile(i - 1)
                store_tile(T - 1)
                sp.wait_ge(a_lg, T)
                for s in s_x1s + s_h2s:
                    sp.wait_ge(s, 16 * (T // 2))
                for b in range(4):
                    load_expert(l * E + b, b, s_w13[b], s_w2[b])
                with sp.Fori(1, E // 4) as it:
                    for j in range(4):
                        sp.wait_ge(m_dn, 8 * it + (2 * j - 6))
                        load_expert(l * E + 4 * it + j, j, s_w13[j], s_w2[j])
                sp.dma_start(X[:, :, :], x1d.rearrange("(t p) d -> p t d", p=P)).then_inc(s_x1l, 16)
                sp.wait_ge(dv_slot, 2)
                n = sp.value_load(ov_i[0:1, NOV:NOV + 1], min_val=0, max_val=NOV)
                with sp.Fori(0, NOV) as j:
                    with sp.If(j < n):
                        sp.wait_ge(o_free, j + 1)
                        sp.sem_inc(s_tick, 1)
                        e = sp.value_load(ov_i[0:1, bass.ds(j, 1)], min_val=0, max_val=E - 1)
                        load_expert(l * E + e, 0, o_w, o_w)
                sp.wait_ge(y_done, 1)
                for i in range(T):
                    if i >= NYG:
                        sp.wait_ge(c_x, i - NYG + 1)
                    for k in range(2):
                        row = k * SEQ + i * P
                        sp.dma_start(yg[i % NYG][k], yd[row:row + P, :]).then_inc(s_yg[i % NYG], 16)
                with sp.If(l > DEPTH - 2):
                    for i in range(T):
                        sp.wait_ge(c_x, i + 1)
                        sp.dma_start(xrd[tile(i), :], X[:, i, :]).then_inc(s_out, 16)
                sp.drain().then_inc(end_sp, 1)
            sp.wait_ge(s_layer, DEPTH + 1)
            sp.wait_ge(s_out, 16 * T)

        @block.gpsimd
        def _(pool):
            chain = [0]

            def rstd(dst, src, n, signal):
                chain[0] += 1
                nc.gpsimd.tensor_scalar(dst, src, 1.0, EPS, ALU.mult, ALU.add).then_inc(pl_ch, 1)
                pool.wait_ge(pl_ch, chain[0])
                nc.gpsimd.tensor_tensor(dst, dst, c_nh[:, 0:n], ALU.pow).then_inc(signal, 1)

            pool.wait_ge(s_con, 32)
            pool.wait_ge(s_zero, 1)
            pool.sem_inc(s_layer, 1)
            with pool.Fori(0, DEPTH) as l:
                nc.gpsimd.memset(l_in[:, :, 0:3], 0.0).then_inc(s_pad, 1)
                for i in range(T):
                    pool.wait_ge(a_ss, i + 1)
                    rstd(rs1[:, i:i + 1], ms1[:, i:i + 1], 1, pl_rs)
                for q in range(4 * T):
                    if q < 2 * T:
                        n = 12
                        pool.wait_ge(dv_ss, q + 1)
                    elif q < 3 * T:
                        n = 2
                        pool.wait_ge(a_sq, q + 1)
                    else:
                        n = MH
                        pool.wait_ge(dv_ss, q - T + 1)
                    if 2 <= q < 3 * T + 2:
                        pool.wait_ge(dv_qn, q - 1)
                    elif q >= 3 * T + 2:
                        pool.wait_ge(dv_kn, 3 * (q - 2 - 3 * T) + 3)
                    rstd(rs[q % 2][:, 0:n], ss[q % 2][:, 0:n], n, pl_qk)
                    if q >= 3 * T:
                        pool.wait_ge(dv_qs, q - 3 * T + 1)
                        rstd(qrs, qss, MH, pl_q)
                for p in range(DH):
                    pool.wait_ge(dv_os, 2 * p + 1)
                    rstd(ors[:, p, :], oss[:, p, :], T, pl_o)
                pool.wait_ge(dv_os, 2 * DH + 1)
                rstd(mrs, mss, T, pl_o)
                for i in range(T):
                    pool.wait_ge(a_x1, i + 1)
                    rstd(xrs[:, i % 2:i % 2 + 1], xss[:, i % 2:i % 2 + 1], 1, pl_x1)
                pool.wait_ge(dv_idx, 1)
                pool.wait_ge(dv_xg0, 2)
                for s in s_h2s:
                    pool.wait_ge(s, 16 * (T // 2))

                def gather(dst, table, index, signal, bound):
                    nc.gpsimd.indirect_dma_start(dst, None, table[:, :], bass.IndirectOffsetOnAxis(ap=index, axis=0),
                                                 bounds_check=bound, oob_is_err=False).then_inc(signal, 16)

                def gather_rows(b):
                    if b >= 2:
                        pool.wait_ge(m_tx, 2 * (b - 1))
                    gather(xg[b % 2], h2d, gidx[:, b:b + 1], g_x[b % 2], SEQ - 1)

                def scatter(src, index, signal):
                    nc.gpsimd.indirect_dma_start(yd[:, :], bass.IndirectOffsetOnAxis(ap=index, axis=0), src, None,
                                                 bounds_check=2 * SEQ - 1, oob_is_err=False).then_inc(signal, 16)

                for b in range(3):
                    gather_rows(b)
                for b in range(E):
                    if b + 3 < E:
                        gather_rows(b + 3)
                    pool.wait_ge(m_y, 2 * b + 2)
                    scatter(yo[b % 2], yidx[:, b:b + 1], g_y[b % 2])
                n = pool.value_load(ov_i[0:1, NOV:NOV + 1], min_val=0, max_val=NOV)
                before = pool.value_load(ov_i[0:1, NOV + 1:NOV + 2], min_val=0, max_val=NOV * DEPTH)
                for j in range(NOV):
                    with pool.If(n > j):
                        pool.wait_ge(o_free, j + 1)
                        gather(xg[0], h2d, gidx[:, E + j:E + j + 1], g_ov, SEQ - 1)
                        pool.wait_ge(o_y, j + 1)
                        scatter(yo[0], yidx[:, E + j:E + j + 1], g_os)
                        pool.wait_ge(g_os, 16 * before + (16 * j + 16))
                        pool.sem_inc(o_st, 1)
                for s in g_y:
                    pool.wait_ge(s, l * (8 * E) + 8 * E)
                    pool.sem_inc(s_tick, 1)
                pool.sem_inc(y_done, 1)
                for s in (end_sp, end_act, end_dve, end_pe):
                    pool.wait_ge(s, 1)
                pool.sem_clear(range(lay[0].num, lay[-1].num + 1))
                pool.sem_inc(s_layer, 1)

        @block.scalar
        def _(act):
            A = nc.scalar.activation
            for i in range(T):
                act.dma_start(X[:, i, :], a["x"][0, tile(i), :]).then_inc(s_x[i // 4], 16)
            with act.Fori(0, DEPTH) as l:
                new_layer(act, l)
                for i in range(T):
                    if i % 4 == 0:
                        act.wait_ge(s_x[i // 4], 16 * 4)
                    if i >= 2:
                        act.wait_ge(a_ss, i - 1)
                    A(xsq[i % 2], X[:, i, :], ACT.Square, scale=D ** -0.5,
                      accum_out=ms1[:, i:i + 1]).then_inc(a_ss, 1)
                act.wait_ge(dv_par, 1)
                for k in range(8):
                    f, c = k // 2, k % 2
                    act.wait_ge(pe_pj, PJ["lru", k] + 1)
                    dst = l_in[:, f, 3 + 512 * c:515 + 512 * c] if f < 2 else yl[:, f - 2, 512 * c:512 * c + 512]
                    A(dst, bank(PJ["lru", k] % 4), ACT.Copy).then_inc(l_u, 1)
                act.wait_ge(s_xrs, 16)
                act.wait_ge(dv_lam, 1)
                A(lex, lsum, ACT.Exp)
                A(sp_[:, 1, :], sp_[:, 0, :], ACT.Exp, scale=-1.0).then_inc(a_lam, 1)

                def square_qk(q):
                    if q >= 2:
                        act.wait_ge(dv_ss, q - 1)
                    b = PJ[1 + q // T, q % T]
                    act.wait_ge(pe_pj, b + 1)
                    A(sq[q % 2], bank(b % 4, 0, 384), ACT.Square, scale=DHD ** -0.5).then_inc(a_sq, 1)

                def k_out(i):
                    act.wait_ge(pe_tr, T + i + 1)
                    if i % 4 == 0:
                        act.wait_ge(s_qks[i // 4], 32)
                    A(qk[i // 4][:, :, tile(i % 4)], bank(4 + i % 2, 0, 384).rearrange("p (a b) -> p a b", a=3),
                      ACT.Copy).then_inc(a_kT, 1)

                def high_part(g):
                    if g < 2:
                        act.wait_ge(dv_qT, 4 * g + 4)
                    else:
                        act.wait_ge(a_kT, 4 * g - 4)
                        act.wait_ge(s_qks[g % 2], 32)
                    A(qk_hi[g % 2].bitcast(F32R), qk[g % 2], ACT.Copy).then_inc(a_qh, 1)

                for q in range(T):
                    square_qk(q)
                    if q == 6:
                        high_part(0)
                square_qk(T)
                high_part(1)
                act.wait_ge(dv_pr, 1)
                for k in range(8):
                    m, f, c = k // 4, (k // 2) % 2, k % 2
                    b = PJ["gate", k]
                    act.wait_ge(pe_pj, b + 1)
                    dst = (l_t2, l_t3)[m][:, f, 512 * c:512 * c + 512]
                    A(dst, bank(b % 4), ACT.Tanh, bias=hb[:, 2 * m + f:2 * m + f + 1], scale=0.5).then_inc(l_sig, 1)
                for i in range(1, T):
                    square_qk(T + i)
                    k_out(i - 1)

                def v_out(i):
                    act.wait_ge(pe_pj, PJ[3, i] + 1)
                    A(Vd[:, i, :], bank(PJ[3, i] % 4, 0, 384), ACT.Copy).then_inc(a_v, 1)

                v_out(0)
                k_out(T - 1)
                high_part(2)
                high_part(3)
                act.wait_ge(l_dec, 2)
                A(l_t4[:, :, :], l_t2[:, :, :], ACT.Exp).then_inc(l_exp, 1)
                act.wait_ge(l_exp, 1)
                A(l_t2[:, :, :], l_t2[:, :, :], ACT.Tanh, scale=-1.0).then_inc(l_exp, 1)
                act.wait_ge(l_gp, 1)
                A(l_g[:, :, :], l_g[:, :, :], ACT.Tanh, scale=GELU_C).then_inc(l_exp, 1)
                v_out(1)
                v_out(2)
                act.wait_ge(l_b2, 1)
                A(l_t2[:, :, :], l_t2[:, :, :], ACT.Sqrt).then_inc(l_sr, 1)
                for i in range(3, T):
                    v_out(i)
                for i in range(T):
                    q = 2 * T + i
                    b = PJ[4, i]
                    act.wait_ge(pe_pj, b + 1)
                    act.wait_ge(pl_qk, q - 1)
                    act.wait_ge(a_sq, q - 1)
                    bb = b % 4
                    A(sq[q % 2][:, 0:QR], bank(bb, 0, QR), ACT.Square, scale=QR ** -0.5, accum_out=ss[q % 2][:, 0:1])
                    A(sq[q % 2][:, QR:QR + KVR], bank(bb, QR, QR + KVR), ACT.Square, scale=KVR ** -0.5,
                      accum_out=ss[q % 2][:, 1:2])
                    A(sq[q % 2][:, QR + KVR:QR + KVR + MR], bank(bb, QR + KVR, QR + KVR + MR), ACT.Square,
                      scale=MQK ** -0.5, accum_out=krs[:, i:i + 1])
                    A(kr[:, i, :], bank(bb, QR + KVR, QR + KVR + MR), ACT.Copy).then_inc(a_sq, 1)
                    if i == 3:
                        act.wait_ge(l_y, 1)
                        A(l_t2[:, :, :], yl[:, :, :], ACT.Square, scale=LRU ** -0.5).then_inc(l_y2, 1)
                    if i == T - 3:
                        for c in range(2):
                            b = PJ["lss", c]
                            act.wait_ge(pe_pj, b + 1)
                            A(l_t3[:, 0, 512 * c:512 * c + 512], bank(b % 4), ACT.Sqrt, bias=c_eps).then_inc(l_ms, 1)

                def heads_out(i, kind):
                    for c in (2 * kind, 2 * kind + 1):
                        act.wait_ge(pe_tr, 3 * T + 4 * i + c + 1)
                        h, nh = 4 * (c % 2), 4 - 2 * (c % 2)
                        A((kTm, qTm)[c // 2][:, h:h + nh, tile(i)],
                          bank(4 + c % 2, 0, nh * P, parts=MQK).rearrange("p (a b) -> p a b", a=nh),
                          ACT.Copy, scale=1.0 if c < 2 else gm[0:MQK, :]).then_inc(a_kTm, 1)

                for s in s_qks:
                    act.wait_ge(s, 64)
                for i in range(T):
                    q = 3 * T + i
                    if i < 2:
                        act.wait_ge(a_sq, q - 1)
                        act.wait_ge(l_fin, 2)
                    else:
                        act.wait_ge(dv_ss, 2 * T + i - 1)
                    for c in range(2):
                        b = PJ["kv", 2 * i + c]
                        act.wait_ge(pe_pj, b + 1)
                        kv = bank(head_bank("kv", 2 * i + c), 0, 384).rearrange("p (h w) -> p h w", h=3)
                        A(Vm[:, i, 3 * c:3 * c + 3, :], kv[:, :, MN:MN + MV], ACT.Copy).then_inc(a_vm, 1)
                        ins = A(sq[q % 2][:, 192 * c:192 * c + 192].rearrange("p (h w) -> p h w", h=3), kv[:, :, 0:MN],
                                ACT.Square, scale=MQK ** -0.5)
                    ins.then_inc(a_sq, 1)
                    if i >= 1:
                        heads_out(i - 1, 0)
                        act.wait_ge(dv_qs, i)
                    for c, (lo, hi) in enumerate(((0, 4), (4, 6))):
                        act.wait_ge(pe_pj, PJ["qu", 2 * i + c] + 1)
                        ins = A(qsq[:, lo:hi, :], bank(head_bank("qu", 2 * i + c), 0, (hi - lo) * MQK).rearrange("p (h w) -> p h w", w=MQK),
                                ACT.Square, scale=MQK ** -0.5)
                    ins.then_inc(a_q, 1)
                    if i >= 1:
                        heads_out(i - 1, 1)
                heads_out(T - 1, 0)
                heads_out(T - 1, 1)

                def exp_maps(u):
                    kind, n, i = UNITS[u]
                    for m in range(maps_of(u)):
                        k = 2 * (u % NPM) + m
                        act.wait_ge(dv_pass, MAPS_BEFORE[u] + m + 1)
                        v = Pm[u % NPM][m][:, 0:(i + 1) * P]
                        A(v, v, ACT.Exp, bias=mxs[:, k:k + 1], scale=-1.0,
                          accum_out=sums[:, k:k + 1]).then_inc(a_exp, 1)

                def p_out(u):
                    for c, (lo, hi) in enumerate(chunks_of(u)):
                        r = CHUNKS_BEFORE[u] + c
                        act.wait_ge(pe_t, r + 1)
                        if r >= 4:
                            act.wait_ge(pe_v, r - 3)
                        n = (hi - lo) * P
                        A(PT[r % 4][:, 0:n], bank(4 + r % 2, 0, n), ACT.Copy).then_inc(a_pt, 1)

                def square_o(h):
                    act.wait_ge(dv_o, h + 1)
                    if h >= 1:
                        act.wait_ge(dv_os, h)
                    o = 64 * (h // 2 + DH * (h % 2))
                    n = MH * MV if h % 2 else DVD
                    A(osq.rearrange("p (t d) -> p t d", t=T), O[:, :, o:o + 64], ACT.Square,
                      scale=n ** -0.5).then_inc(a_o, 1)

                for u in range(AHEAD):
                    exp_maps(u)
                for u in range(NU):
                    if u + AHEAD < NU:
                        exp_maps(u + AHEAD)
                    p_out(u)
                    j = u - PAIR * (DH - 1) - 7
                    if 0 <= j < KC:
                        if j == 0:
                            act.wait_ge(s_wout, 16 * KC)
                        if WO_HI[j] in (52, 84):
                            act.wait_ge(pe_s, MAPS_BEFORE[NU])
                        A(wo_hi[j].bitcast(F32R), w_out_sb[j], ACT.Copy).then_inc(a_wh, 1)
                    if u % PAIR in (3, 5) and u >= PAIR:
                        square_o(2 * (u // PAIR) - 2 + (u % PAIR == 5))
                act.wait_ge(pe_v, CHUNKS_BEFORE[NU])
                square_o(2 * DH - 2)
                square_o(2 * DH - 1)
                A(yl_hi.bitcast(F32R), yl[:, :, :], ACT.Copy).then_inc(a_wh, 1)

                def logits_out(i):
                    act.wait_ge(pe_lg, i + 1)
                    A(lg[:, i, :], bank(6 + i % 2, 0, G + E), ACT.Copy).then_inc(a_lg, 1)

                def y_high(i):
                    act.wait_ge(dv_yr, 2 * i + 2)
                    if i >= 2:
                        act.wait_ge(pe_x1, i - 1)
                    A(yT_hi[i % 2].bitcast(F32R), yT[i % 2], ACT.Copy).then_inc(a_yh, 1)

                y_high(0)
                for i in range(T):
                    if i + 1 < T:
                        y_high(i + 1)
                    act.wait_ge(dv_x1, i + 1)
                    if i >= 1:
                        act.wait_ge(a_x1, i)
                    if i >= 2:
                        act.wait_ge(pl_x1, i - 1)
                    A(xsq2, xr[i % 2], ACT.Square, scale=D ** -0.5, accum_out=xss[:, i % 2:i % 2 + 1]).then_inc(a_x1, 1)
                    if i >= 1:
                        logits_out(i - 1)
                logits_out(T - 1)

                act.wait_ge(dv_r, 1)
                A(r_ge, r_gs, ACT.Exp)
                A(r_p, r_es, ACT.Exp).then_inc(a_r, 1)

                def tanh_a1(b4, b):
                    k = b % 2
                    act.wait_ge(m_up, 4 * b4 + b + 1)
                    if not (isinstance(b4, int) and 4 * b4 + b < 2):
                        act.wait_ge(m_u, 4 * b4 + b - 1)
                    A(th[k], bank(2 + k, 0, FE), ACT.Tanh, scale=0.5).then_inc(m_th, 1)

                def finish(b4, b):
                    k = b % 2
                    early = isinstance(b4, int) and 4 * b4 + b < 2
                    act.wait_ge(m_ht, 4 * b4 + b + 1)
                    if not early:
                        act.wait_ge(m_dn, 8 * b4 + 2 * b - 2)
                    A(hT[k], bank(4, 0, 256).rearrange("p (a b) -> p a b", a=2), ACT.Copy).then_inc(m_hte, 1)
                    if not early:
                        act.wait_ge(g_y[k], l * (8 * E) + (32 * b4 + 16 * (b // 2)))
                        act.sem_inc(s_tick, 1)
                    for c in range(2):
                        act.wait_ge(m_dn, 8 * b4 + 2 * b + c + 1)
                        A(yo[k][:, 512 * c:512 * c + 512], bank(5 + c), ACT.Copy).then_inc(m_y, 1)

                tanh_a1(0, 0)
                for b in range(4):
                    tanh_a1(0, b + 1)
                    finish(0, b)
                with act.Fori(1, E // 4 - 1) as it:
                    for b in range(4):
                        tanh_a1(it, b + 1)
                        finish(it, b)
                for b in range(4):
                    if b < 3:
                        tanh_a1(E // 4 - 1, b + 1)
                    finish(E // 4 - 1, b)
                for s in g_y:
                    act.wait_ge(s, l * (8 * E) + 8 * E)
                    act.sem_inc(s_tick, 1)
                act.wait_ge(dv_slot, 2)
                n = act.value_load(ov_i[0:1, NOV:NOV + 1], min_val=0, max_val=NOV)
                with act.Fori(0, NOV) as j:
                    with act.If(j < n):
                        act.wait_ge(o_up, j + 1)
                        A(th[0], bank(2, 0, FE), ACT.Tanh, scale=0.5).then_inc(o_th, 1)
                        act.wait_ge(o_ht, j + 1)
                        A(hT[0], bank(4, 0, 256).rearrange("p (a b) -> p a b", a=2), ACT.Copy).then_inc(o_hte, 1)
                        act.wait_ge(o_dn, j + 1)
                        A(yo[0], PS[:, 5 * 512:7 * 512], ACT.Copy).then_inc(o_y, 1)
                        act.wait_ge(o_st, j + 1)
                        act.sem_inc(s_tick, 1)
                act.drain().then_inc(end_act, 1)

        @block.vector
        def _(dve):
            V = nc.vector
            chain = [0]

            def link(ins):
                chain[0] += 1
                ins.then_inc(dv_ch, 1)
                dve.wait_ge(dv_ch, chain[0])

            V.memset(ov_tot[:, :], 0.0).then_inc(s_zero, 1)
            with dve.Fori(0, DEPTH) as l:
                new_layer(dve, l)
                dve.wait_ge(pe_par, 1)
                V.tensor_copy(prm, bank(7, 0, NROW)).then_inc(dv_par, 1)
                dve.wait_ge(dv_par, 1)

                def xn_out(i):
                    for c in range(2):
                        r = 2 * i + c
                        dve.wait_ge(pe_xn, r + 1)
                        V.tensor_tensor(xnT[:, 4 * c:4 * c + 4, tile(i)],
                                        bank(4 + c).rearrange("p (a b) -> p a b", a=4),
                                        spread(prm[:, R_G1 + 4 * c:R_G1 + 4 * c + 4], 2, [P, 4, P]),
                                        ALU.mult).then_inc(dv_xe, 1)

                for i in range(T):
                    dve.wait_ge(pl_rs, i + 1)
                    if i >= 2:
                        dve.wait_ge(pe_xn, 2 * (i - 1))
                    V.tensor_scalar(xs[i % 2], X[:, i, :], rs1[:, i:i + 1], None, ALU.mult).then_inc(dv_xs, 1)
                    if i >= 1:
                        xn_out(i - 1)
                xn_out(T - 1)

                dve.wait_ge(s_bc, 32)
                link(V.tensor_tensor(tmp1, prm[:, R_DQ:R_DQ + 1], prm[:, R_DK:R_DK + 1], ALU.mult))
                V.tensor_scalar(gd3, c_slope, tmp1, None, ALU.mult)
                V.tensor_scalar(hb, prm[:, R_BA:R_BA + 4], 0.5, None, ALU.mult)
                V.tensor_copy(lcur, c_lam[:, bass.ds(2 * l, 2)])
                V.scalar_tensor_tensor(sp_[:, 0, :], prm[:, R_LAM:R_LAM + 2], -1.0, prm[:, R_LAM:R_LAM + 2], ALU.mult, ALU.max)
                link(V.tensor_tensor(gm[0:MQK, :], prm[0:MQK, R_MQ:R_MQ + 1], prm[0:MQK, R_MK:R_MK + 1], ALU.mult))
                V.tensor_scalar(gm[0:MN, :], gm[0:MN, :], MSCALE, None, ALU.mult)
                V.memset(gm[MN:MQK, :], MSCALE)
                V.tensor_scalar(dsub, prm[:, R_SUB:R_SUB + 1], lcur[:, 0:1], None, ALU.mult).then_inc(dv_pr, 1)
                V.tensor_tensor_reduce(uw[:, 0, 0, :], lqk[:, 0, :], lqk[:, 1, :], 1.0, 0.0, ALU.mult, ALU.add,
                                       lsum[:, 0:1])
                V.tensor_tensor_reduce(uw[:, 1, 0, :], lqk[:, 2, :], lqk[:, 3, :], 1.0, 0.0, ALU.mult, ALU.add,
                                       lsum[:, 1:2]).then_inc(dv_lam, 1)
                V.tensor_tensor(tabq[:, :, :, :].rearrange("p t a b -> p t (a b)"), ropes[:, :, :],
                                spread(gr[:, 0, :], 1, [P, T, 64]), ALU.mult)
                link(V.tensor_tensor(tabk[:, :, :, :].rearrange("p t a b -> p t (a b)"), ropes[:, :, :],
                                     spread(gr[:, 1, :], 1, [P, T, 64]), ALU.mult))
                dve.wait_ge(a_lam, 1)
                link(V.tensor_tensor(neglam, lex[:, 1:2], lex[:, 0:1], ALU.subtract))
                link(V.tensor_tensor(neglam, neglam, lcur[:, 1:2], ALU.subtract))
                z, s1, s2, po, mx0 = (sp_[:, k, :] for k in range(1, 6))
                link(V.tensor_scalar(s1, z, 2.0, None, ALU.add))
                link(V.reciprocal(s1, s1))
                link(V.tensor_tensor(s1, s1, z, ALU.mult))
                link(V.tensor_tensor(s2, s1, s1, ALU.mult))
                link(V.tensor_scalar(po, s2, 1.0 / 17, None, ALU.mult))
                for k in (15, 13, 11, 9, 7, 5, 3):
                    link(V.scalar_tensor_tensor(po, po, 1.0 / k, s2, ALU.add, ALU.mult))
                link(V.scalar_tensor_tensor(po, po, 1.0, s1, ALU.add, ALU.mult))
                link(V.tensor_scalar(mx0, prm[:, R_LAM:R_LAM + 2], -1.0, 0.0, ALU.mult, ALU.max))
                link(V.scalar_tensor_tensor(po, po, 2.0, mx0, ALU.mult, ALU.add))
                link(V.tensor_scalar(c4, po, -RG_C / 2, None, ALU.mult))

                def conv(k):
                    f, j = k // 4, k % 4
                    w = prm[:, R_CW + 2 * j + f:R_CW + 2 * j + f + 1]
                    if k == 0:
                        dve.wait_ge(l_u, 8)
                        dve.wait_ge(s_pad, 1)
                    else:
                        dve.wait_ge(l_conv, k)
                    win = l_in[:, f, j:j + SEQ]
                    if j == 0:
                        V.tensor_scalar(l_xc[:, f, :], win, w, prm[:, R_CB + f:R_CB + f + 1], ALU.mult,
                                        ALU.add).then_inc(l_conv, 1)
                    else:
                        V.scalar_tensor_tensor(l_xc[:, f, :], win, w, l_xc[:, f, :], ALU.mult,
                                               ALU.add).then_inc(l_conv, 1)

                def gelu_poly(k):
                    if k == 0:
                        dve.wait_ge(l_conv, 8)
                        link(V.tensor_tensor(l_g[:, :, :], yl[:, :, :], yl[:, :, :], ALU.mult))
                    elif k == 1:
                        link(V.tensor_scalar(l_g[:, :, :], l_g[:, :, :], 0.044715, 1.0, ALU.mult, ALU.add))
                    else:
                        V.tensor_tensor(l_g[:, :, :], l_g[:, :, :], yl[:, :, :], ALU.mult).then_inc(l_gp, 1)

                def decay():
                    dve.wait_ge(l_sig, 8)
                    for f in range(2):
                        V.tensor_scalar(l_t2[:, f, :], l_t2[:, f, :], 1.0, c4[:, f:f + 1], ALU.add,
                                        ALU.mult).then_inc(l_dec, 1)

                def low_part(g):
                    dve.wait_ge(a_qh, g + 1)
                    V.tensor_tensor(qk_lo[g % 2].bitcast(F32R), qk[g % 2], qk_hi[g % 2],
                                    ALU.subtract).then_inc(dv_ql, 1)

                def q_out(i):
                    dve.wait_ge(pe_tr, i + 1)
                    V.tensor_tensor(qk[i // 4][:, :, tile(i % 4)], bank(4 + i % 2, 0, 384).rearrange("p (a b) -> p a b", a=3),
                                    spread(gd3, 2, [P, 3, P]), ALU.mult).then_inc(dv_qT, 1)

                dve.wait_ge(s_xrs, 16)
                for q in range(2 * T):
                    b = PJ[1 + q // T, q % T]
                    dve.wait_ge(a_sq, q + 1)
                    if q >= 2:
                        dve.wait_ge(pl_qk, q - 1)
                    V.tensor_reduce(ss[q % 2], sq[q % 2].rearrange("p (m d) -> p m d", d=DHD), AX.X,
                                    ALU.add).then_inc(dv_ss, 1)
                    if q < T:
                        conv(q)
                    elif q in (T + 1, T + 2, T + 3):
                        gelu_poly(q - T - 1)
                    elif q == T + 5:
                        decay()
                    dve.wait_ge(pl_qk, q + 1)
                    if q >= 2:
                        dve.wait_ge(pe_tr, q - 1)
                    V.tensor_tensor(qn[q % 2][:, 0:384].rearrange("p (m d) -> p m d", d=DHD),
                                    bank(b % 4, 0, 384).rearrange("p (m d) -> p m d", d=DHD),
                                    spread(rs[q % 2], 2, [P, 12, DHD]), ALU.mult).then_inc(dv_qn, 1)
                    if 1 <= q <= T:
                        q_out(q - 1)

                    if T - 1 <= q <= T:
                        low_part(q - T + 1)
                dve.wait_ge(l_exp, 2)
                link(V.tensor_tensor(l_t5[:, :, :], l_t4[:, :, :], l_t4[:, :, :], ALU.mult))
                V.scalar_tensor_tensor(l_t2[:, :, :], l_t5[:, :, :], 1.0, l_t2[:, :, :], ALU.add,
                                       ALU.mult).then_inc(l_b2, 1)
                link(V.scalar_tensor_tensor(l_t3[:, :, :], l_t3[:, :, :], 1.0, l_xc[:, :, :], ALU.add, ALU.mult))
                dve.wait_ge(l_sr, 1)
                link(V.scalar_tensor_tensor(l_t3[:, :, :], l_t3[:, :, :], 0.5, l_t2[:, :, :], ALU.mult, ALU.mult))
                for f in range(2):
                    link(V.tensor_tensor_scan(l_xc[:, f, :], l_t4[:, f, :], l_t3[:, f, :], 0.0, ALU.mult, ALU.add))
                dve.wait_ge(l_exp, 3)
                link(V.scalar_tensor_tensor(l_g[:, :, :], l_g[:, :, :], 1.0, yl[:, :, :], ALU.add, ALU.mult))
                V.scalar_tensor_tensor(yl[:, :, :], l_g[:, :, :], 0.5, l_xc[:, :, :], ALU.mult,
                                       ALU.mult).then_inc(l_y, 1)

                low_part(2)
                low_part(3)

                def latents_out(i):
                    r = 2 * T + i
                    dve.wait_ge(pe_tr, r + 1)
                    b = 4 + r % 2
                    V.tensor_scalar(cqT[:, 0, tile(i)], bank(b, 0, P), prm[:, R_CQ:R_CQ + 1], None, ALU.mult)
                    V.tensor_scalar(cqT[0:64, 1, tile(i)], bank(b, P, 2 * P, parts=64), prm[0:64, R_CQ + 1:R_CQ + 2],
                                    None, ALU.mult)
                    V.tensor_scalar(ckvT[:, tile(i)], bank(b, 2 * P, 3 * P), prm[:, R_CKV:R_CKV + 1], None,
                                    ALU.mult).then_inc(dv_cT, 1)

                for i in range(T):
                    q = 2 * T + i
                    b = PJ[4, i] % 4
                    dve.wait_ge(a_sq, q + 1)
                    dve.wait_ge(pl_qk, q + 1)
                    dve.wait_ge(pe_tr, q - 1)
                    V.tensor_scalar(qn[q % 2][:, 0:QR], bank(b, 0, QR), rs[q % 2][:, 0:1], None, ALU.mult)
                    V.tensor_scalar(qn[q % 2][:, QR:QR + KVR], bank(b, QR, QR + KVR), rs[q % 2][:, 1:2], None,
                                    ALU.mult).then_inc(dv_qn, 1)
                    if i >= 1:
                        latents_out(i - 1)
                    if i == T - 3:
                        dve.wait_ge(l_ms, 2)
                        link(V.reciprocal(l_t3[:, 0, :], l_t3[:, 0, :]))
                        for f in range(2):
                            V.scalar_tensor_tensor(yl[:, f, :], yl[:, f, :], prm[:, R_LOUT + f:R_LOUT + f + 1],
                                                   l_t3[:, 0, :], ALU.mult, ALU.mult).then_inc(l_fin, 1)
                latents_out(T - 1)
                kx = qn[0][:, 0:512].rearrange("p (t a b) -> p t a b", t=T, a=2)
                link(V.tensor_tensor(kx, spread(kr, 2, [P, T, 2, MR]), tabk, ALU.mult))
                V.tensor_tensor(kr[:, :, 0:16], kx[:, :, 0, 0:16], kx[:, :, 0, 16:32], ALU.subtract)
                link(V.tensor_tensor(kr[:, :, 16:32], kx[:, :, 1, 0:16], kx[:, :, 1, 16:32], ALU.add))

                for k in range(3):
                    V.tensor_copy(gy[:, k:k + 1], dsub)
                link(V.tensor_copy(gy[:, 3:6], prm[:, R_MOUT:R_MOUT + 3]))

                def queries(i):
                    dve.wait_ge(pl_q, i + 1)
                    if i >= 1:
                        dve.wait_ge(pe_tr, 3 * T + 4 * i)
                    for c, (lo, hi) in enumerate(((0, 4), (4, 6))):
                        b = head_bank("qu", 2 * i + c)
                        V.tensor_tensor(qraw[:, lo:hi, :], bank(b, 0, (hi - lo) * MQK).rearrange("p (h w) -> p h w", w=MQK),
                                        spread(qrs[:, lo:hi], 2, [P, hi - lo, MQK]), ALU.mult).then_inc(dv_qu, 1)
                    dve.wait_ge(dv_qu, 2 * i + 2)
                    link(V.tensor_tensor(uw[:, :, :, :], spread(qraw[:, :, MN:MQK], 2, [P, MH, 2, MR]),
                                         spread(tabq[:, i, :, :], 1, [P, MH, 2, MR]), ALU.mult))
                    V.tensor_tensor(qraw[:, :, MN:MN + 16], uw[:, :, 0, 0:16], uw[:, :, 0, 16:32], ALU.subtract)
                    V.tensor_tensor(qraw[:, :, MN + 16:MQK], uw[:, :, 1, 0:16], uw[:, :, 1, 16:32],
                                    ALU.add).then_inc(dv_qr, 1)

                for i in range(T):
                    q = 3 * T + i
                    dve.wait_ge(a_sq, q + 1)
                    dve.wait_ge(pl_qk, q - 1)
                    link(V.tensor_reduce(ss[q % 2][:, 0:MH], sq[q % 2].rearrange("p (h d) -> p h d", d=MN), AX.X,
                                         ALU.add))
                    V.tensor_scalar(ss[q % 2][:, 0:MH], ss[q % 2][:, 0:MH], krs[:, i:i + 1], None,
                                    ALU.add).then_inc(dv_ss, 1)
                    if i >= 1:
                        queries(i - 1)
                    dve.wait_ge(pl_qk, q + 1)
                    dve.wait_ge(pe_tr, 3 * T + (4 * i - 6 if i >= 2 else 0))
                    kn = qn[q % 2].rearrange("p (h d) -> p h d", h=MH)
                    for c in range(2):
                        b = head_bank("kv", 2 * i + c)
                        V.tensor_tensor(kn[:, 3 * c:3 * c + 3, 0:MN],
                                        bank(b, 0, 384).rearrange("p (h w) -> p h w", h=3)[:, :, 0:MN],
                                        spread(rs[q % 2][:, 3 * c:3 * c + 3], 2, [P, 3, MN]),
                                        ALU.mult).then_inc(dv_kn, 1)
                    V.tensor_tensor(kn[:, :, MN:MQK], spread(kr[:, i, :], 1, [P, MH, MR]),
                                    spread(rs[q % 2][:, 0:MH], 2, [P, MH, MR]), ALU.mult).then_inc(dv_kn, 1)
                    dve.wait_ge(a_q, i + 1)
                    V.tensor_reduce(qss, qsq[:, :, :], AX.X, ALU.add).then_inc(dv_qs, 1)
                queries(T - 1)

                def bias_maps(u):
                    kind, n, i = UNITS[u]
                    nk = (i + 1) * P
                    for m in range(maps_of(u)):
                        k = 2 * (u % NPM) + m
                        s = MAPS_BEFORE[u] + m
                        dve.wait_ge(pe_s, s + 1)
                        if u >= NPM:
                            dve.wait_ge(pe_t, CHUNKS_BEFORE[u - AHEAD])
                        V.tensor_tensor_reduce(Pm[u % NPM][m][:, 0:nk], PS[:, (s % 2) * 1024:(s % 2) * 1024 + nk],
                                               (mask if kind else dist)[:, SEQ - nk:SEQ],
                                               -1.0 if kind else -SLOPE[n], 3.0e38, ALU.add,
                                               ALU.min, mxs[:, k:k + 1]).then_inc(dv_pass, 1)

                def combine(u):
                    kind, p, i = UNITS[u]
                    k = 2 * (u % NPM)
                    dve.wait_ge(a_exp, MAPS_BEFORE[u + 1])
                    ri = rinv[:, 2 * kind + p % 2, i, :]
                    if kind:
                        V.reciprocal(ri[:, 0:1], sums[:, k:k + 1])
                        return
                    link(V.reciprocal(ri, sums[:, k:k + 2]))
                    ratio = rat[:, u % NPM:u % NPM + 1]
                    link(V.scalar_tensor_tensor(ratio, sums[:, k:k + 1], neglam, ri[:, 1:2], ALU.mult, ALU.mult))
                    nk = (i + 1) * P
                    P1, P2 = Pm[u % NPM]
                    V.scalar_tensor_tensor(P1[:, 0:nk], P2[:, 0:nk], ratio, P1[:, 0:nk], ALU.mult,
                                           ALU.add).then_inc(dv_comb, 1)

                def o_out(h):
                    p, kind = h // 2, h % 2
                    dve.wait_ge(pe_v, CHUNKS_BEFORE[PAIR * (p + 1) - 1 + kind])
                    o = 64 * (p + DH * kind)
                    chain[0] += 1
                    V.memset(tmp1, 0.0).then_inc(dv_ch, 1)
                    dve.wait_ge(dv_ch, chain[0])
                    V.tensor_tensor(O[:, :, o:o + 64], bank(6 + kind).rearrange("p (t d) -> p t d", t=T),
                                    spread(rinv[:, 2 * kind + p % 2, :, 0], 2, [P, T, 64]), ALU.mult).then_inc(dv_o, 1)

                def sum_o(h):
                    dve.wait_ge(a_o, h + 1)
                    V.tensor_reduce(oss[:, h // 2 + DH * (h % 2), :], osq.rearrange("p (t d) -> p t d", t=T), AX.X,
                                    ALU.add).then_inc(dv_os, 1)

                def scale_o(p):
                    dve.wait_ge(pl_o, p + 1)
                    V.tensor_tensor(O[:, :, 64 * p:64 * p + 64], O[:, :, 64 * p:64 * p + 64],
                                    spread(ors[:, p, :], 2, [P, T, 64]), ALU.mult).then_inc(dv_on, 1)

                dve.wait_ge(s_bias, 32)
                for u in range(AHEAD):
                    bias_maps(u)
                combine(0)
                for u in range(NU):
                    p, r = u // PAIR, u % PAIR
                    if p >= 1 and r in (1, 2):
                        o_out(2 * p - 3 + r)
                    if u + AHEAD < NU:
                        bias_maps(u + AHEAD)
                    if u + 1 < NU:
                        combine(u + 1)
                    if p >= 1 and r in (4, 6):
                        sum_o(2 * p - 2 + (r == 6))
                    if p >= 1 and r == 8:
                        scale_o(p - 1)
                    j = u - PAIR * (DH - 1) - 8
                    if 0 <= j < KC:
                        dve.wait_ge(a_wh, j + 1)
                        V.tensor_tensor(wo_lo[j].bitcast(F32R), w_out_sb[j], wo_hi[j], ALU.subtract).then_inc(dv_wl, 1)
                o_out(2 * DH - 2)
                o_out(2 * DH - 1)
                sum_o(2 * DH - 2)
                sum_o(2 * DH - 1)
                dve.wait_ge(dv_os, 2 * DH)
                V.tensor_reduce(mss, oss[:, DH:HEADS, :].rearrange("p h t -> p t h"), AX.X, ALU.add).then_inc(dv_os, 1)
                scale_o(DH - 1)
                dve.wait_ge(a_wh, KC + 1)
                V.tensor_tensor(yl_lo.bitcast(F32R), yl[:, :, :], yl_hi, ALU.subtract).then_inc(dv_wl, 1)

                def scale_y(i):
                    if i == 0:
                        dve.wait_ge(pl_o, DH + 1)
                    V.tensor_scalar(O[:, i, 384:768], O[:, i, 384:768], mrs[:, i:i + 1], None,
                                    ALU.mult).then_inc(dv_on, 1)

                def y_out(i):
                    for c, (lo, hi) in enumerate(((0, 4), (4, 6))):
                        dve.wait_ge(pe_y, 2 * i + c + 1)
                        if i >= 2:
                            dve.wait_ge(pe_x1, i - 1)
                        V.tensor_tensor(yT[i % 2][:, lo:hi, :], bank(4 + c, 0, (hi - lo) * P).rearrange(
                            "p (a b) -> p a b", b=P), spread(gy[:, lo:hi], 2, [P, hi - lo, P]), ALU.mult).then_inc(dv_yr, 1)

                def y_low(i):
                    dve.wait_ge(a_yh, i + 1)
                    V.tensor_tensor(yT_lo[i % 2].bitcast(F32R), yT[i % 2], yT_hi[i % 2],
                                    ALU.subtract).then_inc(dv_yT, 1)

                def h2_out(i):
                    for c in range(2):
                        dve.wait_ge(pe_h2, 2 * i + c + 1)
                        if i >= 2:
                            dve.wait_ge(pe_lg, i - 1)
                        V.tensor_tensor(h2T[i % 2][:, 4 * c:4 * c + 4, :], bank(4 + c).rearrange("p (a b) -> p a b", a=4),
                                        spread(prm[:, R_G2 + 4 * c:R_G2 + 4 * c + 4], 2, [P, 4, P]),
                                        ALU.mult).then_inc(dv_h2T, 1)

                scale_y(0)
                scale_y(1)
                y_out(0)
                y_low(0)
                for i in range(T):
                    if i + 2 < T:
                        scale_y(i + 2)
                    if i + 1 < T:
                        y_out(i + 1)
                    if i >= 1:
                        h2_out(i - 1)
                    if i + 1 < T:
                        y_low(i + 1)
                    dve.wait_ge(pe_x1, i + 1)
                    dve.wait_ge(s_xr[i % 2], 16 * (i // 2 + 1))
                    o = (i % 2) * 1024
                    V.tensor_tensor(xr[i % 2], PS[:, o:o + 1024], xr[i % 2], ALU.add).then_inc(dv_x1, 1)
                    dve.wait_ge(pl_x1, i + 1)
                    if i >= 2:
                        dve.wait_ge(s_h2s[i % 2], 16 * (i // 2))
                        dve.wait_ge(pe_h2, 2 * i - 2)
                    V.tensor_scalar(h2[i % 2], xr[i % 2], xrs[:, i % 2:i % 2 + 1], None, ALU.mult).then_inc(dv_h2, 1)
                h2_out(T - 1)

                dve.wait_ge(a_lg, T)
                for k in range(2):
                    V.memset(xg[k], 0.0).then_inc(dv_xg0, 1)

                def first_max(dst, x, mx, tmp, n):
                    link(V.tensor_reduce(mx, x, AX.X, ALU.max))
                    link(V.tensor_tensor(tmp, x, spread(mx, 2, [P, T, n]), ALU.is_equal))
                    link(V.tensor_tensor(tmp, tmp, spread(c_first[:, 0:n], 1, [P, T, n]), ALU.mult))
                    link(V.tensor_reduce(r_m, tmp, AX.X, ALU.max))
                    link(V.tensor_tensor(dst, tmp, spread(r_m, 2, [P, T, n]), ALU.is_equal))

                link(V.tensor_tensor(lg[:, :, :], lg[:, :, :], spread(rbias, 1, [P, T, G + E]), ALU.add))
                gl = lg[:, :, 0:G]
                first_max(r_oh, gl, r_gm, r_t4, G)
                V.tensor_tensor(r_gs, gl, spread(r_gm, 2, [P, T, G]), ALU.subtract)
                link(V.tensor_tensor(r_prod, lg[:, :, G:G + E].rearrange("p t (g e) -> p t g e", g=G),
                                     spread(r_oh, 3, [P, T, G, EPG]), ALU.mult))
                link(V.tensor_reduce(r_ein, r_prod.rearrange("p t g e -> p t e g"), AX.X, ALU.add))
                link(V.tensor_reduce(r_m, r_ein, AX.X, ALU.max))
                V.tensor_tensor(r_es, r_ein, spread(r_m, 2, [P, T, EPG]), ALU.subtract).then_inc(dv_r, 1)
                dve.wait_ge(a_r, 1)
                V.tensor_reduce(r_pg, r_ge, AX.X, ALU.add)
                link(V.tensor_reduce(r_m, r_p, AX.X, ALU.add))
                V.reciprocal(r_pg, r_pg)
                link(V.reciprocal(r_m, r_m))
                link(V.tensor_tensor(r_p, r_p, spread(r_m, 2, [P, T, EPG]), ALU.mult))
                first_max(r_o1, r_p, r_m1, r_t8, EPG)
                link(V.scalar_tensor_tensor(r_p, r_o1, -2.0, r_p, ALU.mult, ALU.add))
                first_max(r_o2, r_p, r_m2, r_t8, EPG)
                link(V.tensor_tensor(r_m, r_m1, r_m2, ALU.add))
                link(V.reciprocal(r_m, r_m))
                link(V.tensor_tensor(r_m, r_m, r_pg, ALU.mult))
                V.tensor_tensor(gate1, r_m1, r_m, ALU.mult)
                V.tensor_tensor(gate2, r_m2, r_m, ALU.mult)
                for mk, o in ((r_M1, r_o1), (r_M2, r_o2)):
                    V.tensor_tensor(mk.rearrange("p t (g e) -> p t g e", g=G), spread(r_oh, 3, [P, T, G, EPG]),
                                    spread(o, 2, [P, T, G, EPG]), ALU.mult)
                link(V.memset(r_pre[:, 0, :], 0.0))
                link(V.tensor_tensor(r_M, r_M1, r_M2, ALU.add))
                for k in range(T):
                    link(V.tensor_tensor(r_pre[:, k + 1, :], r_pre[:, k, :], r_M[:, k, :], ALU.add))
                V.tensor_copy(r_cnt, r_pre[:, T, :]).then_inc(dv_r, 1)
                dve.wait_ge(pe_r, 1)
                rank = bank(7, 0, T * E).rearrange("p (t e) -> p t e", t=T)
                link(V.tensor_copy(r_cnt, bank(7, T * E, T * E + E)))
                link(V.tensor_scalar(r_ov, r_cnt, float(P), None, ALU.is_gt))
                for k in range(2, SEQ // P):
                    link(V.scalar_tensor_tensor(r_ov, r_cnt, float(k * P), r_ov, ALU.is_gt, ALU.add))
                link(V.tensor_tensor_scan(r_inc, ones[:, 0:E], r_ov, 0.0, ALU.mult, ALU.add))
                link(V.tensor_tensor(r_ov, r_inc, r_ov, ALU.subtract))
                link(V.scalar_tensor_tensor(r_ov, r_ov, float(P), c_toov, ALU.mult, ALU.add))
                link(V.scalar_tensor_tensor(r_sl, rank, float(P), spread(r_ov, 1, [P, T, E]), ALU.is_ge, ALU.mult))
                link(V.tensor_tensor(r_sl, rank, r_sl, ALU.add))
                link(V.tensor_tensor(r_sl, r_sl, spread(c_e128, 1, [P, T, E]), ALU.add))
                for mk in (r_M1, r_M2):
                    link(V.tensor_tensor(mk, mk, r_sl, ALU.mult))
                for k, mk in enumerate((r_M1, r_M2)):
                    link(V.tensor_reduce(r_blk[:, k, :], mk, AX.X, ALU.add))
                blk, row = (v.rearrange("p k t -> p (k t)") for v in (r_blk, r_row))
                link(V.tensor_copy(slot_i[:, :], blk))
                link(V.tensor_scalar(row_i[:, :], slot_i[:, :], P - 1, None, ALU.bitwise_and))
                link(V.tensor_copy(row, row_i[:, :]))
                link(V.tensor_tensor(blk, blk, row, ALU.subtract))
                link(V.tensor_scalar(blk, blk, 1.0 / P, None, ALU.mult))
                link(V.tensor_tensor(hot_blk, spread(c_iota[:, 0:NBLK], 1, [P, 2 * T, NBLK]),
                                     spread(blk, 2, [P, 2 * T, NBLK]), ALU.is_equal))
                V.tensor_tensor(hot_blk, hot_blk, spread(c_yrow, 2, [P, 2 * T, NBLK]), ALU.mult)
                V.tensor_tensor(hot_row, spread(c_iota, 1, [P, 2 * T, P]), spread(row, 2, [P, 2 * T, P]),
                                ALU.is_equal).then_inc(dv_slot, 1)
                link(V.tensor_tensor(r_le, spread(r_inc, 1, [P, NOV, E]), spread(c_j, 2, [P, NOV, E]), ALU.is_le))
                link(V.tensor_reduce(r_ej, r_le, AX.X, ALU.add))
                link(V.tensor_scalar(r_ej, r_ej, float(E - 1), None, ALU.min))
                V.tensor_copy(ov_i[:, 0:NOV], r_ej)
                V.tensor_copy(ov_i[:, NOV:NOV + 1], r_inc[:, E - 1:E])
                link(V.tensor_copy(ov_i[:, NOV + 1:NOV + 2], ov_tot[:, :]))
                V.tensor_tensor(ov_tot[:, :], ov_tot[:, :], r_inc[:, E - 1:E], ALU.add).then_inc(dv_slot, 1)
                dve.wait_ge(pe_r, 2)
                link(V.tensor_scalar(r_yrow, bank(6, 0, NBLK), float(NO_ROW), None, ALU.add))
                V.tensor_copy(yidx[:, :], r_yrow)
                link(V.tensor_scalar(r_second, r_yrow, float(SEQ), -float(SEQ), ALU.is_ge, ALU.mult))
                link(V.tensor_tensor(r_yrow, r_yrow, r_second, ALU.add))
                V.tensor_copy(gidx[:, :], r_yrow).then_inc(dv_idx, 1)
                dve.wait_ge(dv_idx, 1)

                def rows_out(b4, b):
                    k = b % 2
                    if not (isinstance(b4, int) and 4 * b4 + b < 2):
                        dve.wait_ge(m_up, 4 * b4 + b - 1)
                    for c in range(2):
                        dve.wait_ge(m_tx, 8 * b4 + 2 * b + c + 1)
                        V.tensor_tensor(xgT[k][:, 4 * c:4 * c + 4, :], bank(c).rearrange("p (a b) -> p a b", a=4),
                                        spread(prm[:, R_G2P + 4 * c:R_G2P + 4 * c + 4], 2, [P, 4, P]),
                                        ALU.mult).then_inc(m_xt, 1)

                def hidden(b4, b):
                    k = b % 2
                    dve.wait_ge(m_th, 4 * b4 + b + 1)
                    V.scalar_tensor_tensor(th[k], th[k], 1.0, bank(2 + k, 0, FE), ALU.add, ALU.mult).then_inc(m_u, 1)
                    dve.wait_ge(m_u, 4 * b4 + b + 1)
                    if not (isinstance(b4, int) and 4 * b4 + b < 2):
                        dve.wait_ge(m_ht, 4 * b4 + b - 1)
                    V.scalar_tensor_tensor(hh[k], th[k], 0.5, bank(2 + k, FE, 2 * FE), ALU.mult,
                                           ALU.mult).then_inc(m_h, 1)

                rows_out(0, 0)
                rows_out(0, 1)
                hidden(0, 0)
                for b in range(4):
                    hidden(0, b + 1)
                    rows_out(0, b + 2)
                with dve.Fori(1, E // 4 - 1) as it:
                    for b in range(4):
                        hidden(it, b + 1)
                        rows_out(it, b + 2)
                for b in range(4):
                    if b < 3:
                        hidden(E // 4 - 1, b + 1)
                    if b < 2:
                        rows_out(E // 4 - 1, b + 2)
                n = dve.value_load(ov_i[0:1, NOV:NOV + 1], min_val=0, max_val=NOV)
                with dve.Fori(0, NOV) as j:
                    with dve.If(j < n):
                        for c in range(2):
                            dve.wait_ge(o_tx, 2 * j + c + 1)
                            V.tensor_tensor(xgT[0][:, 4 * c:4 * c + 4, :], bank(c).rearrange("p (a b) -> p a b", a=4),
                                            spread(prm[:, R_G2P + 4 * c:R_G2P + 4 * c + 4], 2, [P, 4, P]),
                                            ALU.mult).then_inc(o_xt, 1)
                        dve.wait_ge(o_th, j + 1)
                        V.scalar_tensor_tensor(th[0], th[0], 1.0, bank(2, 0, FE), ALU.add, ALU.mult).then_inc(o_u, 1)
                        dve.wait_ge(o_u, j + 1)
                        V.scalar_tensor_tensor(hh[0], th[0], 0.5, bank(2, FE, 2 * FE), ALU.mult,
                                               ALU.mult).then_inc(o_h, 1)

                dve.wait_ge(s_x1l, 16)
                for i in range(T):
                    dve.wait_ge(s_yg[i % NYG], 32 * (i // NYG + 1))
                    V.scalar_tensor_tensor(X[:, i, :], yg[i % NYG][0], gate1[:, i:i + 1], X[:, i, :], ALU.mult,
                                           ALU.add).then_inc(c_t, 1)
                    dve.wait_ge(c_t, i + 1)
                    V.scalar_tensor_tensor(X[:, i, :], yg[i % NYG][1], gate2[:, i:i + 1], X[:, i, :], ALU.mult,
                                           ALU.add).then_inc(c_x, 1)
                dve.wait_ge(c_x, T)
                dve.drain().then_inc(end_dve, 1)

        @block.tensor
        def _(pe):
            MM, TR = nc.tensor.matmul, nc.tensor.transpose

            def released(key):
                kind, i = key
                if kind == "lru":
                    return l_u, i + 1
                if kind in (1, 2):
                    return dv_qn, (kind - 1) * T + i + 1
                if kind == "gate":
                    return l_sig, i + 1
                if kind == 3:
                    return a_v, i + 1
                if kind == 4:
                    return dv_qn, 2 * T + i + 1
                if kind == "lss":
                    return l_ms, i + 1
                if kind == "qu":
                    return dv_qu, i + 1
                return dv_kn, 3 * (i // 2) + i % 2 + 1

            key_of = {n: k for k, n in PJ.items()}

            def take(key):
                n = PJ[key]
                if n >= 4:
                    pe.wait_ge(*released(key_of[n - 4]))
                return n % 4

            pe.wait_ge(s_con, 32)
            with pe.Fori(0, DEPTH) as l:
                new_layer(pe, l)
                pe.wait_ge(s_row, 16)
                TR(bank(7, 0, NROW), rows, ident[0:NROW, 0:NROW]).then_inc(pe_par, 1)
                for i in range(T):
                    pe.wait_ge(dv_xs, i + 1)
                    for c in range(2):
                        if i >= 1:
                            pe.wait_ge(dv_xe, 2 * (i - 1) + c + 1)
                        for k in range(4):
                            o = (4 * c + k) * P
                            ins = TR(bank(4 + c, k * P, k * P + P), xs[i % 2][:, o:o + P], ident)
                        ins.then_inc(pe_xn, 1)
                pe.wait_ge(dv_xe, 2 * T)

                def token_major(g, i):
                    c, n = GROUPS[g]
                    if i == 0:
                        pe.wait_ge(s_win[g % 2], 16 * (g // 2 + 1))
                    b = take((g, i))
                    for k in range(KC):
                        ins = MM(bank(b, 0, n), xnT[:, k, tile(i)], w_in_sb[g % 2][:, k, 0:n], start=(k == 0),
                                 stop=(k == KC - 1))
                    ins.then_inc(pe_pj, 1)

                def turn_qk(q):
                    pe.wait_ge(dv_qn, q + 1)
                    if q >= 2:
                        pe.wait_ge(*((dv_qT, q - 1) if q - 2 < T else (a_kT, q - 1 - T)))
                    for k in range(3):
                        ins = TR(bank(4 + q % 2, k * P, k * P + P), qn[q % 2][:, k * P:k * P + P], ident)
                    ins.then_inc(pe_tr, 1)

                def turn_latents(i):
                    q = 2 * T + i
                    pe.wait_ge(dv_qn, q + 1)
                    pe.wait_ge(*((a_kT, T - 1 + i) if i < 2 else (dv_cT, i - 1)))
                    b = 4 + q % 2
                    TR(bank(b, 0, P), qn[q % 2][:, 0:P], ident)
                    TR(bank(b, P, 2 * P, parts=64), qn[q % 2][:, P:QR], ident)
                    TR(bank(b, 2 * P, 3 * P), qn[q % 2][:, QR:QR + KVR], ident).then_inc(pe_tr, 1)

                pe.wait_ge(s_win[0], 16)
                for m in range(8):
                    f, c = m // 2, m % 2
                    b = take(("lru", m))
                    for k in range(KC):
                        ins = MM(bank(b), w_in_sb[0][:, k, f * P:f * P + P], xnT[:, k, 512 * c:512 * c + 512],
                                 start=(k == 0), stop=(k == KC - 1))
                    ins.then_inc(pe_pj, 1)
                for q in range(2 * T):
                    token_major(1 + q // T, q % T)
                    if q >= 1:
                        turn_qk(q - 1)
                    if q == T:
                        pe.wait_ge(l_conv, 8)
                        pe.wait_ge(s_wab, 16)
                        for n in range(8):
                            m, f, c = n // 4, (n // 2) % 2, n % 2
                            b = take(("gate", n))
                            MM(bank(b), wab[:, m, f, :], l_xc[:, f, 512 * c:512 * c + 512], start=True,
                               stop=True).then_inc(pe_pj, 1)
                for i in range(T):
                    token_major(3, i)
                    if i == 0:
                        turn_qk(2 * T - 1)
                for i in range(T):
                    token_major(4, i)
                    if i >= 1:
                        turn_latents(i - 1)
                    if i == T - 3:
                        pe.wait_ge(l_y2, 1)
                        for c in range(2):
                            b = take(("lss", c))
                            for f in range(2):
                                ins = MM(bank(b), ones, l_t2[:, f, 512 * c:512 * c + 512], start=(f == 0),
                                         stop=(f == 1))
                            ins.then_inc(pe_pj, 1)
                turn_latents(T - 1)

                def turn_heads(i, kind):
                    for c in (2 * kind, 2 * kind + 1):
                        if c == 0:
                            pe.wait_ge(dv_kn, 3 * i + 3)
                        elif c == 2:
                            pe.wait_ge(dv_qr, i + 1)
                        if i == 0 and c < 2:
                            pe.wait_ge(dv_cT, T - 1 + c)
                        else:
                            pe.wait_ge(a_kTm, 4 * i + c - 1)
                        for k in range(4 - 2 * (c % 2)):
                            h = 4 * (c % 2) + k
                            src = qn[(3 * T + i) % 2][:, h * MQK:h * MQK + MQK] if c < 2 else qraw[:, h, :]
                            ins = TR(bank(4 + c % 2, k * P, k * P + P, parts=MQK), src, ident)
                        ins.then_inc(pe_tr, 1)

                def before(b):
                    pe.wait_ge(*released(key_of[max(n for n in range(PJ["kv", 0]) if n % 4 == b)]))

                pe.wait_ge(s_wq, 48)
                pe.wait_ge(dv_cT, T)
                for i in range(T):
                    for c in range(2):
                        b = head_bank("kv", 2 * i + c)
                        if i < 1:
                            before(b)
                        else:
                            pe.wait_ge(dv_kn, 3 * (i - 1) + c + 1)
                        MM(bank(b, 0, 384), ckvT[:, tile(i)], wukv[:, 384 * c:384 * c + 384], start=True,
                           stop=True).then_inc(pe_pj, 1)
                    if i >= 1:
                        turn_heads(i - 1, 0)
                    for c, (lo, hi) in enumerate(((0, 384), (384, 576))):
                        b = head_bank("qu", 2 * i + c)
                        if i == 0:
                            before(b)
                        elif i >= 2:
                            pe.wait_ge(dv_qu, 2 * (i - 2) + c + 1)
                        MM(bank(b, 0, hi - lo), cqT[:, 0, tile(i)], wuq[:, 0, lo:hi], start=True, stop=False)
                        MM(bank(b, 0, hi - lo), cqT[0:QR - P, 1, tile(i)], wuq[0:QR - P, 1, lo:hi], start=False,
                           stop=True).then_inc(pe_pj, 1)
                    if i >= 1:
                        turn_heads(i - 1, 1)
                turn_heads(T - 1, 0)
                turn_heads(T - 1, 1)

                pe.wait_ge(dv_qu, 2 * T)
                pe.wait_ge(a_kTm, 4 * T)
                pe.wait_ge(a_vm, 2 * T)
                pe.wait_ge(a_v, T)
                pe.wait_ge(l_ms, 2)

                def scores(u):
                    kind, n, i = UNITS[u]
                    nk = (i + 1) * P
                    if kind == 0 and u % PAIR == 0:
                        pe.wait_ge(s_st[n % 2], 96 * (n // 2 + 1))
                    for m in range(maps_of(u)):
                        s = MAPS_BEFORE[u] + m
                        if s >= 2:
                            pe.wait_ge(dv_pass, s - 1)
                        o = (s % 2) * 1024
                        if kind:
                            lhs, rhs = qTm[:, n, tile(i)], kTm[:, n, 0:nk]
                        else:
                            lhs, rhs = qst[n % 2][:, m, tile(i)].bitcast(F32R), kst[n % 2][:, m, 0:nk].bitcast(F32R)
                        for c in range(0, nk, 512):
                            w = min(512, nk - c)
                            ins = MM(PS[:, o + c:o + c + w], lhs, rhs[:, c:c + w], start=True, stop=True)
                        ins.then_inc(pe_s, 1)

                def turn_p(u):
                    if UNITS[u][0]:
                        pe.wait_ge(a_exp, MAPS_BEFORE[u + 1])
                    else:
                        pe.wait_ge(dv_comb, DIFFS_BEFORE[u + 1])
                    for c, (lo, hi) in enumerate(chunks_of(u)):
                        r = CHUNKS_BEFORE[u] + c
                        if r >= 2:
                            pe.wait_ge(a_pt, r - 1)
                        for k in range(lo, hi):
                            ins = TR(bank(4 + r % 2, (k - lo) * P, (k - lo) * P + P),
                                     Pm[u % NPM][0][:, k * P:k * P + P], ident)
                        ins.then_inc(pe_t, 1)

                def pv(u):
                    kind, n, i = UNITS[u]
                    if u % PAIR < 2 and n >= 1:
                        pe.wait_ge(dv_o, 2 * n - 1 + kind)
                    for c, (lo, hi) in enumerate(chunks_of(u)):
                        r = CHUNKS_BEFORE[u] + c
                        pe.wait_ge(a_pt, r + 1)
                        for k in range(lo, hi):
                            v = Vm[:, k, n, :] if kind else Vd[:, k, n * DVD:(n + 1) * DVD]
                            ins = MM(bank(6 + kind, 64 * i, 64 * i + 64), PT[r % 4][:, (k - lo) * P:(k - lo) * P + P],
                                     v, start=(k == 0), stop=(k == i))
                        ins.then_inc(pe_v, 1)

                for u in range(AHEAD):
                    scores(u)
                for u in range(NU):
                    if u + AHEAD < NU:
                        scores(u + AHEAD)
                    if u >= 2:
                        pv(u - 2)
                    turn_p(u)
                pv(NU - 2)
                pv(NU - 1)

                def turn_y(i):
                    pe.wait_ge(dv_on, DH + i + 1)
                    for c, (lo, hi) in enumerate(((0, 4), (4, 6))):
                        if i == 1:
                            pe.wait_ge(dv_yr, c + 1)
                        elif i == 2:
                            pe.wait_ge(dv_yr, c + 3)
                        elif i >= 3:
                            pe.wait_ge(dv_h2T, 2 * (i - 3) + c + 1)
                        else:
                            pe.wait_ge(a_pt, CHUNKS_BEFORE[NU])
                        for k in range(lo, hi):
                            ins = TR(bank(4 + c, (k - lo) * P, (k - lo) * P + P), O[:, i, k * P:k * P + P], ident)
                        ins.then_inc(pe_y, 1)

                def turn_h2(i):
                    pe.wait_ge(dv_h2, i + 1)
                    for c in range(2):
                        if i + 2 < T:
                            pe.wait_ge(dv_yr, 2 * (i + 2) + c + 1)
                        else:
                            pe.wait_ge(dv_h2T, 2 * (i - 1) + c + 1)
                        for k in range(4):
                            o = (4 * c + k) * P
                            ins = TR(bank(4 + c, k * P, k * P + P), h2[i % 2][:, o:o + P], ident)
                        ins.then_inc(pe_h2, 1)

                def route(i):
                    pe.wait_ge(dv_h2T, 2 * i + 2)
                    if i == 0:
                        pe.wait_ge(s_wr, 16)
                    if i < 2:
                        pe.wait_ge(dv_o, 2 * DH)
                    else:
                        pe.wait_ge(a_lg, i - 1)
                    for k in range(KC):
                        ins = MM(bank(6 + i % 2, 0, G + E), h2T[i % 2][:, k, :], wr[:, k, :], start=(k == 0),
                                 stop=(k == KC - 1))
                    ins.then_inc(pe_lg, 1)

                turn_y(0)
                pe.wait_ge(dv_wl, KC)
                for i in range(T):
                    if i >= 2:
                        pe.wait_ge(dv_x1, i - 1)
                    pe.wait_ge(dv_yT, i + 1)
                    for c in range(2):
                        o = (i % 2) * 1024 + 512 * c
                        n = 0
                        for k in (2, 3, 4, 5, 6, 7, 0, 1):
                            if c == 1 and k == 4 and i >= 1:
                                turn_h2(i - 1)
                            if k < 2:
                                pe.wait_ge(dv_wl, KC + 1)
                                y_h, y_l = yl_hi[:, k, tile(i)], yl_lo[:, k, tile(i)]
                            else:
                                y_h, y_l = yT_hi[i % 2][:, k - 2, :], yT_lo[i % 2][:, k - 2, :]
                            w_h, w_l = wo_hi[k][:, 0, 512 * c:512 * c + 512], wo_lo[k][:, 0, 512 * c:512 * c + 512]
                            for y_, w_ in ((y_h, w_h), (y_h, w_l), (y_l, w_h)):
                                ins = MM(PS[:, o:o + 512], y_.bitcast(F32R), w_.bitcast(F32R), start=(n == 0),
                                         stop=(n == 3 * KC - 1))
                                n += 1
                        if c == 0:
                            if i + 1 < T:
                                turn_y(i + 1)
                    ins.then_inc(pe_x1, 1)
                    if i >= 1:
                        route(i - 1)
                turn_h2(T - 1)
                route(T - 1)

                pe.wait_ge(dv_r, 2)
                MM(bank(7, 0, T * E), tri, r_M.rearrange("p t e -> p (t e)"), start=True, stop=False)
                MM(bank(7, 0, T * E), ones, r_pre[:, 0:T, :].rearrange("p t e -> p (t e)"), start=False, stop=True)
                MM(bank(7, T * E, T * E + E), ones, r_pre[:, T, :], start=True, stop=True).then_inc(pe_r, 1)
                pe.wait_ge(dv_slot, 1)
                for k in range(2 * T):
                    ins = MM(bank(6, 0, NBLK), hot_row[:, k, :], hot_blk[:, k, :], start=(k == 0), stop=(k == 2 * T - 1))
                ins.then_inc(pe_r, 1)

                def turn_rows(b4, b):
                    k = b % 2
                    first = isinstance(b4, int) and 4 * b4 + b == 0
                    pe.wait_ge(g_x[k], l * (8 * E) + (32 * b4 + 16 * (b // 2) + 16))
                    for c in range(2):
                        if not first:
                            pe.wait_ge(m_xt, 8 * b4 + 2 * b + c - 1)
                        for m in range(4):
                            ins = TR(bank(c, m * P, m * P + P), xgp[k][:, 4 * c + m, :], ident)
                        ins.then_inc(m_tx, 1)

                def up(b4, b):
                    k, w = b % 2, b % 4
                    pe.wait_ge(m_xt, 8 * b4 + 2 * b + 2)
                    if not (isinstance(b4, int) and 4 * b4 + b < 2):
                        pe.wait_ge(m_h, 4 * b4 + b - 1)
                    pe.wait_ge(s_w13[w], 32 * b4 + 32 * (b // 4 + 1))
                    for m in range(KC):
                        ins = MM(bank(2 + k), xgT[k][:, m, :], w_ex[w][0][:, :, m, :], start=(m == 0),
                                 stop=(m == KC - 1))
                    ins.then_inc(m_up, 1)

                def turn_hidden(b4, b):
                    k = b % 2
                    pe.wait_ge(m_h, 4 * b4 + b + 1)
                    if not (isinstance(b4, int) and 4 * b4 + b == 0):
                        pe.wait_ge(m_hte, 4 * b4 + b)
                    for m in range(2):
                        ins = TR(bank(4, m * P, m * P + P), hh[k][:, m * P:m * P + P], ident)
                    ins.then_inc(m_ht, 1)

                def down(b4, b):
                    k, w = b % 2, b % 4
                    pe.wait_ge(m_hte, 4 * b4 + b + 1)
                    pe.wait_ge(s_w2[w], 16 * b4 + 16 * (b // 4 + 1))
                    for c in range(2):
                        if not (isinstance(b4, int) and 4 * b4 + b == 0):
                            pe.wait_ge(m_y, 8 * b4 + 2 * b + c - 1)
                        for m in range(2):
                            ins = MM(bank(5 + c), hT[k][:, m, :], w_ex[w][1][:, m, 512 * c:512 * c + 512],
                                     start=(m == 0), stop=(m == 1))
                        ins.then_inc(m_dn, 1)

                turn_rows(0, 0)
                turn_rows(0, 1)
                up(0, 0)
                for b in range(4):
                    up(0, b + 1)
                    turn_hidden(0, b)
                    turn_rows(0, b + 2)
                    down(0, b)
                with pe.Fori(1, E // 4 - 1) as it:
                    for b in range(4):
                        up(it, b + 1)
                        turn_hidden(it, b)
                        turn_rows(it, b + 2)
                        down(it, b)
                for b in range(4):
                    if b < 3:
                        up(E // 4 - 1, b + 1)
                    turn_hidden(E // 4 - 1, b)
                    if b < 2:
                        turn_rows(E // 4 - 1, b + 2)
                    down(E // 4 - 1, b)
                pe.wait_ge(m_y, 2 * E)
                pe.sem_inc(o_free, 1)
                n = pe.value_load(ov_i[0:1, NOV:NOV + 1], min_val=0, max_val=NOV)
                before = pe.value_load(ov_i[0:1, NOV + 1:NOV + 2], min_val=0, max_val=NOV * DEPTH)
                with pe.Fori(0, NOV) as j:
                    with pe.If(j < n):
                        pe.wait_ge(g_ov, 16 * before + 16 * j + 16)
                        for c in range(2):
                            for m in range(4):
                                ins = TR(bank(c, m * P, m * P + P), xgp[0][:, 4 * c + m, :], ident)
                            ins.then_inc(o_tx, 1)
                        pe.wait_ge(o_xt, 2 * j + 2)
                        pe.wait_ge(o_w, 48 * j + 48)
                        for m in range(KC):
                            ins = MM(bank(2), xgT[0][:, m, :], w_ex[0][0][:, :, m, :], start=(m == 0),
                                     stop=(m == KC - 1))
                        ins.then_inc(o_up, 1)
                        pe.wait_ge(o_h, j + 1)
                        for m in range(2):
                            ins = TR(bank(4, m * P, m * P + P), hh[0][:, m * P:m * P + P], ident)
                        ins.then_inc(o_ht, 1)
                        pe.wait_ge(o_hte, j + 1)
                        for c in range(2):
                            for m in range(2):
                                ins = MM(bank(5 + c), hT[0][:, m, :], w_ex[0][1][:, m, 512 * c:512 * c + 512],
                                         start=(m == 0), stop=(m == 1))
                        ins.then_inc(o_dn, 1)
                        pe.wait_ge(o_y, j + 1)
                        pe.sem_inc(o_free, 1)
                pe.drain().then_inc(end_pe, 1)


_INS = ["x", "w_in", "mla_w_uq", "mla_w_ukv", "w_out", "exp_w1", "exp_w3", "exp_w2"]


def packed(inputs):
    a = {n: np.asarray(v) for n, v in inputs.items()}
    rows = np.zeros((DEPTH, NROW, P), np.float32)
    for r, n in ((R_G1, "norm1_g"), (R_G2, "norm2_g"), (R_LOUT, "lru_out_g"), (R_MOUT, "mla_out_g"),
                 (R_CKV, "mla_ckv_g"), (R_CW, "lru_conv_w"), (R_CB, "lru_conv_b"), (R_BA, "lru_ba"),
                 (R_BX, "lru_bx"), (R_LAM, "lru_lambda")):
        v = a[n].reshape(DEPTH, -1, P)
        rows[:, r:r + v.shape[1]] = v
    for r, n in ((R_SUB, "diff_sub_g"), (R_DQ, "diff_q_g"), (R_DK, "diff_k_g")):
        rows[:, r] = np.tile(a[n], (1, P // a[n].shape[1]))
    rows[:, R_G2P:R_G2P + KC] = a["norm2_g"].reshape(DEPTH, P, KC).transpose(0, 2, 1)
    rows[:, R_CQ] = a["mla_cq_g"][:, 0:P]
    rows[:, R_CQ + 1, 0:QR - P] = a["mla_cq_g"][:, P:QR]
    rows[:, R_MQ, 0:MQK] = a["mla_q_g"]
    rows[:, R_MK, 0:MQK] = a["mla_k_g"]
    wide = np.concatenate([a["diff_lq1"], a["diff_lk1"], a["diff_lq2"], a["diff_lk2"]]
                          + [a[n][:, MN:MQK] for n in ("mla_q_g", "mla_q_g", "mla_k_g", "mla_k_g")]
                          + [a["router_g_b"], a["router_e_b"]], axis=1)
    gates = np.zeros((DEPTH, P, 2, 2, P), np.float32)
    for m, n in enumerate(("lru_wa", "lru_wx")):
        for b in range(4):
            o = 64 * (b % 2)
            gates[:, o:o + 64, m, b // 2, o:o + 64] = a[n][:, b]
    router = np.concatenate([a["router_g_w"], a["router_e_w"]], axis=2)
    return {"rows": rows, "wide": wide, "gates": gates.reshape(DEPTH, P, 4 * P), "router": router}


def kernel(**inputs):
    import concourse.bacc as bacc
    from concourse.bass_utils import run_bass_kernel_spmd

    nc = bacc.Bacc("TRN2", target_bir_lowering=False, num_devices=1)
    arrays, aps = {}, {}
    for name, value in [(n, inputs[n]) for n in _INS] + list(packed(inputs).items()) + list(constants().items()):
        value = np.ascontiguousarray(value)
        arrays[f"in_{name}"] = value
        aps[name] = nc.dram_tensor(f"in_{name}", value.shape, mybir.dt.from_np(value.dtype), kind="ExternalInput").ap()
    out = nc.dram_tensor("out_0", (1, SEQ, D), F32, kind="ExternalOutput").ap()
    build(nc, aps, out)
    r = run_bass_kernel_spmd(nc, [arrays], core_ids=[0])
    return r.results[0]["out_0"]
```
